# Optimizing a Trainium2 kernel written in Bass

```python
import jax
import jax.numpy as jnp
from jax import lax
import numpy as np
import math

D_MODEL = 1024
BATCH = 1
SEQ = 512
DEPTH = 1

N_MEM = 256
EPS = 1e-6
D_FF = 2816
HG_HEADS = 4
HG_DK = 128
HG_DV = 128
HG_CHUNK = 64
HG_K = HG_HEADS * HG_DK
HG_V = HG_HEADS * HG_DV
HG_COLS = 2 * HG_K + 2 * HG_V
DIL_GROUPS = ((128, 1), (512, 4), (2048, 16))
DIL_HEADS = 4
DIL_DH = 128
DIL_W = DIL_HEADS * DIL_DH
DIL_COLS = len(DIL_GROUPS) * 3 * DIL_W
ALIBI_HEADS = len(DIL_GROUPS) * DIL_HEADS
MEM_HEADS = 4
MEM_DH = 128
MEM_W = MEM_HEADS * MEM_DH
N_BRANCH = 3
GATE_COLS = N_BRANCH * D_MODEL
SPLITS = (HG_K, 2 * HG_K, 2 * HG_K + HG_V, HG_COLS, HG_COLS + DIL_COLS, HG_COLS + DIL_COLS + MEM_W)
D_IN = HG_COLS + DIL_COLS + MEM_W + GATE_COLS


def rmsnorm(x, w):
    xf = x.astype(jnp.float32)
    y = xf * lax.rsqrt(jnp.mean(xf * xf, axis=-1, keepdims=True) + EPS)
    return (y * w.astype(jnp.float32)).astype(x.dtype)

def swiglu(x, w_gu, w_down):
    g, u = jnp.split(x @ w_gu, 2, axis=-1)
    return (jax.nn.silu(g) * u) @ w_down

def alibi_slopes():
    return 2.0 ** (-8.0 * jnp.arange(1, ALIBI_HEADS + 1, dtype=jnp.float32) / ALIBI_HEADS)

def hgrn2(q_raw, f_raw, i_raw, lb):
    B, S = q_raw.shape[:2]
    C = HG_CHUNK
    N = S // C
    f32 = jnp.float32
    q = jax.nn.silu(q_raw.astype(f32)).reshape(B, N, C, HG_HEADS, HG_DK)
    lbh = lb.reshape(HG_HEADS, HG_DK)
    f = lbh + (1.0 - lbh) * jax.nn.sigmoid(f_raw.astype(f32).reshape(B, N, C, HG_HEADS, HG_DK))
    k = 1.0 - f
    v = i_raw.astype(f32).reshape(B, N, C, HG_HEADS, HG_DV)
    b = jnp.cumsum(jnp.log(f), axis=2)
    ref = b[:, :, C // 2 - 1:C // 2]
    scores = jnp.einsum('bnchk,bnshk->bnhcs', q * jnp.exp(b - ref), k * jnp.exp(ref - b))
    causal = jnp.tril(jnp.ones((C, C), dtype=bool))
    scores = jnp.where(causal, scores, 0.0)
    o_intra = jnp.einsum('bnhcs,bnshv->bnchv', scores, v)
    b_last = b[:, :, -1:]
    kv = jnp.einsum('bnshk,bnshv->nbhkv', k * jnp.exp(b_last - b), v)
    decay = jnp.moveaxis(jnp.exp(b_last[:, :, 0]), 1, 0)

    def step(state, inp):
        kv_n, dec_n = inp
        return dec_n[..., None] * state + kv_n, state

    s0 = jnp.zeros((B, HG_HEADS, HG_DK, HG_DV), f32)
    _, s_prev = lax.scan(step, s0, (kv, decay))
    o_inter = jnp.einsum('bnchk,nbhkv->bnchv', q * jnp.exp(b), s_prev)
    return (o_intra + o_inter).reshape(B, S, HG_HEADS, HG_DV)

def dilated_group(q, k, v, window, dil, slopes):
    B, S, H, dh = q.shape
    nk = window // dil
    span = nk * dil
    Sp = -(-S // span) * span
    L = Sp // dil
    nb = L // nk

    def to_sub(t):
        t = jnp.pad(t, ((0, 0), (0, Sp - S), (0, 0), (0, 0)))
        return t.reshape(B, L, dil, H, dh).transpose(0, 2, 1, 3, 4).reshape(B * dil, nb, nk, H, dh)

    qs, ks, vs = to_sub(q), to_sub(k), to_sub(v)
    kb = jnp.concatenate([jnp.pad(ks, ((0, 0), (1, 0), (0, 0), (0, 0), (0, 0)))[:, :-1], ks], axis=2)
    vb = jnp.concatenate([jnp.pad(vs, ((0, 0), (1, 0), (0, 0), (0, 0), (0, 0)))[:, :-1], vs], axis=2)
    s = jnp.einsum('znqhd,znkhd->znhqk', qs, kb).astype(jnp.float32) * (dh ** -0.5)
    qi = jnp.arange(nk)[:, None]
    kj = jnp.arange(2 * nk)[None, :]
    delta = nk + qi - kj
    blk = jnp.arange(nb)[:, None, None]
    valid = (delta >= 0) & (delta <= nk) & ((blk > 0) | (kj >= nk))
    s = s - slopes[:, None, None] * (delta * dil).astype(jnp.float32)
    s = jnp.where(valid[:, None], s, -jnp.inf)
    m = jnp.max(s, axis=-1)
    p = jnp.exp(s - m[..., None])
    l = jnp.sum(p, axis=-1)
    o = jnp.einsum('znhqk,znkhd->znqhd', p.astype(vb.dtype), vb).astype(jnp.float32)
    o = o.reshape(B, dil, L, H, dh).transpose(0, 2, 1, 3, 4).reshape(B, Sp, H, dh)[:, :S]

    def stat_back(t):
        return t.transpose(0, 1, 3, 2).reshape(B, dil, L, H).transpose(0, 2, 1, 3).reshape(B, Sp, H)[:, :S]

    return o, stat_back(m), stat_back(l)

def dilated_attention(dil_cols):
    B, S = dil_cols.shape[:2]
    qkv = dil_cols.reshape(B, S, len(DIL_GROUPS), 3, DIL_HEADS, DIL_DH)
    slopes = alibi_slopes()
    outs, maxs, sums = [], [], []
    for g, (window, dil) in enumerate(DIL_GROUPS):
        o, m, l = dilated_group(qkv[:, :, g, 0], qkv[:, :, g, 1], qkv[:, :, g, 2], window, dil,
                                slopes[g * DIL_HEADS:(g + 1) * DIL_HEADS])
        outs.append(o)
        maxs.append(m)
        sums.append(l)
    m_all = jnp.stack(maxs)
    w = jnp.exp(m_all - jnp.max(m_all, axis=0))
    num = jnp.sum(w[..., None] * jnp.stack(outs), axis=0)
    den = jnp.sum(w * jnp.stack(sums), axis=0)
    return (num / den[..., None]).reshape(B, S, DIL_W).astype(dil_cols.dtype)

def memory_attention(mq, mem, mem_norm_w, w_mem_kv):
    B, S = mq.shape[:2]
    mk, mv = jnp.split(rmsnorm(mem, mem_norm_w) @ w_mem_kv, 2, axis=-1)
    mq = mq.reshape(B, S, MEM_HEADS, MEM_DH)
    mk = mk.reshape(B, N_MEM, MEM_HEADS, MEM_DH)
    mv = mv.reshape(B, N_MEM, MEM_HEADS, MEM_DH)
    s = jnp.einsum('bshd,bmhd->bhsm', mq, mk).astype(jnp.float32) * (MEM_DH ** -0.5)
    p = jax.nn.softmax(s, axis=-1).astype(mv.dtype)
    return jnp.einsum('bhsm,bmhd->bshd', p, mv).reshape(B, S, MEM_W)

def token_mixing(u, mem, w_in, b_gate, lb, hg_norm_w, mem_norm_w, w_mem_kv, w_br_hg, w_br_dil, w_br_mem, w_out):
    B, S, D = u.shape
    proj = u @ w_in
    hq, hf, hi, hog, dcols, mq, gl = jnp.split(proj, SPLITS, axis=-1)
    o_hg = rmsnorm(hgrn2(hq, hf, hi, lb), hg_norm_w)
    o_hg = o_hg * jax.nn.sigmoid(hog.astype(jnp.float32)).reshape(B, S, HG_HEADS, HG_DV)
    y_hg = o_hg.reshape(B, S, HG_V).astype(u.dtype)
    y_dil = dilated_attention(dcols)
    y_mem = memory_attention(mq, mem, mem_norm_w, w_mem_kv)
    gates = jax.nn.sigmoid((gl + b_gate).astype(jnp.float32)).astype(u.dtype).reshape(B, S, N_BRANCH, D)
    y = (gates[:, :, 0] * (y_hg @ w_br_hg)
         + gates[:, :, 1] * (y_dil @ w_br_dil)
         + gates[:, :, 2] * (y_mem @ w_br_mem))
    return y @ w_out

def first_inputs(seed: int = 0) -> dict:
    key = jax.random.key(seed)
    ks = jax.random.split(key, 22)
    f32 = jnp.float32

    def w(k, shape, fan_in):
        return jax.random.normal(k, shape, f32) * (fan_in ** -0.5)

    def gain(k, n):
        return 1.0 + 0.05 * jax.random.normal(k, (DEPTH, n), f32)

    return {
        'x': jax.random.normal(ks[0], (BATCH, SEQ, D_MODEL), f32),
        'mem': jax.random.normal(ks[1], (BATCH, N_MEM, D_MODEL), f32),
        'ffn1_pre_w': gain(ks[2], D_MODEL),
        'ffn1_w_gu': w(ks[3], (DEPTH, D_MODEL, 2 * D_FF), D_MODEL),
        'ffn1_w_down': w(ks[4], (DEPTH, D_FF, D_MODEL), D_FF),
        'ffn1_post_w': gain(ks[5], D_MODEL),
        'mix_pre_w': gain(ks[6], D_MODEL),
        'w_in': w(ks[7], (DEPTH, D_MODEL, D_IN), D_MODEL),
        'b_gate': 0.01 * jax.random.normal(ks[8], (DEPTH, GATE_COLS), f32),
        'hg_lb_logits': 0.1 * jax.random.normal(ks[9], (DEPTH + 1, HG_K), f32),
        'hg_norm_w': gain(ks[10], HG_DV),
        'mem_norm_w': gain(ks[11], D_MODEL),
        'w_mem_kv': w(ks[12], (DEPTH, D_MODEL, 2 * MEM_W), D_MODEL),
        'w_br_hg': w(ks[13], (DEPTH, HG_V, D_MODEL), HG_V),
        'w_br_dil': w(ks[14], (DEPTH, DIL_W, D_MODEL), DIL_W),
        'w_br_mem': w(ks[15], (DEPTH, MEM_W, D_MODEL), MEM_W),
        'w_out': w(ks[16], (DEPTH, D_MODEL, D_MODEL), D_MODEL),
        'mix_post_w': gain(ks[17], D_MODEL),
        'ffn2_pre_w': gain(ks[18], D_MODEL),
        'ffn2_w_gu': w(ks[19], (DEPTH, D_MODEL, 2 * D_FF), D_MODEL),
        'ffn2_w_down': w(ks[20], (DEPTH, D_FF, D_MODEL), D_FF),
        'ffn2_post_w': gain(ks[21], D_MODEL),
    }

def first_block(x, mem, ffn1_pre_w, ffn1_w_gu, ffn1_w_down, ffn1_post_w, mix_pre_w, w_in, b_gate,
              hg_lb_logits, hg_norm_w, mem_norm_w, w_mem_kv, w_br_hg, w_br_dil, w_br_mem, w_out,
              mix_post_w, ffn2_pre_w, ffn2_w_gu, ffn2_w_down, ffn2_post_w):
    lb_all = jnp.cumsum(jax.nn.softmax(hg_lb_logits.astype(jnp.float32), axis=0), axis=0)
    h = x
    for l in range(DEPTH):
        h = h + 0.5 * rmsnorm(swiglu(rmsnorm(h, ffn1_pre_w[l]), ffn1_w_gu[l], ffn1_w_down[l]), ffn1_post_w[l])
        u = rmsnorm(h, mix_pre_w[l])
        y = token_mixing(u, mem, w_in[l], b_gate[l], lb_all[l], hg_norm_w[l], mem_norm_w[l], w_mem_kv[l],
                         w_br_hg[l], w_br_dil[l], w_br_mem[l], w_out[l])
        h = h + rmsnorm(y, mix_post_w[l])
        h = h + 0.5 * rmsnorm(swiglu(rmsnorm(h, ffn2_pre_w[l]), ffn2_w_gu[l], ffn2_w_down[l]), ffn2_post_w[l])
    return h


GRID_W = 64
CTX_LEN = 256
N_MOD = 6

D_HY = 512
HY_ORDER = 2
HY_BANDS = 16
HY_EMB = 1 + 2 * HY_BANDS
HY_FFN = 64
HY_DECAY_TARGET = 1e-2
HY_FAST_PCT = 0.3
HY_SLOW_PCT = 1.5

NA_HEADS = 8
HEAD_DIM = 64
D_NA = NA_HEADS * HEAD_DIM
WIN_ROWS = 8
WIN_COLS = 16
ROPE_THETA = 10000.0
NEG_INF = -1e30

PEER_HEADS = 8
PEER_N_KEYS = 128
PEER_N_EXPERTS = PEER_N_KEYS * PEER_N_KEYS
PEER_TOPK = 16
PEER_D_KEY = 256
PEER_D_HALF = PEER_D_KEY // 2
PEER_BLOCK = 128

COL_HY = 0
COL_Q = COL_HY + 3 * D_HY
COL_K = COL_Q + D_NA
COL_V = COL_K + D_NA
COL_G_HY = COL_V + D_NA
COL_G_NA = COL_G_HY + D_MODEL
N_PROJ = COL_G_NA + D_MODEL


def rmsnorm_2(x, g):
    x32 = x.astype(jnp.float32)
    y = x32 * lax.rsqrt(jnp.mean(x32 * x32, axis=-1, keepdims=True) + EPS)
    return (y * g.astype(jnp.float32)).astype(x.dtype)

def modulate(x, g, shift, scale):
    return rmsnorm_2(x, g) * (1.0 + scale) + shift

def adaln(cond, p):
    m = jax.nn.silu(cond) @ p['w_ada'] + p['b_ada']
    return m.reshape(cond.shape[:-1] + (N_MOD, D_MODEL))

def hyena_filters(L, p):
    f32 = jnp.float32
    t = jnp.linspace(0.0, 1.0, L, dtype=f32)[:, None]
    w = (2.0 * math.pi / L) * jnp.arange(L, dtype=f32)[:, None]
    bands = jnp.linspace(1e-4, HY_BANDS - 1.0, HY_BANDS, dtype=f32)[None, :]
    feats = jnp.concatenate([t, jnp.cos(bands * w), -jnp.sin(bands * w)], axis=-1)
    freq = p['hy_sin_freq'].astype(f32)
    h = jnp.sin(freq * (feats @ p['hy_f1_w'].astype(f32) + p['hy_f1_b'].astype(f32)))
    h = jnp.sin(freq * (h @ p['hy_f2_w'].astype(f32) + p['hy_f2_b'].astype(f32)))
    h = jnp.sin(freq * (h @ p['hy_f3_w'].astype(f32) + p['hy_f3_b'].astype(f32)))
    h = (h @ p['hy_f4_w'].astype(f32)).reshape(L, HY_ORDER, 2, D_HY)
    deltas = jnp.abs(jnp.linspace(math.log(HY_DECAY_TARGET) / HY_SLOW_PCT,
                                  math.log(HY_DECAY_TARGET) / HY_FAST_PCT, D_HY, dtype=f32))
    h = h * jnp.exp(-t * deltas)[:, None, None, :]
    h = h / jnp.sum(jnp.abs(h), axis=(0, 2), keepdims=True)
    fwd, bwd = h[:, :, 0], h[:, :, 1]
    return jnp.concatenate([fwd, jnp.zeros_like(fwd[:1]), bwd[:0:-1]], axis=0)

def hyena(zh, p):
    B, L, _ = zh.shape
    cw = p['hy_conv_w']
    zp = jnp.pad(zh, ((0, 0), (1, 1), (0, 0)))
    zc = cw[0] * zp[:, :-2] + cw[1] * zp[:, 1:-1] + cw[2] * zp[:, 2:] + p['hy_conv_b']
    v, x1, x2 = jnp.split(zc.astype(jnp.float32), 3, axis=-1)
    kf = jnp.fft.rfft(hyena_filters(L, p), axis=0)
    skip = p['hy_skip'].astype(jnp.float32)
    y = v
    for o, gate in enumerate((x1, x2)):
        yf = jnp.fft.rfft(y, n=2 * L, axis=1)
        conv = jnp.fft.irfft(yf * kf[:, o][None], n=2 * L, axis=1)[:, :L]
        y = gate * (conv + skip[o] * y)
    return y.astype(zh.dtype)

def axial_rope(x):
    f32 = jnp.float32
    S = x.shape[1]
    pos = jnp.arange(S, dtype=jnp.int32)
    rows = (pos // GRID_W).astype(f32)
    cols = (pos % GRID_W).astype(f32)
    half = HEAD_DIM // 2
    nf = half // 2
    inv = ROPE_THETA ** (-jnp.arange(nf, dtype=f32) / nf)

    def rot(xp, ps):
        ang = ps[:, None] * inv[None, :]
        cos = jnp.cos(ang)[None, :, None, :]
        sin = jnp.sin(ang)[None, :, None, :]
        a, b = xp[..., :nf], xp[..., nf:]
        return jnp.concatenate([a * cos - b * sin, a * sin + b * cos], axis=-1)

    x32 = x.astype(f32)
    return jnp.concatenate([rot(x32[..., :half], rows), rot(x32[..., half:], cols)], axis=-1).astype(x.dtype)

def neighbourhood_attention(q, k, v, k_ctx, v_ctx, rpb):
    B, S, H, Dh = q.shape
    rows = S // GRID_W
    wr = min(WIN_ROWS, rows)
    r = np.arange(rows)
    row_start = np.clip(r - wr // 2, 0, rows - wr)
    row_idx = row_start[:, None] + np.arange(wr)[None, :]
    col = np.arange(GRID_W)
    col_start = np.clip(col - WIN_COLS // 2, 0, GRID_W - WIN_COLS)
    col_mask = (col[None, :] >= col_start[:, None]) & (col[None, :] < col_start[:, None] + WIN_COLS)
    dr_idx = row_idx - r[:, None] + (WIN_ROWS - 1)
    dc_idx = np.clip(col[None, :] - col[:, None], -(WIN_COLS - 1), WIN_COLS - 1) + (WIN_COLS - 1)
    bias = rpb[:, dr_idx[:, None, :, None], dc_idx[None, :, None, :]]

    qg = q.reshape(B, rows, GRID_W, H, Dh)
    kg = k.reshape(B, rows, GRID_W, H, Dh)[:, row_idx]
    vg = v.reshape(B, rows, GRID_W, H, Dh)[:, row_idx]
    scale = HEAD_DIM ** -0.5
    s_loc = jnp.einsum('brqhd,brikhd->bhrqik', qg, kg).astype(jnp.float32) * scale + bias.astype(jnp.float32)
    s_loc = jnp.where(col_mask[:, None, :], s_loc, NEG_INF).reshape(B, H, rows, GRID_W, wr * GRID_W)
    s_ctx = jnp.einsum('brqhd,bchd->bhrqc', qg, k_ctx).astype(jnp.float32) * scale
    p = jax.nn.softmax(jnp.concatenate([s_loc, s_ctx], axis=-1), axis=-1).astype(v.dtype)
    n_loc = wr * GRID_W
    p_loc = p[..., :n_loc].reshape(B, H, rows, GRID_W, wr, GRID_W)
    out = (jnp.einsum('bhrqik,brikhd->brqhd', p_loc, vg)
           + jnp.einsum('bhrqc,bchd->brqhd', p[..., n_loc:], v_ctx))
    return out.reshape(B, S, H, Dh)

def context_attention(q, k, v):
    s = jnp.einsum('bqhd,bkhd->bhqk', q, k).astype(jnp.float32) * (HEAD_DIM ** -0.5)
    p = jax.nn.softmax(s, axis=-1).astype(v.dtype)
    return jnp.einsum('bhqk,bkhd->bqhd', p, v)

def context_kv(h_ctx, p):
    B, C, _ = h_ctx.shape
    k = (h_ctx @ p['w_in'][:, COL_K:COL_V] + p['b_in'][COL_K:COL_V]).reshape(B, C, NA_HEADS, HEAD_DIM)
    v = (h_ctx @ p['w_in'][:, COL_V:COL_G_HY] + p['b_in'][COL_V:COL_G_HY]).reshape(B, C, NA_HEADS, HEAD_DIM)
    return rmsnorm_2(k, p['k_norm_g']), v

def token_mixer(h, p, attend):
    B, L, _ = h.shape
    z = h @ p['w_in'] + p['b_in']
    q = rmsnorm_2(z[..., COL_Q:COL_K].reshape(B, L, NA_HEADS, HEAD_DIM), p['q_norm_g'])
    k = rmsnorm_2(z[..., COL_K:COL_V].reshape(B, L, NA_HEADS, HEAD_DIM), p['k_norm_g'])
    v = z[..., COL_V:COL_G_HY].reshape(B, L, NA_HEADS, HEAD_DIM)
    y_hy = hyena(z[..., COL_HY:COL_Q], p) @ p['w_hy_out']
    y_na = attend(q, k, v).reshape(B, L, D_NA) @ p['w_na_out']
    gate = jax.nn.sigmoid(z[..., COL_G_HY:N_PROJ].astype(jnp.float32)).astype(h.dtype)
    merged = gate[..., :D_MODEL] * y_hy + gate[..., D_MODEL:] * y_na
    return merged @ p['w_out']

def peer(h, p):
    B, L, D = h.shape
    T = B * L
    hf = h.reshape(T, D)
    q = (hf @ p['peer_w_q']).reshape(T, PEER_HEADS, 2, PEER_D_HALF)
    s = jnp.einsum('thpd,hpnd->thpn', q, p['peer_keys']).astype(jnp.float32)
    top_s, top_i = lax.top_k(s, PEER_TOPK)
    cand_s = (top_s[:, :, 0, :, None] + top_s[:, :, 1, None, :]).reshape(T, PEER_HEADS, PEER_TOPK * PEER_TOPK)
    cand_i = (top_i[:, :, 0, :, None] * PEER_N_KEYS + top_i[:, :, 1, None, :]).reshape(T, PEER_HEADS, PEER_TOPK * PEER_TOPK)
    best_s, best_pos = lax.top_k(cand_s, PEER_TOPK)
    idx = jnp.take_along_axis(cand_i, best_pos, axis=-1)
    g = jax.nn.softmax(best_s, axis=-1).astype(h.dtype)
    nb = T // PEER_BLOCK
    u_tab, v_tab = p['peer_u'], p['peer_v']

    def block(args):
        xb, ib, gb = args
        act = jax.nn.gelu(jnp.einsum('td,thkd->thk', xb, u_tab[ib]), approximate=False)
        return jnp.einsum('thk,thkd->td', gb * act, v_tab[ib])

    out = lax.map(block, (hf.reshape(nb, PEER_BLOCK, D),
                          idx.reshape(nb, PEER_BLOCK, PEER_HEADS, PEER_TOPK),
                          g.reshape(nb, PEER_BLOCK, PEER_HEADS, PEER_TOPK)))
    return out.reshape(B, L, D)

def second_inputs(seed: int = 0) -> dict:
    key = jax.random.key(seed)
    ks = jax.random.split(key, 32)
    f32 = jnp.float32

    def nrm(k, shape, scale):
        return jax.random.normal(k, shape, f32) * scale

    Ld = DEPTH
    return {
        'x': nrm(ks[0], (BATCH, SEQ, D_MODEL), 1.0),
        'c': nrm(ks[1], (BATCH, D_MODEL), 1.0),
        'ctx': nrm(ks[2], (BATCH, CTX_LEN, D_MODEL), 1.0),
        'c_ctx': nrm(ks[3], (D_MODEL,), 1.0),
        'norm1_g': 1.0 + nrm(ks[4], (Ld, D_MODEL), 0.02),
        'norm2_g': 1.0 + nrm(ks[5], (Ld, D_MODEL), 0.02),
        'w_ada': nrm(ks[6], (Ld, D_MODEL, N_MOD * D_MODEL), D_MODEL ** -0.5),
        'b_ada': nrm(ks[7], (Ld, N_MOD * D_MODEL), 0.02),
        'w_in': nrm(ks[8], (Ld, D_MODEL, N_PROJ), D_MODEL ** -0.5),
        'b_in': nrm(ks[9], (Ld, N_PROJ), 0.02),
        'hy_conv_w': nrm(ks[10], (Ld, 3, 3 * D_HY), 3 ** -0.5),
        'hy_conv_b': nrm(ks[11], (Ld, 3 * D_HY), 0.02),
        'hy_f1_w': nrm(ks[12], (Ld, HY_EMB, HY_FFN), HY_EMB ** -0.5),
        'hy_f1_b': nrm(ks[13], (Ld, HY_FFN), 0.02),
        'hy_f2_w': nrm(ks[14], (Ld, HY_FFN, HY_FFN), HY_FFN ** -0.5),
        'hy_f2_b': nrm(ks[15], (Ld, HY_FFN), 0.02),
        'hy_f3_w': nrm(ks[16], (Ld, HY_FFN, HY_FFN), HY_FFN ** -0.5),
        'hy_f3_b': nrm(ks[17], (Ld, HY_FFN), 0.02),
        'hy_f4_w': nrm(ks[18], (Ld, HY_FFN, HY_ORDER * 2 * D_HY), HY_FFN ** -0.5),
        'hy_sin_freq': 1.0 + nrm(ks[19], (Ld, HY_FFN), 0.02),
        'hy_skip': nrm(ks[20], (Ld, HY_ORDER, D_HY), 0.5),
        'q_norm_g': 1.0 + nrm(ks[21], (Ld, HEAD_DIM), 0.02),
        'k_norm_g': 1.0 + nrm(ks[22], (Ld, HEAD_DIM), 0.02),
        'na_rpb': nrm(ks[23], (Ld, NA_HEADS, 2 * WIN_ROWS - 1, 2 * WIN_COLS - 1), 0.02),
        'w_hy_out': nrm(ks[24], (Ld, D_HY, D_MODEL), D_HY ** -0.5),
        'w_na_out': nrm(ks[25], (Ld, D_NA, D_MODEL), D_NA ** -0.5),
        'w_out': nrm(ks[26], (Ld, D_MODEL, D_MODEL), D_MODEL ** -0.5),
        'peer_w_q': nrm(ks[27], (Ld, D_MODEL, PEER_HEADS * PEER_D_KEY), D_MODEL ** -0.5),
        'peer_keys': nrm(ks[28], (Ld, PEER_HEADS, 2, PEER_N_KEYS, PEER_D_HALF), PEER_D_HALF ** -0.5),
        'peer_u': nrm(ks[29], (Ld, PEER_N_EXPERTS, D_MODEL), D_MODEL ** -0.5),
        'peer_v': nrm(ks[30], (Ld, PEER_N_EXPERTS, D_MODEL), 0.5),
    }

def second_block(x, c, ctx, c_ctx, norm1_g, norm2_g, w_ada, b_ada, w_in, b_in, hy_conv_w, hy_conv_b,
              hy_f1_w, hy_f1_b, hy_f2_w, hy_f2_b, hy_f3_w, hy_f3_b, hy_f4_w, hy_sin_freq, hy_skip,
              q_norm_g, k_norm_g, na_rpb, w_hy_out, w_na_out, w_out, peer_w_q, peer_keys, peer_u, peer_v):
    for layer in range(DEPTH):
        p = {
            'norm1_g': norm1_g[layer], 'norm2_g': norm2_g[layer],
            'w_ada': w_ada[layer], 'b_ada': b_ada[layer],
            'w_in': w_in[layer], 'b_in': b_in[layer],
            'hy_conv_w': hy_conv_w[layer], 'hy_conv_b': hy_conv_b[layer],
            'hy_f1_w': hy_f1_w[layer], 'hy_f1_b': hy_f1_b[layer],
            'hy_f2_w': hy_f2_w[layer], 'hy_f2_b': hy_f2_b[layer],
            'hy_f3_w': hy_f3_w[layer], 'hy_f3_b': hy_f3_b[layer],
            'hy_f4_w': hy_f4_w[layer], 'hy_sin_freq': hy_sin_freq[layer], 'hy_skip': hy_skip[layer],
            'q_norm_g': q_norm_g[layer], 'k_norm_g': k_norm_g[layer], 'na_rpb': na_rpb[layer],
            'w_hy_out': w_hy_out[layer], 'w_na_out': w_na_out[layer], 'w_out': w_out[layer],
            'peer_w_q': peer_w_q[layer], 'peer_keys': peer_keys[layer],
            'peer_u': peer_u[layer], 'peer_v': peer_v[layer],
        }
        m_lat = adaln(c, p)
        m_ctx = adaln(c_ctx, p)
        sh1, sc1, g1, sh2, sc2, g2 = [m_lat[:, i:i + 1] for i in range(N_MOD)]
        ch1, cs1, cg1, ch2, cs2, cg2 = [m_ctx[i:i + 1] for i in range(N_MOD)]

        h_ctx = modulate(ctx, p['norm1_g'], ch1, cs1)
        k_ctx, v_ctx = context_kv(h_ctx, p)

        def attend_latent(q, k, v, k_ctx=k_ctx, v_ctx=v_ctx, rpb=p['na_rpb']):
            return neighbourhood_attention(axial_rope(q), axial_rope(k), v, k_ctx, v_ctx, rpb)

        h = modulate(x, p['norm1_g'], sh1, sc1)
        x_next = x + g1 * token_mixer(h, p, attend_latent)
        x_next = x_next + g2 * peer(modulate(x_next, p['norm2_g'], sh2, sc2), p)

        if layer + 1 < DEPTH:
            ctx_next = ctx + cg1 * token_mixer(h_ctx, p, context_attention)
            ctx = ctx_next + cg2 * peer(modulate(ctx_next, p['norm2_g'], ch2, cs2), p)
        x = x_next
    return x


def setup_inputs(seed=0):
    out = dict(first_inputs(seed))
    for name, value in second_inputs(seed + 1).items():
        if name != "x":
            out[name + "_2"] = value
    return out


def reference(
    x, mem, ffn1_pre_w, ffn1_w_gu, ffn1_w_down, ffn1_post_w, mix_pre_w, w_in, b_gate,
    hg_lb_logits, hg_norm_w, mem_norm_w, w_mem_kv, w_br_hg, w_br_dil, w_br_mem, w_out,
    mix_post_w, ffn2_pre_w, ffn2_w_gu, ffn2_w_down, ffn2_post_w, c_2, ctx_2, c_ctx_2, norm1_g_2,
    norm2_g_2, w_ada_2, b_ada_2, w_in_2, b_in_2, hy_conv_w_2, hy_conv_b_2, hy_f1_w_2, hy_f1_b_2,
    hy_f2_w_2, hy_f2_b_2, hy_f3_w_2, hy_f3_b_2, hy_f4_w_2, hy_sin_freq_2, hy_skip_2, q_norm_g_2,
    k_norm_g_2, na_rpb_2, w_hy_out_2, w_na_out_2, w_out_2, peer_w_q_2, peer_keys_2, peer_u_2,
    peer_v_2,
):
    x = first_block(
        x, mem, ffn1_pre_w, ffn1_w_gu, ffn1_w_down, ffn1_post_w, mix_pre_w, w_in, b_gate,
        hg_lb_logits, hg_norm_w, mem_norm_w, w_mem_kv, w_br_hg, w_br_dil, w_br_mem, w_out,
        mix_post_w, ffn2_pre_w, ffn2_w_gu, ffn2_w_down, ffn2_post_w,
    )
    return second_block(
        x, c_2, ctx_2, c_ctx_2, norm1_g_2, norm2_g_2, w_ada_2, b_ada_2, w_in_2, b_in_2,
        hy_conv_w_2, hy_conv_b_2, hy_f1_w_2, hy_f1_b_2, hy_f2_w_2, hy_f2_b_2, hy_f3_w_2,
        hy_f3_b_2, hy_f4_w_2, hy_sin_freq_2, hy_skip_2, q_norm_g_2, k_norm_g_2, na_rpb_2,
        w_hy_out_2, w_na_out_2, w_out_2, peer_w_q_2, peer_keys_2, peer_u_2, peer_v_2,
    )


_drawn_inputs = setup_inputs


def setup_inputs(seed=0):
    import zlib

    import numpy as np

    out = dict(_drawn_inputs(seed))
    spreads = {}
    factors = {'b_gate': 8.0,
     'hg_lb_logits': 15.286,
     'mem_norm_w': 4.099,
     'ctx_2': 2.671,
     'norm1_g_2': 6.239,
     'norm2_g_2': 27.408,
     'b_in_2': 5.068,
     'hy_conv_b_2': 6.41,
     'hy_f1_b_2': 8.0,
     'hy_f2_b_2': 6.565,
     'hy_f3_b_2': 5.721,
     'hy_sin_freq_2': 8.0,
     'q_norm_g_2': 60.191,
     'k_norm_g_2': 64.0,
     'na_rpb_2': 64.0,
     'hg_norm_w': 2.929,
     'peer_w_q_2': 2.71,
     'peer_u_2': 3.21,
     'peer_v_2': 2.69}
    for name, (base, spread) in spreads.items():
        noise = np.random.default_rng([zlib.crc32(name.encode()), seed]).standard_normal(out[name].shape)
        drawn = base * np.exp(spread * noise) if base else spread * noise
        out[name] = jnp.asarray(drawn.astype(out[name].dtype))
    for name, factor in factors.items():
        out[name] = (out[name] * factor).astype(out[name].dtype)
    return out
```

```python
from contextlib import ExitStack

import numpy as np

import concourse.bass as bass
from concourse import mybir

F32 = mybir.dt.float32
F32R = mybir.dt.float32r
U32 = mybir.dt.uint32
ALU = mybir.AluOpType
ACT = mybir.ActivationFunctionType
AX_X = mybir.AxisListType.X

P = 128
TOK = 512
TT = TOK // P
D = 1024
DC = D // P
EPS = 1e-6
FF = 2816
FC = FF // P
NMEM = 256
HEADS = 4
CH = 64
NCH = TOK // CH
HYC = 4
FB = 8
KB = 9
NAH = 8
TOPK = 16
EXP_GROUPS = 16
UNIT = 8
RING = 4
BIG = 3.0e38
MASKED = -1.0e30

PARTS = [
    ("ada", 48), ("ffn1_gu", 2 * FC), ("ffn1_down", DC * FC // UNIT),
    ("hg", 16), ("dil", 36), ("memkv", 8), ("mq", 4), ("merge1", 36), ("wout1", 8),
    ("ffn2_gu", 2 * FC), ("ffn2_down", DC * FC // UNIT),
    ("ctxkv", 8), ("hyk", KB), ("hyz", 12), ("hyc", 16), ("naqkv", 12), ("merge2", 24),
    ("wout2", 8), ("wq", 16), ("peer", 16 * EXP_GROUPS),
]
START = {}
_n = 0
for _name, _count in PARTS:
    START[_name] = _n
    _n += _count
TOTAL = _n

VECS = [
    ("ffn1_pre", 8), ("ffn1_post", 8), ("mix_pre", 8), ("mem_norm", 8), ("mix_post", 8),
    ("ffn2_pre", 8), ("ffn2_post", 8), ("norm1", 8), ("norm2", 8), ("b_gate", 24),
    ("lb0", 4), ("lb1", 4), ("hgn", 1), ("b_in2", 40), ("cw0", 12), ("cw1", 12), ("cw2", 12),
    ("cb", 12), ("qg", 1), ("kg", 1), ("b_ada", 48), ("cond", 16),
]
VCOL = {}
_n = 0
for _name, _count in VECS:
    VCOL[_name] = _n
    _n += _count
NVEC = _n


def attention_steps(kind):
    steps = []
    for h in range(NAH if kind == "na" else HEADS):
        for t in range(TT):
            if kind == "dil":
                ranges = [(max(0, P * (t - 1)), P * (t + 1)), (0, P * (t + 1)), (0, P * (t + 1))]
            elif kind == "mem":
                ranges = [(0, NMEM)]
            else:
                ranges = [(0, TOK), (0, NMEM)]
            steps.append((h, t, ranges))
    return steps


class Stepper:

    def __init__(self):
        self.step = 0
        self.told = 0
        self.block = 0
        self.units = 0

    def steps_(self, v):
        return v + UNIT * self.units if not isinstance(self.units, int) else v

    def units_(self, v):
        return v + self.units if not isinstance(self.units, int) else v

    def skip(self, units, blocks):
        self.step += UNIT * units
        self.told = self.step
        self.block += blocks
        self.units = 0


def wait(engine, sem, value):
    if not isinstance(value, int) or value > 0:
        engine.wait_ge(sem, value)


class Link:

    def __init__(self, engine, sem):
        self.engine, self.sem, self.n, self.turn = engine, sem, 0, 0

    def __call__(self, ins):
        self.n += 1
        ins.then_inc(self.sem, 1)
        self.engine.wait_ge(self.sem, self.n + self.turn if not isinstance(self.turn, int) else self.n)


def program(nc, a):
    with ExitStack() as ctx:
        cache = {}

        def sem(name):
            if name not in cache:
                cache[name] = ctx.enter_context(nc.semaphore(name))
            return cache[name]

        base = -(-nc.sbuf_base // 64) * 64
        fixed = [base]

        def place(name, shape, dt=F32, at=None):
            size = 4 * int(np.prod(shape[1:]))
            if at is None:
                at = fixed[0]
                fixed[0] += -(-size // 32) * 32
            return nc.alloc_sbuf_tensor_at(name, shape, dt, offset=at)

        HT = place("residual", [P, DC, TOK])
        RAW = place("weights_raw", [P, RING, UNIT * P])
        HI = place("weights_hi", [P, RING, UNIT * P], F32R)
        LO = place("weights_lo", [P, RING, UNIT * P], F32R)
        x_at = fixed[0]
        XH = place("operand_hi", [P, DC, TOK], F32R)
        XL = place("operand_lo", [P, DC, TOK], F32R)
        ONES = place("ones", [P, P])
        PAIR = place("pair_ones", [P, P])
        IDENT = place("identity", [P, P])
        VEC = place("vectors", [P, NVEC])
        SQ = place("squares", [P, 2, TOK])
        MS = place("mean_square", [P, TOK])
        RT = place("root", [P, TOK])
        RSTD = place("reciprocal_root", [P, TOK])
        LB = place("lower_bound", [P, 6, 4])
        MOD = place("modulation", [P, 48, 2])
        COEF = place("modulation_gain", [P, 3, DC])
        CS = place("cond_silu", [P, DC, 2])
        CSH = place("cond_hi", [P, DC, 2], F32R)
        CSL = place("cond_lo", [P, DC, 2], F32R)
        NMX = place("negated_max", [P, 2])
        SUM = place("exp_sum", [P, 2])
        RSUM = place("exp_sum_reciprocal", [P, 2])
        A0 = fixed[0]
        END = 229344
        Y2 = END - 32768
        Y3 = END - 49152
        assert END - A0 >= 98304, END - A0

        KBYTE = 1024
        FH = place("hidden_hi", [P, FC, TOK], F32R, A0)
        FL = place("hidden_lo", [P, FC, TOK], F32R, A0 + FC * 2048)
        SG = place("gate_silu", [P, 2, TOK], F32, A0 + FC * 4096)
        HF = place("hidden", [P, 2, TOK], F32, A0 + FC * 4096 + 4096)
        YT = place("branch_out", [P, DC, TOK], F32, x_at)
        XF = place("operand", [P, DC, TOK], F32, A0)

        ZQ, ZF, ZI, ZOG, KF, K2, B0, B1, Q1, K1, Q2, VT = [
            place(n, [P, HEADS, TOK], F32, A0 + i * 8192)
            for i, n in enumerate(["hg_q", "hg_f", "hg_i", "hg_og", "hg_k", "hg_k2", "hg_b0", "hg_b1",
                                   "hg_q1", "hg_k1", "hg_q2", "hg_v"])]
        K2T = place("hg_k2t", [P, HEADS, TOK], F32, A0 + 8192)
        SC = place("hg_scores", [P, HEADS, TT, P], F32, A0 + 2 * 8192)
        TRI = place("hg_causal", [P, 4, CH], U32, A0 + 12 * 8192 + 128)
        assert A0 + 12 * 8192 + 1152 <= END
        STATE = place("hg_state", [P, NCH, HEADS, P], F32, A0 + 6 * 8192)
        DEC = place("hg_decay", [P, HEADS * NCH], F32, A0 + 12 * 8192)
        OF = place("hg_out", [P, HEADS, TOK], F32, A0)
        YH = [place(f"branch{i}_hi", [P, 4, TOK], F32R, Y3 + i * 16384) for i in range(3)]
        YL = [place(f"branch{i}_lo", [P, 4, TOK], F32R, Y3 + i * 16384 + 8192) for i in range(3)]
        DZ = place("dil_qkv", [P, 9, TOK], F32, A0)
        DV = place("dil_v", [P, 3, TT, P], F32, A0 + 18432)
        DB = place("dil_bias", [P, 3, TOK], F32, A0 + 24576)
        DS = place("att_scores", [P, 2, 3 * TOK], F32, A0 + 30720)
        DP = place("att_probs_t", [P, 2, 4 * P], F32, A0 + 43008)
        DO = place("att_out", [P, HEADS, TOK], F32, Y3 + 2 * 16384)
        MT = place("memory", [P, DC, NMEM], F32, A0)
        MF = place("memory_operand", [P, DC, NMEM], F32, A0 + 8192)
        MH = place("memory_hi", [P, DC, NMEM], F32R, A0 + 16384)
        ML = place("memory_lo", [P, DC, NMEM], F32R, A0 + 24576)
        MKV = place("memory_kv", [P, 8, NMEM], F32, A0)
        MQ = place("memory_q", [P, 4, TOK], F32, A0 + 8192)
        MV = place("memory_v", [P, HEADS, 2, P], F32, A0 + 16384)
        MO = place("memory_out", [P, HEADS, TOK], F32, A0 + 20480)
        MG = place("merge_gates", [P, 6, TOK], F32, A0)
        MP = place("merge_products", [P, 3, TOK], F32, A0 + 12288)
        MY = place("merged", [P, DC, TOK], F32, A0 + 18432)
        CT = place("context", [P, DC, NMEM], F32, A0)
        CF = place("context_operand", [P, DC, NMEM], F32, A0 + 8192)
        CXH = place("context_hi", [P, DC, NMEM], F32R, A0 + 16384)
        CXL = place("context_lo", [P, DC, NMEM], F32R, A0 + 24576)
        CVF = place("context_vt", [P, 4, NMEM], F32, A0 + 32768)
        CK = place("context_k", [P, 4, NMEM], F32, END - 8192)
        CV = place("context_v", [P, 2, TOK], F32, END - 4096)
        KHAT = place("filter_dft", [P, 2, KB, TOK], F32, A0)
        W1 = A0 + 2 * KB * 2048
        FX = place("f_hidden", [64, TOK], F32, W1)
        FW4 = place("f4", [64, 2048], F32, W1 + 2048)
        FVEC = place("f_vectors", [64, 8], F32, W1 + 10240)
        FFW = place("filter_forward", [P, TT, TOK], F32, W1 + 10304)
        FBW = place("filter_backward", [P, TT, TOK], F32, W1 + 18496)
        FE = place("filter_even", [P, TT, TOK], F32, W1 + 26688)
        FAB = place("filter_abs", [P, 2, TOK], F32, W1 + 34880)
        DCY = place("filter_decay", [P, TT, TOK], F32, W1 + 38976)
        SKIP = place("hy_skip", [1, 2, TOK], F32, W1 + 47168)
        FTS = place("positions", [33, TOK], F32, W1 + 26688)
        FW1 = place("f1", [33, 64], F32, W1 + 28736)
        FW = place("f23", [64, 2, 64], F32, W1 + 28992)
        FA = place("f_argument", [64, 3, TOK], F32, W1 + 10304)
        assert W1 + 47168 + 4096 <= END - 8192
        EOH = place("filter_hi", [P, 8, TOK], F32R, x_at)
        EOL = place("filter_lo", [P, 8, TOK], F32R, x_at + 16384)
        HZ = place("hy_z", [P, 12, TOK], F32, W1)
        HCV = place("hy_conv", [P, 2, TOK], F32, W1 + 24576)
        HTM = place("hy_token_major", [P, 3, TT, TOK], F32, W1 + 28672)
        XF2 = place("operand_2", [P, DC, TOK], F32, W1)
        SH = place("signal_hi", [P, TT, TOK], F32R, W1)
        SL = place("signal_lo", [P, TT, TOK], F32R, W1 + 8192)
        HY = place("hy_out", [P, HYC, TOK], F32, W1 + 16384)
        SPH = place("spectrum_hi", [P, FB, TOK], F32R, x_at)
        SPL = place("spectrum_lo", [P, FB, TOK], F32R, x_at + 16384)
        Y2H = [place(f"second{i}_hi", [P, 4, TOK], F32R, Y2 + i * 16384) for i in range(2)]
        Y2L = [place(f"second{i}_lo", [P, 4, TOK], F32R, Y2 + i * 16384 + 8192) for i in range(2)]
        assert W1 + 53248 <= END - 8192
        NZ = place("na_qkv", [P, 12, TOK], F32, A0)
        NV = place("na_v", [P, TT, TOK], F32, A0 + 24576)
        COS = place("rope_cos", [P, TOK], F32, A0 + 32768)
        SIN = place("rope_sin", [P, TOK], F32, A0 + 34816)
        SWAP = place("rope_swap", [P, P], F32, A0 + 36864)
        CMASK = place("column_mask", [P, 64], F32, A0 + 37376)
        NB = place("na_bias", [P, 2, 14 * 64], F32, A0 + 37632)
        NS = place("na_scores", [P, 2, TOK + NMEM], F32, A0 + 44800)
        NP = place("na_probs_t", [P, 2, 4 * P], F32, A0 + 50944)
        NO = place("na_out", [P, HYC, TOK], F32, A0 + 55040)
        RP = place("rope_products", [P, 2, TOK], F32, A0 + 55040)
        assert A0 + 63232 <= Y2
        QT = place("peer_q", [P, 16, TOK], F32, A0)
        KEYS = place("peer_keys", [P, 16, P], F32, A0 + 32768)
        PS = place("peer_scores", [P, 16, P], F32, A0 + 40960)
        PR = place("peer_scores_rest", [P, 16, P], F32, A0 + 49152)
        CA = place("candidates", [P, 8, 256], F32, A0 + 57344)
        CR = place("candidates_rest", [P, 8, 256], F32, A0 + 65536)
        EQ = place("matches", [P, 8, 256], F32, A0 + 73728)
        s0 = A0 + 81920
        TOPS = place("top_scores", [P, 16, 16], F32, s0)
        TOPI = place("top_index", [P, 16, 16], U32, s0 + 1024)
        TOPF = place("top_index_f", [P, 16, 16], F32, s0 + 2048)
        BS = place("best_scores", [P, 8, 16], F32, s0 + 3072)
        BP = place("best_position", [P, 8, 16], U32, s0 + 3584)
        PA = place("position_parts", [P, 2, 8, 16], U32, s0 + 4096)
        PAF = place("position_parts_f", [P, 2, 8, 16], F32, s0 + 5120)
        IJG = place("expert_ijg", [P, 3, P], F32, s0 + 6144)
        IJGT = place("expert_ijg_t", [P, 3, TOK], F32, s0 + 7680)
        IOTA = place("iota", [P, P], F32, s0 + 13824)
        PSUMS = place("peer_sums", [P, 8], F32, s0 + 14336)
        PRS = place("peer_sums_reciprocal", [P, 8], F32, s0 + 14400)
        assert s0 + 14464 <= END
        OI = place("one_hot_i", [P, 8, P], F32, A0)
        OJ = place("one_hot_j", [P, 8, P], F32, A0 + 4096)
        STG = place("gate_stage", [P, 2, P, 16], F32, A0 + 8192)
        WH = place("expert_hi", [P, 8, TOK], F32R, A0)
        WL = place("expert_lo", [P, 8, TOK], F32R, A0 + 16384)
        ACC = place("peer_sum", [P, DC, TOK], F32, A0 + 32768)
        GG = place("expert_gates", [P, 32, 8, 16], F32, A0 + 49152)
        GE = place("expert_gelu", [P, 2, TOK], F32, A0 + 65536)
        WF = place("expert_act", [P, 2, TOK], F32, A0 + 69632)

        GD = nc.dram_tensor("peer_gates", [32, P, P, 16], F32, kind="Internal").ap()

        BANK = [ctx.enter_context(nc.psum_tensor(f"bank{i}", [P, TOK], F32)) for i in range(8)]
        SCB = [BANK[5], BANK[6]]
        TRB = [BANK[4], BANK[7]]
        OB = [BANK[2], BANK[3]]
        STB = BANK[4]

        def vec(name, c=0):
            return VEC[:, VCOL[name] + c:VCOL[name] + c + 1]

        block = ctx.enter_context(nc.Block())

        @block.sync
        def _(sp):
            sp.dma_start(VEC[:], a["vecs"]).then_inc(sem("vec_loaded"), 16)
            for n, (dst, src) in enumerate([(ONES, "ones"), (PAIR, "pair"), (IDENT, "ident")]):
                sp.dma_start(dst[:], a[src]).then_inc(sem("const_loaded"), 16)
            sp.dma_start(HT[:], a["x"]).then_inc(sem("x_loaded"), 16)

            def unit(src, n, slot):
                wait(sp, sem("lo_ready"), n - RING + 1)
                sp.dma_start(RAW[:, slot, :], src).then_inc(sem(f"raw_loaded{slot}"), 16)

            def part(name, first=0, count=None):
                n0, src = START[name] + first, a["w_" + name]
                count = (dict(PARTS)[name] if count is None else count)
                done = 0
                while count - done >= 8 and n0 + done < RING:
                    unit(src[first + done], n0 + done, (n0 + done) % RING)
                    done += 1
                turns = (count - done) // RING
                if turns > 1:
                    with sp.Fori(0, turns) as i:
                        for u in range(RING):
                            n = n0 + done + u
                            unit(src[first + done + u + RING * i], n + RING * i, n % RING)
                    done += turns * RING
                while done < count:
                    unit(src[first + done], n0 + done, (n0 + done) % RING)
                    done += 1

            for name, _ in PARTS[:-1]:
                part(name)
            part("peer", 0, RING)
            for s in range(2):
                sp.wait_ge(sem("stage_ready"), 4 * (s + 1))
                sp.dma_start(GD[s].rearrange("i j t -> i (j t)"),
                             STG[:, s].rearrange("p j t -> p (j t)")).then_inc(sem(f"stage_stored{s}"), 16)
            with sp.Fori(1, 16) as i:
                for s in range(2):
                    sp.wait_ge(sem("stage_ready"), 8 * i + 4 * (s + 1))
                    sp.dma_start(GD[2 * i + s].rearrange("i j t -> i (j t)"),
                                 STG[:, s].rearrange("p j t -> p (j t)")).then_inc(sem(f"stage_stored{s}"), 16)
            for s in range(2):
                sp.wait_ge(sem(f"stage_stored{s}"), 256)
            gates = GD.rearrange("b i j t -> i b j t")
            sp.dma_start(GG[:], gates[:, :, 0:8, :]).then_inc(sem("gates_loaded"), 16)
            n0, src = START["peer"], a["w_peer"]
            part("peer", RING, 8)
            sp.wait_ge(sem("gates_used"), 8)
            sp.dma_start(GG[:], gates[:, :, 8:16, :]).then_inc(sem("gates_loaded"), 16)
            with sp.Fori(0, EXP_GROUPS - 2) as g:
                for u in range(16):
                    n = n0 + 12 + u
                    unit(src[12 + u + 16 * g], n + 16 * g, n % RING)
                sp.wait_ge(sem("gates_used"), 8 * g + 16)
                sp.dma_start(GG[:], gates[:, :, bass.ds(8 * g + 16, 8), :]).then_inc(sem("gates_loaded"), 16)
            part("peer", 12 + 16 * (EXP_GROUPS - 2), 20)
            sp.wait_ge(sem("out_ready"), DC)
            sp.dma_start(a["out"], HT[:]).then_inc(sem("out_stored"), 16)
            sp.wait_ge(sem("out_stored"), 16)

        @block.gpsimd
        def _(pool):
            def low(n, slot):
                wait(pool, sem("hi_ready"), n + 1)
                wait(pool, sem("pe_steps"), UNIT * (n - RING + 1))
                pool.tensor_tensor(LO[:, slot, :], RAW[:, slot, :], HI[:, slot, :].bitcast(F32),
                                   ALU.subtract).then_inc(sem("lo_ready"), 1)

            for n in range(RING):
                low(n, n)
            with pool.Fori(1, TOTAL // RING) as i:
                for u in range(RING):
                    low(RING * i + u, u)
            for n in range(TOTAL // RING * RING, TOTAL):
                low(n, n % RING)

        @block.tensor
        def _(pe):
            st = Stepper()
            owner = {}
            n = {"square": 0, "sum": 0, "turn": 0, "piece": 0, "prob": 0, "ov": 0, "gate": 0,
                 "freed": 0, "ag": 0, "small": 0}

            def claim(b):
                if b in owner:
                    wait(pe, sem(owner[b][0]), owner[b][1])

            def block_(kc, hi, lo, width=TOK, gate=False, in_loop=False):
                b = st.block % 4
                for k in range(kc):
                    if st.step % UNIT == 0:
                        pe.wait_ge(sem("lo_ready"), st.units_(st.step // UNIT + 1))
                    if k == 0 and not in_loop:
                        claim(b)
                    slot, col = (st.step // UNIT) % RING, st.step % UNIT
                    wh = HI[:, slot, col * P:(col + 1) * P]
                    wl = LO[:, slot, col * P:(col + 1) * P]
                    out = BANK[b][:, 0:width]
                    pe.matmul(out, wh, hi(k), start=(k == 0), stop=False)
                    pe.matmul(out, wh, lo(k), start=False, stop=False)
                    ins = pe.matmul(out, wl, hi(k), start=False, stop=(k == kc - 1))
                    st.step += 1
                    if st.step % UNIT == 0 or k == kc - 1:
                        ins.then_inc(sem("pe_steps"), st.step - st.told)
                        st.told = st.step
                st.block += 1
                if gate:
                    n["gate"] += 1
                    owner[b] = ("gate_ready", n["gate"])
                elif not in_loop:
                    n["freed"] += 1
                    owner[b] = ("block_free", n["freed"])

            def x_ops():
                return (lambda k: XH[:, k, :]), (lambda k: XL[:, k, :])

            def operand(total):
                n["operand"] = n.get("operand", 0) + total
                pe.wait_ge(sem("operand_ready"), n["operand"])

            def sums(pieces, matrix, width, first_wait=None):
                claim(4)
                for c in range(pieces):
                    pe.wait_ge(sem("square_ready"), n["square"] + 1)
                    pe.matmul(STB[:, 0:width], matrix[:], SQ[:, n["square"] % 2, 0:width],
                              start=(c == 0), stop=(c == pieces - 1)).then_inc(sem("square_used"), 1)
                    n["square"] += 1
                n["sum"] += 1
                owner[4] = ("sum_read", n["sum"])

            def turn(sources):
                b = 4 if n["turn"] % 2 == 0 else 7
                claim(b)
                for i, src in enumerate(sources):
                    rows = src.shape[0]
                    ins = pe.transpose(BANK[b][0:src.shape[-1], i * P:i * P + rows], src, IDENT[0:rows, 0:rows])
                ins.then_inc(sem("turn_done"), 1)
                n["turn"] += 1
                owner[b] = ("turned", n["turn"])

            def ffn(name):
                operand(DC)
                hi, lo = x_ops()
                for b in range(4):
                    claim(b)
                freed = n["freed"]
                with pe.Fori(0, FC // 2) as i:
                    st.units = 4 * i
                    for u in range(4):
                        if u % 2 == 0:
                            pe.wait_ge(sem("block_free"), freed + 4 * i + u - 2)
                        block_(DC, hi, lo, in_loop=True)
                st.units = 0
                turns = FC // 2
                st.skip(4 * turns - 4, 4 * turns - 4)
                n["freed"] += 2 * FC
                for b in range(4):
                    owner[(st.block - 4 + b) % 4] = ("block_free", n["freed"])
                pe.wait_ge(sem("hidden_ready"), FC * (1 if name == "ffn1" else 2))
                for m in range(DC):
                    block_(FC, lambda k: FH[:, k, :], lambda k: FL[:, k, :])

            def attend(kind, h0=0, h1=None):
                steps = [s for s in attention_steps(kind) if h0 <= s[0] < (h1 or 99)]

                def scores(h, t, ranges):
                    for g, (k0, k1) in enumerate(ranges):
                        b = 5 + n["piece"] % 2
                        claim(b)
                        q0 = P * t
                        if kind == "dil":
                            lhs, rhs = DZ[:, g, q0:q0 + P], DZ[:, 3 + g, k0:k1]
                        elif kind == "mem":
                            lhs, rhs = MQ[:, h, q0:q0 + P], MKV[:, h, k0:k1]
                        else:
                            r0, c = 64 * (h % 2), h // 2
                            lhs = NZ[r0:r0 + 64, c, q0:q0 + P]
                            rhs = NZ[r0:r0 + 64, 4 + c, :] if g == 0 else CK[r0:r0 + 64, c, :]
                        pe.matmul(BANK[b][:, 0:k1 - k0], lhs, rhs, start=True, stop=True)\
                            .then_inc(sem("score_ready"), 1)
                        n["piece"] += 1
                        owner[b] = ("score_read", n["piece"])

                def values(h, t, ranges):
                    probs = (NS if kind == "na" else DS)[:, n["prob"] % 2]
                    n["prob"] += 1
                    pe.wait_ge(sem("prob_ready"), n["prob"])
                    cols, keys = 0, []
                    for g, (k0, k1) in enumerate(ranges):
                        for k in range(k0, k1, P):
                            if kind == "dil":
                                v = DV[:, g, k // P, :]
                            elif kind == "mem":
                                v = MV[:, h, k // P, :]
                            elif g == 0:
                                v = NV[:, k // P, 64 * h:64 * h + 64]
                            else:
                                v = CV[:, k // P, 64 * h:64 * h + 64]
                            keys.append((cols, v))
                            cols += P
                    b = 2 + n["ov"] % 2
                    claim(b)
                    r0, rows = (64 * (h % 2), 64) if kind == "na" else (0, P)
                    groups = [keys[i:i + 4] for i in range(0, len(keys), 4)]
                    base_ = n["turn"]
                    turn([probs[:, c:c + P] for c, _ in groups[0]])
                    for i, group in enumerate(groups):
                        if i + 1 < len(groups):
                            turn([probs[:, c:c + P] for c, _ in groups[i + 1]])
                        pe.wait_ge(sem("turned"), base_ + i + 1)
                        for j, (_, v) in enumerate(group):
                            ins = pe.matmul(BANK[b][r0:r0 + rows, 0:P], v,
                                            (NP if kind == "na" else DP)[:, n["ag"] % 2, j * P:(j + 1) * P],
                                            start=(i == 0 and j == 0),
                                            stop=(i == len(groups) - 1 and j == len(group) - 1))
                        ins.then_inc(sem("group_used"), 1)
                        n["ag"] += 1
                    n["ov"] += 1
                    owner[b] = ("out_read", n["ov"])

                before = None
                for s in steps:
                    scores(*s)
                    if before:
                        values(*before)
                    before = s
                values(*before)

            pe.wait_ge(sem("const_loaded"), 48)
            sums(DC, ONES, TOK)
            operand(1)
            for m in range(48):
                block_(DC, lambda k: CSH[:, k, :], lambda k: CSL[:, k, :], width=2)
            ffn("ffn1")
            sums(DC, ONES, TOK)
            sums(DC, ONES, TOK)
            operand(DC)
            for m in range(16):
                block_(DC, *x_ops())

            pe.wait_ge(sem("block_free"), n["freed"])
            for h in range(HEADS):
                turn([ZI[:, h, t * P:(t + 1) * P] for t in range(TT)])
            pe.wait_ge(sem("hg_factors_ready"), 1)
            for h in range(HEADS):
                turn([K2[:, h, t * P:(t + 1) * P] for t in range(TT)])
            for h in range(HEADS):
                b = 5 + h // 2
                if h % 2 == 0:
                    claim(b)
                for c in range(NCH):
                    r0, t = CH * (c % 2), c // 2
                    ins = pe.matmul(BANK[b][r0:r0 + CH, 256 * (h % 2) + CH * t:256 * (h % 2) + CH * t + CH],
                                    K1[:, h, CH * c:CH * c + CH], Q1[:, h, CH * c:CH * c + CH],
                                    start=True, stop=True)
                if h % 2:
                    ins.then_inc(sem("hg_scores_done"), 1)
                    owner[b] = ("hg_scores_read", h // 2 + 1)
            pe.wait_ge(sem("turned"), n["turn"])
            for c in range(NCH - 1):
                b, r0, t = c % 2, CH * (c % 2), c // 2
                claim(b)
                for h in range(HEADS):
                    ins = pe.matmul(BANK[b][:, h * P:(h + 1) * P], K2T[r0:r0 + CH, h, t * P:(t + 1) * P],
                                    VT[r0:r0 + CH, h, t * P:(t + 1) * P], start=True, stop=True)
                ins.then_inc(sem("kv_done"), 1)
                owner[b] = ("state_ready", c + 1)
            pe.wait_ge(sem("hg_scores_read"), 2)
            pe.wait_ge(sem("state_ready"), NCH - 1)
            for h in range(HEADS):
                b = 5 + h % 2
                claim(b)
                for t in range(TT):
                    pe.matmul(BANK[b][:, P * t:P * t + P], VT[:, h, t * P:(t + 1) * P], SC[:, h, t, :],
                              start=True, stop=False)
                    for c in range(max(1, 2 * t), 2 * t + 2):
                        ins = pe.matmul(BANK[b][:, CH * c:CH * c + CH], STATE[:, c, h, :],
                                        Q2[:, h, CH * c:CH * c + CH], start=False, stop=(c == 2 * t + 1))
                ins.then_inc(sem("hg_out_done"), 1)
                owner[b] = ("hg_out_read", h + 1)
            for h in range(HEADS):
                sums(1, ONES, TOK)

            for h in range(HEADS):
                for m in range(9):
                    block_(DC, *x_ops())
                pe.wait_ge(sem("block_free"), n["freed"])
                for g in range(3):
                    turn([DZ[:, 6 + g, t * P:(t + 1) * P] for t in range(TT)])
                attend("dil", h, h + 1)

            sums(DC, ONES, NMEM)
            operand(4 + 4 + DC)
            for m in range(8):
                block_(DC, lambda k: MH[:, k, :], lambda k: ML[:, k, :], width=NMEM)
            for m in range(4):
                block_(DC, *x_ops())
            pe.wait_ge(sem("block_free"), n["freed"])
            for h in range(HEADS):
                turn([MKV[:, 4 + h, t * P:(t + 1) * P] for t in range(2)])
            attend("mem")

            operand(4)
            for m in range(DC // 2):
                for _ in range(6):
                    block_(DC, *x_ops(), gate=True)
                for _ in range(2):
                    for br in range(3):
                        block_(4, lambda k: YH[br][:, k, :], lambda k: YL[br][:, k, :])
            operand(DC)
            for m in range(DC):
                block_(DC, *x_ops())
            sums(DC, ONES, TOK)
            sums(DC, ONES, TOK)
            ffn("ffn2")
            sums(DC, ONES, TOK)

            sums(DC, ONES, NMEM)
            operand(DC)
            for m in range(8):
                block_(DC, lambda k: CXH[:, k, :], lambda k: CXL[:, k, :], width=NMEM)
            for c in range(4):
                sums(1, PAIR, NMEM)
            pe.wait_ge(sem("block_free"), n["freed"])
            for t in range(2):
                turn([CVF[:, c, t * P:(t + 1) * P] for c in range(4)])

            pe.wait_ge(sem("filter_weights_loaded"), 80)
            for layer in range(3):
                if layer:
                    pe.wait_ge(sem("sin_ready"), layer)
                claim(5)
                lhs = FW1[0:33, :] if layer == 0 else FW[:, layer - 1, :]
                rhs = FTS[0:33, :] if layer == 0 else FX[:]
                pe.matmul(BANK[5][0:64, :], lhs, rhs, start=True, stop=True).then_inc(sem("layer_done"), 1)
                owner[5] = ("layer_read", layer + 1)
            pe.wait_ge(sem("sin_ready"), 3)
            for o in range(2):
                for t in range(TT):
                    for d in range(2):
                        b = 5 + n["small"] % 2
                        claim(b)
                        pe.matmul(BANK[b][:], FX[:, t * P:(t + 1) * P],
                                  FW4[:, (2 * o + d) * TOK:(2 * o + d + 1) * TOK], start=True, stop=True)\
                            .then_inc(sem("filter_done"), 1)
                        n["small"] += 1
                        owner[b] = ("filter_read", n["small"])
                claim(7)
                for i in range(2 * TT):
                    pe.wait_ge(sem("abs_ready"), 8 * o + i + 1)
                    pe.matmul(BANK[7][:], ONES[:], FAB[:, i % 2, :], start=(i == 0), stop=(i == 2 * TT - 1))\
                        .then_inc(sem("abs_used"), 1)
                owner[7] = ("norm_read", o + 1)
                operand(8)
                for m in range(KB):
                    e0 = 0 if m < 5 else 4
                    block_(TT, lambda k: EOH[:, e0 + k, :], lambda k: EOL[:, e0 + k, :])

            sums(DC, ONES, TOK)
            operand(DC)
            for m in range(12):
                block_(DC, *x_ops())
            for c in range(12):
                pe.wait_ge(sem("conv_ready"), c + 1)
                turn([HCV[:, c % 2, t * P:(t + 1) * P] for t in range(TT)])
            for o in range(2):
                operand(TT)
                for m in range(FB):
                    block_(TT, lambda k: SH[:, k, :], lambda k: SL[:, k, :])
                operand(FB)
                for m in range(TT):
                    block_(FB, lambda k: SPH[:, k, :], lambda k: SPL[:, k, :])
            pe.wait_ge(sem("block_free"), n["freed"])
            for t in range(TT):
                turn([HTM[:, 0, t, c * P:(c + 1) * P] for c in range(HYC)])

            operand(4 + DC)
            for m in range(12):
                block_(DC, *x_ops())
            pe.wait_ge(sem("rope_loaded"), 64)
            for c in range(8):
                sums(1, PAIR, TOK)
                pe.wait_ge(sem("normed_ready"), c + 1)
                claim(5)
                pe.matmul(BANK[5][:], SWAP[:], NZ[:, c, :], start=True, stop=True).then_inc(sem("swap_done"), 1)
                owner[5] = ("swap_read", c + 1)
            for t in range(TT):
                turn([NZ[:, 8 + c, t * P:(t + 1) * P] for c in range(4)])
            pe.wait_ge(sem("na_ready"), 1)
            attend("na")

            operand(4)
            for m in range(DC):
                for _ in range(2):
                    block_(DC, *x_ops(), gate=True)
                for br in range(2):
                    block_(4, lambda k: Y2H[br][:, k, :], lambda k: Y2L[br][:, k, :])
            operand(DC)
            for m in range(DC):
                block_(DC, *x_ops())
            sums(DC, ONES, TOK)

            operand(DC)
            for m in range(16):
                block_(DC, *x_ops())
            pe.wait_ge(sem("keys_loaded"), 16)
            pe.wait_ge(sem("block_free"), n["freed"])
            for t in range(TT):
                for q in range(4):
                    b = 5 + n["piece"] % 2
                    claim(b)
                    for j in range(4):
                        ins = pe.matmul(BANK[b][:, j * P:(j + 1) * P], QT[:, 4 * q + j, t * P:(t + 1) * P],
                                        KEYS[:, 4 * q + j, :], start=True, stop=True)
                    ins.then_inc(sem("score_ready"), 1)
                    n["piece"] += 1
                    owner[b] = ("score_read", n["piece"])
                pe.wait_ge(sem("best_ready"), t + 1)
                turn([IJG[:, i, :] for i in range(3)])
            pe.wait_ge(sem("turned"), n["turn"])

            for b in (5, 6):
                claim(b)

            def gates_of(i, q):
                for u in range(4):
                    ins = pe.matmul(BANK[5 + q][:, u * P:(u + 1) * P], OI[:, 4 * q + u, :], OJ[:, 4 * q + u, :],
                                    start=True, stop=True)
                ins.then_inc(sem("gates_done"), 1)

            for q in range(2):
                pe.wait_ge(sem("hot_ready"), q + 1)
                gates_of(0, q)
            with pe.Fori(1, TOK // 8) as i:
                for q in range(2):
                    pe.wait_ge(sem("hot_ready"), 2 * i + q + 1)
                    pe.wait_ge(sem("stage_ready"), 2 * i + q - 1)
                    gates_of(i, q)
            for b in (5, 6):
                owner[b] = ("stage_ready", TOK // 4)

            for b in range(4):
                claim(b)
            freed = n["freed"]

            def group(g):
                for m in range(8):
                    pe.wait_ge(sem("block_free"), freed + 16 * g + m - 3)
                    block_(DC, *x_ops(), in_loop=True)
                pe.wait_ge(sem("expert_ready"), 8 * g + 8)
                for m in range(8):
                    pe.wait_ge(sem("block_free"), freed + 16 * g + 8 + m - 3)
                    block_(8, lambda k: WH[:, k, :], lambda k: WL[:, k, :], in_loop=True)

            with pe.Fori(0, EXP_GROUPS) as g:
                st.units = 16 * g
                group(g)
            st.units = 0

        @block.scalar
        def _(act):
            n = {"unit": 0, "square": 0, "sum": 0, "turn": 0, "ag": 0, "ov": 0, "f": 0, "gate": 0,
                 "exp": 0, "freed": 0, "h": 0}

            def split(k, shift=0):
                if isinstance(shift, int):
                    k += shift
                slot = k % RING
                loaded, used = 16 * (k // RING + 1), UNIT * (k - RING + 1)
                if isinstance(shift, int):
                    wait(act, sem(f"raw_loaded{slot}"), loaded)
                    wait(act, sem("pe_steps"), used)
                else:
                    act.wait_ge(sem(f"raw_loaded{slot}"), loaded + 4 * shift)
                    act.wait_ge(sem("pe_steps"), used + UNIT * shift)
                act.activation(HI[:, slot, :], RAW[:, slot, :], ACT.Copy).then_inc(sem("hi_ready"), 1)

            def units(count):
                for _ in range(count):
                    if n["unit"] + 3 < TOTAL:
                        split(n["unit"] + 3)
                    n["unit"] += 1

            def square(src, width, sem_name, value):
                act.wait_ge(sem(sem_name), value)
                wait(act, sem("square_used"), n["square"] - 1)
                act.activation(SQ[:, n["square"] % 2, 0:width], src, ACT.Square)\
                    .then_inc(sem("square_ready"), 1)
                n["square"] += 1

            def root(width):
                n["sum"] += 1
                act.wait_ge(sem("sum_read"), n["sum"])
                act.activation(RT[:, 0:width], MS[:, 0:width], ACT.Sqrt).then_inc(sem("root_ready"), 1)

            def high(dst, src):
                n["f"] += 1
                act.wait_ge(sem("piece_made"), n["f"])
                act.activation(dst, src, ACT.Copy).then_inc(sem("piece_high"), 1)

            def highs(hi, src, count):
                for c in range(count):
                    high(hi[:, c, :], src[:, c, :])

            def highs_after(hi, src, count, name, first, each=0):
                for c in range(count):
                    act.wait_ge(sem(name), first + each * c)
                    act.activation(hi[:, c, :], src[:, c, :], ACT.Copy).then_inc(sem("piece_high"), 1)

            def turned(dst, view=None):
                b = 4 if n["turn"] % 2 == 0 else 7
                n["turn"] += 1
                act.wait_ge(sem("turn_done"), n["turn"])
                cols = int(np.prod(dst.shape[1:]))
                src = BANK[b][0:dst.shape[0], 0:cols]
                if len(dst.shape) == 3:
                    src = src.rearrange("p (a b) -> p a b", a=dst.shape[1])
                act.activation(dst, src, ACT.Copy).then_inc(sem("turned"), 1)

            def ffn(name, freed0):
                n0 = n["unit"]
                with act.Fori(0, FC // 2) as i:
                    for u in range(4):
                        split(n0 + 3 + u, 4 * i)
                        if u % 2:
                            act.wait_ge(sem("pe_steps"), UNIT * (n0 + u) + UNIT * 4 * i)
                            act.wait_ge(sem("block_free"), freed0 + 4 * i + u - 3)
                            b = (n0_block[0] + u - 1) % 4
                            act.activation(SG[:, u // 2, :], BANK[b][:], ACT.Silu)\
                                .then_inc(sem("silu_ready"), 1)
                n["unit"] += 2 * FC
                n["freed"] = freed0 + 2 * FC
                n0_block[0] += 2 * FC
                units(DC * FC // UNIT)
                n["freed"] += DC
                n0_block[0] += DC

            n0_block = [0]

            def blocks(count, kc=DC):
                units(count * kc // UNIT)
                n0_block[0] += count
                n["freed"] += count

            def residual_squares():
                for c in range(DC):
                    square(HT[:, c, :], TOK, "h_ready", n["h"] + c + 1)
                n["h"] += DC
                root(TOK)

            def branch_squares(src):
                for c in range(DC):
                    square(src[:, c, :], TOK, "block_free", n["freed"] - DC + c + 1)
                root(TOK)

            def bias(h):
                if h > 1:
                    act.wait_ge(sem("score_read"), na_pieces[0] + 8 * (h - 1))
                act.dma_start(NB[:, h % 2, :], a["na_bias"][h]).then_inc(sem(f"na_bias_loaded{h % 2}"), 16)

            na_pieces = [HEADS * TT * 3 + HEADS * TT]

            def attend(kind, h0=0, h1=99):
                steps = [s for s in attention_steps(kind) if h0 <= s[0] < h1]
                S = NS if kind == "na" else DS
                T = NP if kind == "na" else DP

                def exps(h, t, ranges):
                    width, e = sum(k1 - k0 for k0, k1 in ranges), n["exp"] % 2
                    n["exp"] += 1
                    act.wait_ge(sem("max_ready"), n["exp"])
                    act.activation(S[:, e, 0:width], S[:, e, 0:width], ACT.Exp, bias=NMX[:, e:e + 1],
                                   accum_out=SUM[:, e:e + 1]).then_inc(sem("exp_ready"), 1)

                def transposed(h, t, ranges):
                    left = sum(k1 - k0 for k0, k1 in ranges) // P
                    while left:
                        k = min(4, left)
                        left -= k
                        wait(act, sem("group_used"), n["ag"] - 1)
                        turned(T[:, n["ag"] % 2, 0:k * P])
                        n["ag"] += 1

                def out(h, t, ranges):
                    groups = -(-(sum(k1 - k0 for k0, k1 in ranges) // P) // 4)
                    out_groups[0] += groups
                    act.wait_ge(sem("group_used"), out_groups[0])
                    b = 2 + n["ov"] % 2
                    n["ov"] += 1
                    if kind == "na":
                        r0 = 64 * (h % 2)
                        dst, src = NO[r0:r0 + 64, h // 2, t * P:(t + 1) * P], BANK[b][r0:r0 + 64, 0:P]
                    else:
                        dst, src = (DO if kind == "dil" else MO)[:, h, t * P:(t + 1) * P], BANK[b][:, 0:P]
                    act.activation(dst, src, ACT.Copy).then_inc(sem("out_read"), 1)

                before = None
                for s in steps:
                    if kind == "na" and s[1] == 1 and s[0] + 1 < NAH:
                        bias(s[0] + 1)
                    exps(*s)
                    if before:
                        transposed(*before)
                        out(*before)
                    before = s
                transposed(*before)
                out(*before)

            out_groups = [0]

            for k in range(3):
                split(k)
            act.wait_ge(sem("vec_loaded"), 16)
            c0 = VCOL["cond"]
            act.activation(CS[:].rearrange("p a b -> p (a b)"), VEC[:, c0:c0 + 16], ACT.Silu)\
                .then_inc(sem("cond_ready"), 1)
            act.wait_ge(sem("lb_shifted"), 1)
            act.activation(LB[:, 3:5, :], LB[:, 1:3, :], ACT.Exp).then_inc(sem("lb_exp"), 1)
            for c in range(DC):
                square(HT[:, c, :], TOK, "x_loaded", 16)
            root(TOK)
            highs(XH, XF, DC)
            blocks(48)
            ffn("ffn1", n["freed"])
            branch_squares(YT)
            residual_squares()
            highs(XH, XF, DC)
            blocks(16)
            act.wait_ge(sem("block_free"), n["freed"])
            act.activation(ZQ[:], ZQ[:], ACT.Silu).then_inc(sem("hg_q_ready"), 1)
            act.activation(ZF[:], ZF[:], ACT.Sigmoid).then_inc(sem("hg_sigmoid"), 1)
            act.activation(ZOG[:], ZOG[:], ACT.Sigmoid).then_inc(sem("hg_og_ready"), 1)
            for h in range(HEADS):
                turned(VT[:, h, :])
            act.dma_start(TRI[:], a["tri"]).then_inc(sem("tri_loaded"), 16)
            act.wait_ge(sem("hg_f_ready"), 1)
            act.activation(B0[:], ZF[:], ACT.Ln).then_inc(sem("hg_log"), 1)
            act.wait_ge(sem("hg_shift"), 1)
            act.activation(Q1[:], B1[:], ACT.Exp).then_inc(sem("hg_exp"), 1)
            act.activation(K1[:], B1[:], ACT.Exp, scale=-1.0).then_inc(sem("hg_exp"), 1)
            act.activation(Q2[:], B0[:], ACT.Exp).then_inc(sem("hg_exp"), 1)
            last = B0[:].rearrange("p h (n c) -> p (h n) c", c=CH)[:, :, CH - 1]
            act.activation(DEC[:], last, ACT.Exp).then_inc(sem("hg_exp"), 1)
            act.wait_ge(sem("hg_shift"), 2)
            act.activation(K2[:], B1[:], ACT.Exp).then_inc(sem("hg_exp"), 1)
            for h in range(HEADS):
                turned(K2T[:, h, :])
            for h in range(HEADS):
                square(OF[:, h, :], TOK, "hg_out_read", h + 1)
                root(TOK)
            highs(YH[0], OF, 4)

            for h in range(HEADS):
                if h:
                    act.wait_ge(sem("score_read"), 12 * h)
                act.dma_start(DB[:], a["dil_bias"][h]).then_inc(sem("bias_loaded"), 16)
                blocks(9)
                for g in range(3):
                    turned(DV[:, g].rearrange("p t d -> p (t d)"))
                attend("dil", h, h + 1)
            highs_after(YH[1], DO, 4, "out_read", n["ov"])

            act.wait_ge(sem("group_used"), out_groups[0])
            act.dma_start(MT[:], a["mem"]).then_inc(sem("mem_loaded"), 16)
            for c in range(DC):
                square(MT[:, c, :], NMEM, "mem_loaded", 16)
            root(NMEM)
            highs(MH, MF, DC)
            blocks(8)
            blocks(4)
            for h in range(HEADS):
                turned(MV[:, h].rearrange("p t d -> p (t d)"))
            attend("mem")
            highs_after(YH[2], MO, 4, "out_read", n["ov"])

            def gate(dst, bias):
                b = n0_block[0] % 4
                units(1)
                act.wait_ge(sem("pe_steps"), UNIT * n["unit"])
                act.activation(dst, BANK[b][:], ACT.Sigmoid, bias=bias).then_inc(sem("gate_ready"), 1)
                n["gate"] += 1
                n0_block[0] += 1

            for m in range(DC // 2):
                wait(act, sem("block_free"), n["freed"])
                for i in range(2):
                    for br in range(3):
                        gate(MG[:, 3 * i + br, :], vec("b_gate", br * DC + 2 * m + i))
                blocks(6, 4)
            highs(XH, MY, DC)
            blocks(DC)
            branch_squares(XF)
            residual_squares()
            highs(XH, XF, DC)
            ffn("ffn2", n["freed"])
            branch_squares(YT)

            act.wait_ge(sem("h_ready"), n["h"] + DC)
            act.dma_start(CT[:], a["ctx"]).then_inc(sem("ctx_loaded"), 16)
            for dst, name in ((FTS, "feats"), (FW1, "f1"), (FW, "f23"), (FW4, "f4"), (FVEC, "fvec")):
                act.dma_start(dst[:], a[name]).then_inc(sem("filter_weights_loaded"), 16)
            act.dma_start(DCY[:], a["decay"]).then_inc(sem("decay_loaded"), 16)
            act.dma_start(SKIP[:], a["skip"]).then_inc(sem("decay_loaded"), 16)
            for c in range(DC):
                square(CT[:, c, :], NMEM, "ctx_loaded", 16)
            root(NMEM)
            highs(CXH, CF, DC)
            blocks(8)
            for c in range(4):
                square(CK[:, c, :], NMEM, "block_free", n["freed"] - 7 + c)
                root(NMEM)
            for t in range(2):
                turned(CV[:, t, :])

            for layer in range(3):
                act.wait_ge(sem("angle_ready"), layer + 1)
                act.activation(FX[:], FA[:, 0, :], ACT.Sin).then_inc(sem("sin_ready"), 1)
            for o in range(2):
                for i in range(2 * TT):
                    t, d = i // 2, i % 2
                    act.wait_ge(sem("filter_read"), 8 * o + i + 1)
                    wait(act, sem("abs_used"), 8 * o + i - 1)
                    act.activation(FAB[:, i % 2, :], (FBW if d else FFW)[:, t, :], ACT.Abs)\
                        .then_inc(sem("abs_ready"), 1)
                highs(EOH[:, 0:4, :], FE, 4)
                highs(EOH[:, 4:8, :], FFW, 4)
                units(4 + o)
                n0_block[0] += KB
                n["freed"] += KB

            for c in range(DC):
                square(HT[:, c, :], TOK, "h_ready", n["h"] + c + 1)
            root(TOK)
            highs(XH, XF2, DC)
            blocks(12)
            for c in range(12):
                turned(HTM[:, c // 4, :, (c % 4) * P:(c % 4 + 1) * P])
            for o in range(2):
                if o == 0:
                    highs_after(SH, HTM[:, 0], TT, "turned", n["turn"])
                else:
                    highs_after(SH, HTM[:, 0], TT, "block_free", n["freed"] - TT + 1, 1)
                for i in range(4):
                    blocks(2, TT)
                    for j in range(2):
                        high(SPH[:, 2 * i + j, :], SQ[:, j, :])
                blocks(TT, FB)
            for t in range(TT):
                turned(HY[:, :, t * P:(t + 1) * P])
            highs_after(Y2H[0], HY, 4, "turned", n["turn"])
            highs(XH, XF, DC)

            for dst, name in ((COS, "cos"), (SIN, "sin"), (SWAP, "swap"), (CMASK, "cmask")):
                act.dma_start(dst[:], a[name]).then_inc(sem("rope_loaded"), 16)
            bias(0)
            blocks(12)
            for c in range(8):
                square(NZ[:, c, :], TOK, "block_free", n["freed"] - 12 + c + 1)
                root(TOK)
            for t in range(TT):
                turned(NV[:, t, :])
            attend("na")
            highs_after(Y2H[1], NO, 4, "out_read", n["ov"])
            for m in range(DC):
                act.wait_ge(sem("block_free"), n["freed"] - (2 if m else 0))
                for br in range(2):
                    gate(MG[:, 2 * (m % 2) + br, :], vec("b_in2", 24 + br * DC + m))
                blocks(2, 4)
            highs(XH, MY, DC)
            blocks(DC)
            branch_squares(HT)

            highs(XH, XF, DC)
            blocks(16)
            act.dma_start(KEYS[:], a["keys"]).then_inc(sem("keys_loaded"), 16)
            act.dma_start(IOTA[:], a["iota"]).then_inc(sem("iota_loaded"), 16)
            for t in range(TT):
                act.wait_ge(sem("best_shift"), t + 1)
                act.activation(BS[:], BS[:], ACT.Exp).then_inc(sem("best_exp"), 1)
                turned(IJGT[:, :, t * P:(t + 1) * P])

            def stage(s, q, done, stored):
                act.wait_ge(sem("gates_done"), done)
                if stored is not None:
                    act.wait_ge(sem(f"stage_stored{s}"), stored)
                act.activation(STG[:, s, :, 4 * q:4 * q + 4].rearrange("p j t -> p t j"),
                               BANK[5 + q % 2][:].rearrange("p (t j) -> p t j", t=4), ACT.Copy)\
                    .then_inc(sem("stage_ready"), 1)

            for s in range(2):
                for q in range(4):
                    stage(s, q, 4 * s + q + 1, None)
            with act.Fori(1, 16) as i:
                for s in range(2):
                    for q in range(4):
                        stage(s, q, 8 * i + 4 * s + q + 1, 16 * i)

            n0 = n["unit"]

            def gelus(g, shift, tail):
                for u in range(16):
                    if not tail or u + 3 < 16:
                        split(n0 + 3 + u, shift)
                    if u < 8:
                        act.wait_ge(sem("pe_steps"), UNIT * (n0 + u + 1) + UNIT * shift)
                        wait(act, sem("gates_used"), 8 * g + u - 1)
                        act.activation(GE[:, u % 2, :], BANK[(n0_block[0] + u) % 4][:], ACT.Gelu)\
                            .then_inc(sem("gelu_ready"), 1)

            gelus(0, 0, False)
            with act.Fori(1, EXP_GROUPS - 1) as g:
                gelus(g, 16 * g, False)
            gelus(EXP_GROUPS - 1, 16 * (EXP_GROUPS - 1), True)

        @block.vector
        def _(dve):
            st = Stepper()
            n = {"freed": 0, "square": 0, "sum": 0, "high": 0, "piece": 0, "exp": 0, "product": 0,
                 "gate": 0, "groups": [], "operand": 1, "made": 0}
            link = Link(dve, sem("dve_order"))

            def done(kc):
                st.step += kc
                dve.wait_ge(sem("pe_steps"), st.steps_(st.step))
                b = st.block % 4
                st.block += 1
                return BANK[b]

            def free(ins, count=1):
                n["freed"] += count
                ins.then_inc(sem("block_free"), count)

            def evacuated():
                dve.wait_ge(sem("block_free"), n["freed"])

            def copy_blocks(dst, count, kc=DC, width=TOK, bias=None):
                for m in range(count):
                    bank = done(kc)
                    if bias is None:
                        free(dve.tensor_copy(dst[:, m, 0:width], bank[:, 0:width]))
                    else:
                        free(dve.tensor_scalar(dst[:, m, 0:width], bank[:, 0:width], bias(m), None, ALU.add))

            def rstd(pieces, denom, width):
                n["square"] += pieces
                n["sum"] += 1
                dve.wait_ge(sem("square_used"), n["square"])
                dve.tensor_scalar(MS[:, 0:width], STB[:, 0:width], 1.0 / denom, EPS, ALU.mult, ALU.add)\
                    .then_inc(sem("sum_read"), 1)
                dve.wait_ge(sem("root_ready"), n["sum"])
                link(dve.reciprocal(RSTD[:, 0:width], RT[:, 0:width]))

            def made(ins):
                ins.then_inc(sem("piece_made"), 1)
                n["made"] += 1

            def low(dst, src, high):
                n["high"] += 1
                dve.wait_ge(sem("piece_high"), n["high"])
                dve.tensor_tensor(dst, src, high.bitcast(F32), ALU.subtract).then_inc(sem("operand_ready"), 1)
                n["operand"] += 1

            def lows(lo, src, hi, count):
                for c in range(count):
                    low(lo[:, c, :], src[:, c, :], hi[:, c, :])
                dve.wait_ge(sem("operand_ready"), n["operand"])

            def normed(dst, src, hi, lo, width, gain, shift=None):
                for c in range(DC):
                    ins = dve.scalar_tensor_tensor(dst[:, c, :], src[:, c, :], gain(c), RSTD[:, 0:width],
                                                   ALU.mult, ALU.mult)
                    if shift is None:
                        made(ins)
                    else:
                        link(ins)
                        made(dve.tensor_scalar(dst[:, c, :], dst[:, c, :], shift(c), None, ALU.add))
                lows(lo, dst, hi, DC)

            def post(src, name, factor):
                for c in range(DC):
                    link(dve.scalar_tensor_tensor(src[:, c, :], src[:, c, :], vec(name, c), RSTD[:],
                                                  ALU.mult, ALU.mult))
                    dve.scalar_tensor_tensor(HT[:, c, :], src[:, c, :], factor, HT[:, c, :],
                                             ALU.mult, ALU.add).then_inc(sem("h_ready"), 1)

            def ffn(k):
                s0, b0, freed0 = st.step, st.block, n["freed"]
                with dve.Fori(0, FC // 2) as i:
                    for p in range(2):
                        dve.wait_ge(sem("pe_steps"), s0 + UNIT * (2 * p + 2) + 4 * UNIT * i)
                        dve.wait_ge(sem("silu_ready"), FC * k + 2 * i + p + 1)
                        dve.tensor_tensor(HF[:, p, :], SG[:, p, :], BANK[(b0 + 2 * p + 1) % 4][:], ALU.mult)\
                            .then_inc(sem("block_free"), 2)
                        dve.wait_ge(sem("block_free"), freed0 + 4 * i + 2 * p + 2)
                        dve.tensor_copy(FH[:, 2 * i + p, :], HF[:, p, :]).then_inc(sem("hidden_high"), 1)
                        dve.wait_ge(sem("hidden_high"), FC * k + 2 * i + p + 1)
                        dve.tensor_tensor(FL[:, 2 * i + p, :], HF[:, p, :], FH[:, 2 * i + p, :].bitcast(F32),
                                          ALU.subtract).then_inc(sem("hidden_ready"), 1)
                st.skip(2 * FC, 2 * FC)
                n["freed"] += 2 * FC
                copy_blocks(YT, DC, FC)

            def attend(kind, h0=0, h1=99):
                steps = [s for s in attention_steps(kind) if h0 <= s[0] < h1]
                S = NS if kind == "na" else DS
                scale = 0.125 if kind == "na" else P ** -0.5

                def scores(h, t, ranges):
                    e = n["exp"] % 2
                    if n["exp"] >= 2:
                        dve.wait_ge(sem("group_used"), n["groups"][n["exp"] - 2])
                    col = 0
                    for g, (k0, k1) in enumerate(ranges):
                        bank = SCB[n["piece"] % 2]
                        n["piece"] += 1
                        dve.wait_ge(sem("score_ready"), n["piece"])
                        w = k1 - k0
                        dst = S[:, e, col:col + w]
                        if kind == "dil":
                            x0 = k0 + (TOK - P) - P * t
                            ins = dve.scalar_tensor_tensor(dst, bank[:, 0:w], scale, DB[:, g, x0:x0 + w],
                                                           ALU.mult, ALU.add)
                        elif kind == "na" and g == 0:
                            ins = dve.scalar_tensor_tensor(dst, bank[:, 0:w], scale,
                                                           NB[:, h % 2, 64 * (6 - 2 * t):64 * (14 - 2 * t)],
                                                           ALU.mult, ALU.add)
                        else:
                            ins = dve.tensor_scalar(dst, bank[:, 0:w], scale, None, ALU.mult)
                        ins.then_inc(sem("score_read"), 1)
                        col += w
                    before = n["groups"][-1] if n["groups"] else 0
                    n["groups"].append(before - (-(col // P) // 4))
                    n["exp"] += 1
                    dve.wait_ge(sem("score_read"), n["piece"])
                    dve.tensor_reduce(NMX[:, e:e + 1], S[:, e, 0:col], AX_X, ALU.max, negate=True)\
                        .then_inc(sem("max_ready"), 1)

                def divide(h, t, ranges):
                    k = n["product"]
                    n["product"] += 1
                    e, width = k % 2, sum(k1 - k0 for k0, k1 in ranges)
                    dve.wait_ge(sem("exp_ready"), k + 1)
                    link(dve.reciprocal(RSUM[:, e:e + 1], SUM[:, e:e + 1]))
                    dve.tensor_scalar(S[:, e, 0:width], S[:, e, 0:width], RSUM[:, e:e + 1], None, ALU.mult)\
                        .then_inc(sem("prob_ready"), 1)

                before = None
                for s in steps:
                    if kind == "na" and s[1] == 0:
                        h = s[0]
                        dve.wait_ge(sem(f"na_bias_loaded{h % 2}"), 16 * (h // 2 + 1))
                        table = NB[:, h % 2, :].rearrange("p (x c) -> p x c", c=64)
                        link(dve.tensor_tensor(table, table, CMASK[:].unsqueeze(1).to_broadcast([P, 14, 64]),
                                               ALU.add))
                    scores(*s)
                    if before:
                        divide(*before)
                    before = s
                divide(*before)

            dve.wait_ge(sem("vec_loaded"), 16)
            lb = [VEC[:, VCOL["lb0"]:VCOL["lb0"] + 4], VEC[:, VCOL["lb1"]:VCOL["lb1"] + 4]]
            link(dve.tensor_tensor(LB[:, 0, :], lb[0], lb[1], ALU.max))
            link(dve.tensor_tensor(LB[:, 1, :], lb[0], LB[:, 0, :], ALU.subtract))
            dve.tensor_tensor(LB[:, 2, :], lb[1], LB[:, 0, :], ALU.subtract).then_inc(sem("lb_shifted"), 1)
            dve.wait_ge(sem("lb_exp"), 1)
            link(dve.tensor_tensor(LB[:, 0, :], LB[:, 3, :], LB[:, 4, :], ALU.add))
            link(dve.reciprocal(LB[:, 1, :], LB[:, 0, :]))
            link(dve.tensor_tensor(LB[:, 2, :], LB[:, 3, :], LB[:, 1, :], ALU.mult))
            link(dve.tensor_scalar(LB[:, 5, :], LB[:, 2, :], -1.0, 1.0, ALU.mult, ALU.add))
            dve.wait_ge(sem("cond_ready"), 1)
            link(dve.tensor_copy(CSH[:], CS[:]))
            dve.tensor_tensor(CSL[:], CS[:], CSH[:].bitcast(F32), ALU.subtract).then_inc(sem("operand_ready"), 1)
            rstd(DC, D, TOK)
            normed(XF, HT, XH, XL, TOK, lambda c: vec("ffn1_pre", c))
            for m in range(48):
                bank = done(DC)
                free(dve.tensor_scalar(MOD[:, m, :], bank[:, 0:2], vec("b_ada", m), None, ALU.add))
            evacuated()
            norm = [VEC[:, VCOL[k]:VCOL[k] + 8] for k in ("norm1", "norm1", "norm2")]
            for i, (c0, who) in enumerate(((8, 0), (8, 1), (32, 0))):
                link(dve.scalar_tensor_tensor(COEF[:, i, :], MOD[:, c0:c0 + 8, who], 1.0, norm[i],
                                              ALU.add, ALU.mult))
            ffn(0)
            rstd(DC, D, TOK)
            post(YT, "ffn1_post", 0.5)
            rstd(DC, D, TOK)
            normed(XF, HT, XH, XL, TOK, lambda c: vec("mix_pre", c))

            for z in (ZQ, ZF, ZI, ZOG):
                copy_blocks(z, 4)
            dve.wait_ge(sem("hg_sigmoid"), 1)
            for h in range(HEADS):
                link(dve.tensor_scalar(ZF[:, h, :], ZF[:, h, :], LB[:, 5, h:h + 1], LB[:, 2, h:h + 1],
                                       ALU.mult, ALU.add))
            dve.tensor_scalar(KF[:], ZF[:], -1.0, 1.0, ALU.mult, ALU.add).then_inc(sem("hg_f_ready"), 1)
            dve.wait_ge(sem("hg_log"), 1)
            chunks = [b[:].rearrange("p h (n c) -> p (h n) c", c=CH) for b in (B0, B1)]
            d = 1
            for i in range(6):
                src, dst = chunks[i % 2], chunks[1 - i % 2]
                link(dve.tensor_copy(dst[:, :, 0:d], src[:, :, 0:d]))
                link(dve.tensor_tensor(dst[:, :, d:CH], src[:, :, d:CH], src[:, :, 0:CH - d], ALU.add))
                d *= 2

            def shifted(at, sign):
                edge = chunks[0][:, :, at:at + 1].to_broadcast([P, HEADS * NCH, CH])
                pair = (chunks[0], edge) if sign > 0 else (edge, chunks[0])
                dve.tensor_tensor(chunks[1], *pair, ALU.subtract).then_inc(sem("hg_shift"), 1)

            shifted(CH // 2 - 1, 1)
            dve.wait_ge(sem("hg_exp"), 2)
            shifted(CH - 1, -1)
            dve.wait_ge(sem("hg_q_ready"), 1)
            link(dve.tensor_tensor(Q1[:], Q1[:], ZQ[:], ALU.mult))
            link(dve.tensor_tensor(K1[:], K1[:], KF[:], ALU.mult))
            dve.wait_ge(sem("hg_exp"), 5)
            link(dve.tensor_tensor(Q2[:], Q2[:], ZQ[:], ALU.mult))
            dve.tensor_tensor(K2[:], K2[:], KF[:], ALU.mult).then_inc(sem("hg_factors_ready"), 1)
            dve.wait_ge(sem("turned"), HEADS)
            link(dve.memset(SC[:], 0.0))
            dve.wait_ge(sem("tri_loaded"), 16)
            for i in range(2):
                dve.wait_ge(sem("hg_scores_done"), i + 1)
                for j in range(4):
                    r0 = CH * (j % 2)
                    bank = BANK[5 + i][r0:r0 + CH, 256 * (j // 2):256 * (j // 2) + 256]
                    ins = dve.copy_predicated(SC[r0:r0 + CH, 2 * i + j // 2, :, r0:r0 + CH],
                                              TRI[r0:r0 + CH], bank.rearrange("p (t c) -> p t c", c=CH))
                    if j < 3:
                        link(ins)
                ins.then_inc(sem("hg_scores_read"), 1)
            for c in range(NCH - 1):
                dve.wait_ge(sem("kv_done"), c + 1)
                for h in range(HEADS):
                    kv = BANK[c % 2][:, h * P:(h + 1) * P]
                    if c == 0:
                        ins = dve.tensor_copy(STATE[:, 1, h, :], kv)
                    else:
                        ins = dve.scalar_tensor_tensor(STATE[:, c + 1, h, :], STATE[:, c, h, :],
                                                       DEC[:, h * NCH + c:h * NCH + c + 1], kv,
                                                       ALU.mult, ALU.add)
                    if h < HEADS - 1:
                        link.n += 1
                        ins.then_inc(sem("dve_order"), 1)
                ins.then_inc(sem("state_ready"), 1)
                dve.wait_ge(sem("state_ready"), c + 1)
                dve.wait_ge(sem("dve_order"), link.n)
            for h in range(HEADS):
                dve.wait_ge(sem("hg_out_done"), h + 1)
                dve.tensor_copy(OF[:, h, :], BANK[5 + h % 2][:]).then_inc(sem("hg_out_read"), 1)
            for h in range(HEADS):
                rstd(1, P, TOK)
                link(dve.scalar_tensor_tensor(OF[:, h, :], OF[:, h, :], vec("hgn"), RSTD[:], ALU.mult, ALU.mult))
                dve.wait_ge(sem("hg_og_ready"), 1)
                made(dve.tensor_tensor(OF[:, h, :], OF[:, h, :], ZOG[:, h, :], ALU.mult))
            lows(YL[0], OF, YH[0], 4)

            for h in range(HEADS):
                copy_blocks(DZ, 9)
                dve.wait_ge(sem("bias_loaded"), 16 * (h + 1))
                attend("dil", h, h + 1)
            lows(YL[1], DO, YH[1], 4)

            rstd(DC, D, NMEM)
            normed(MF, MT, MH, ML, NMEM, lambda c: vec("mem_norm", c))
            copy_blocks(MKV, 8, width=NMEM)
            copy_blocks(MQ, 4)
            attend("mem")
            lows(YL[2], MO, YH[2], 4)

            def merge(dst, gates):
                dve.wait_ge(sem("piece_made"), n["made"])
                for i, gate in enumerate(gates):
                    free(dve.tensor_tensor(MP[:, i, :], gate, done(4)[:], ALU.mult))
                evacuated()
                if len(gates) == 3:
                    link(dve.tensor_tensor(MP[:, 0, :], MP[:, 0, :], MP[:, 1, :], ALU.add))
                made(dve.tensor_tensor(dst, MP[:, 0, :], MP[:, len(gates) - 1, :], ALU.add))

            gates_seen = 0
            for m in range(DC // 2):
                st.step += 6 * UNIT
                st.block += 6
                gates_seen += 6
                dve.wait_ge(sem("gate_ready"), gates_seen)
                for i in range(2):
                    merge(MY[:, 2 * m + i, :], [MG[:, 3 * i + br, :] for br in range(3)])
            lows(XL, MY, XH, DC)
            copy_blocks(XF, DC)
            rstd(DC, D, TOK)
            post(XF, "mix_post", 1.0)
            rstd(DC, D, TOK)
            normed(XF, HT, XH, XL, TOK, lambda c: vec("ffn2_pre", c))
            ffn(1)
            rstd(DC, D, TOK)
            post(YT, "ffn2_post", 0.5)

            rstd(DC, D, NMEM)
            normed(CF, CT, CXH, CXL, NMEM, lambda c: COEF[:, 1, c:c + 1], lambda c: MOD[:, c, 1:2])
            copy_blocks(CK, 4, width=NMEM, bias=lambda m: vec("b_in2", 16 + m))
            copy_blocks(CVF, 4, width=NMEM, bias=lambda m: vec("b_in2", 20 + m))
            for c in range(4):
                rstd(1, 64, NMEM)
                link(dve.scalar_tensor_tensor(CK[:, c, :], CK[:, c, :], vec("kg"), RSTD[:, 0:NMEM],
                                              ALU.mult, ALU.mult))

            dve.wait_ge(sem("filter_weights_loaded"), 80)
            round_up = 1.5 * 2.0 ** 23
            two_pi_hi = 6.28125
            two_pi_lo = 2.0 * np.pi - two_pi_hi
            for layer in range(3):
                dve.wait_ge(sem("layer_done"), layer + 1)
                dve.tensor_scalar(FA[:, 0, :], BANK[5][0:64, :], FVEC[:, layer:layer + 1], FVEC[:, 3:4],
                                  ALU.add, ALU.mult).then_inc(sem("layer_read"), 1)
                dve.wait_ge(sem("layer_read"), layer + 1)
                link(dve.tensor_scalar(FA[:, 1, :], FA[:, 0, :], 1.0 / (2.0 * np.pi), round_up, ALU.mult, ALU.add))
                link(dve.tensor_scalar(FA[:, 1, :], FA[:, 1, :], round_up, None, ALU.subtract))
                link(dve.scalar_tensor_tensor(FA[:, 2, :], FA[:, 1, :], -two_pi_hi, FA[:, 0, :], ALU.mult, ALU.add))
                link(dve.scalar_tensor_tensor(FA[:, 0, :], FA[:, 1, :], -two_pi_lo, FA[:, 2, :], ALU.mult, ALU.add))
                dve.tensor_scalar(FA[:, 0, :], FA[:, 0, :], 3.1415925, -3.1415925, ALU.min, ALU.max)\
                    .then_inc(sem("angle_ready"), 1)
            dve.wait_ge(sem("sin_ready"), 3)
            dve.wait_ge(sem("decay_loaded"), 32)
            for o in range(2):
                for i in range(2 * TT):
                    t, d = i // 2, i % 2
                    k = 8 * o + i
                    dve.wait_ge(sem("filter_done"), k + 1)
                    dve.tensor_tensor((FBW if d else FFW)[:, t, :], BANK[5 + k % 2][:], DCY[:, t, :], ALU.mult)\
                        .then_inc(sem("filter_read"), 1)
                dve.wait_ge(sem("abs_used"), 8 * (o + 1))
                dve.reciprocal(RSTD[:], BANK[7][:]).then_inc(sem("norm_read"), 1)
                dve.wait_ge(sem("norm_read"), o + 1)
                link(dve.memset(FBW[0:1, 0, :], 0.0))
                link(dve.tensor_tensor(FE[:], FFW[:], FBW[:], ALU.add))
                link(dve.tensor_tensor(FFW[:], FFW[:], FBW[:], ALU.subtract))
                for t in range(TT):
                    ins = dve.tensor_tensor(FE[:, t, :], FE[:, t, :], RSTD[:], ALU.mult)
                    if t == 0:
                        link(ins)
                        ins = dve.tensor_tensor(FE[0:1, 0, :], FE[0:1, 0, :], SKIP[0:1, o, :], ALU.add)
                    made(ins)
                for t in range(TT):
                    made(dve.tensor_tensor(FFW[:, t, :], FFW[:, t, :], RSTD[:], ALU.mult))
                lows(EOL[:, 0:4, :], FE, EOH[:, 0:4, :], 4)
                lows(EOL[:, 4:8, :], FFW, EOH[:, 4:8, :], 4)
                copy_blocks(KHAT[:, o], KB, TT)

            rstd(DC, D, TOK)
            normed(XF2, HT, XH, XL, TOK, lambda c: COEF[:, 0, c:c + 1], lambda c: MOD[:, c, 0:1])
            turns0 = 4 + 4 + 12 + sum(-(-(sum(k1 - k0 for k0, k1 in r) // P) // 4)
                                      for kind in ("dil", "mem") for _, _, r in attention_steps(kind)) + 4 + 2
            for c in range(12):
                bank = done(DC)
                free(dve.tensor_scalar(HZ[:, c, :], bank[:], vec("b_in2", c), None, ALU.add))
            evacuated()
            for c in range(12):
                if c >= 2:
                    dve.wait_ge(sem("turned"), turns0 + c - 1)
                z, out = HZ[:, c, :], HCV[:, c % 2, :]
                link(dve.tensor_scalar(out, z, vec("cw1", c), vec("cb", c), ALU.mult, ALU.add))
                link(dve.scalar_tensor_tensor(out[:, 1:TOK], z[:, 0:TOK - 1], vec("cw0", c), out[:, 1:TOK],
                                              ALU.mult, ALU.add))
                dve.scalar_tensor_tensor(out[:, 0:TOK - 1], z[:, 1:TOK], vec("cw2", c), out[:, 0:TOK - 1],
                                         ALU.mult, ALU.add).then_inc(sem("conv_ready"), 1)
            dve.wait_ge(sem("turned"), turns0 + 12)
            for o in range(2):
                lows(SL, HTM[:, 0], SH, TT)
                for i in range(4):
                    ar, ai = done(TT), done(TT)
                    kr, ki = KHAT[:, o, i, :], KHAT[:, o, 5 + i, :]
                    kr2 = KHAT[:, o, 4, :] if i == 0 else kr
                    t0, t1 = HCV[:, 0, :], HCV[:, 1, :]
                    dve.wait_ge(sem("piece_made"), n["made"])
                    link(dve.tensor_tensor(t0, ar[:], kr, ALU.mult))
                    link(dve.tensor_tensor(t1, ai[:], ki, ALU.mult))
                    made(dve.tensor_tensor(SQ[:, 0, :], t0, t1, ALU.subtract))
                    dve.wait_ge(sem("piece_made"), n["made"])
                    link(dve.tensor_tensor(t0, ar[:], ki, ALU.mult))
                    free(dve.tensor_tensor(t1, ai[:], kr2, ALU.mult), 2)
                    evacuated()
                    made(dve.tensor_tensor(SQ[:, 1, :], t0, t1, ALU.add))
                    for j in range(2):
                        low(SPL[:, 2 * i + j, :], SQ[:, j, :], SPH[:, 2 * i + j, :])
                for t in range(TT):
                    bank = done(FB)
                    free(dve.tensor_tensor(HTM[:, 0, t, :], bank[:], HTM[:, 1 + o, t, :], ALU.mult))
                evacuated()
            lows(Y2L[0], HY, Y2H[0], 4)
            normed(XF, HT, XH, XL, TOK, lambda c: COEF[:, 0, c:c + 1], lambda c: MOD[:, c, 0:1])

            copy_blocks(NZ, 12, bias=lambda m: vec("b_in2", 12 + m))
            dve.wait_ge(sem("rope_loaded"), 64)
            for c in range(8):
                rstd(1, 64, TOK)
                dve.scalar_tensor_tensor(NZ[:, c, :], NZ[:, c, :], vec("qg" if c < 4 else "kg"), RSTD[:],
                                         ALU.mult, ALU.mult).then_inc(sem("normed_ready"), 1)
                dve.wait_ge(sem("normed_ready"), c + 1)
                dve.wait_ge(sem("swap_done"), c + 1)
                link(dve.tensor_tensor(RP[:, 0, :], NZ[:, c, :], COS[:], ALU.mult))
                dve.tensor_tensor(RP[:, 1, :], BANK[5][:], SIN[:], ALU.mult).then_inc(sem("swap_read"), 1)
                dve.wait_ge(sem("swap_read"), c + 1)
                ins = dve.tensor_tensor(NZ[:, c, :], RP[:, 0, :], RP[:, 1, :], ALU.add)
                if c == 7:
                    ins.then_inc(sem("na_ready"), 1)
                else:
                    link(ins)
            attend("na")
            lows(Y2L[1], NO, Y2H[1], 4)
            for m in range(DC):
                st.step += 2 * UNIT
                st.block += 2
                gates_seen += 2
                dve.wait_ge(sem("gate_ready"), gates_seen)
                merge(MY[:, m, :], [MG[:, 2 * (m % 2) + br, :] for br in range(2)])
            lows(XL, MY, XH, DC)
            for m in range(DC):
                bank = done(DC)
                free(dve.scalar_tensor_tensor(HT[:, m, :], bank[:], MOD[:, 16 + m, 0:1], HT[:, m, :],
                                              ALU.mult, ALU.add))

            rstd(DC, D, TOK)
            normed(XF, HT, XH, XL, TOK, lambda c: COEF[:, 2, c:c + 1], lambda c: MOD[:, 24 + c, 0:1])
            copy_blocks(QT, 16)
            dve.wait_ge(sem("iota_loaded"), 16)
            turns1 = turns0 + 12 + 4 + 4 + 2 * NAH * TT
            def ordered(instructions):
                for ins in instructions:
                    link.n += 1
                    ins.then_inc(sem("dve_order"), 1)
                dve.wait_ge(sem("dve_order"), link.n)

            for t in range(TT):
                for q in range(4):
                    bank = SCB[n["piece"] % 2]
                    n["piece"] += 1
                    dve.wait_ge(sem("score_ready"), n["piece"])
                    dve.tensor_copy(PS[:, 4 * q:4 * q + 4, :].rearrange("p a b -> p (a b)"), bank[:])\
                        .then_inc(sem("score_read"), 1)
                dve.wait_ge(sem("score_read"), n["piece"])
                ordered(dve.max(TOPS[:, j, 0:8], PS[:, j, :]) for j in range(16))
                ordered(dve.max_index(TOPI[:, j, 0:8], TOPS[:, j, 0:8], PS[:, j, :]) for j in range(16))
                ordered(dve.match_replace(PR[:, j, :], TOPS[:, j, 0:8], PS[:, j, :], -BIG) for j in range(16))
                ordered(dve.max(TOPS[:, j, 8:16], PR[:, j, :]) for j in range(16))
                ordered(dve.max_index(TOPI[:, j, 8:16], TOPS[:, j, 8:16], PR[:, j, :]) for j in range(16))
                link(dve.tensor_copy(TOPF[:], TOPI[:]))
                tops = TOPS[:].rearrange("p (h two) k -> p h two k", two=2)
                topf = TOPF[:].rearrange("p (h two) k -> p h two k", two=2)
                square4 = [P, 8, 16, 16]
                link(dve.tensor_tensor(CA[:].rearrange("p h (a b) -> p h a b", a=16),
                                       tops[:, :, 0, :].unsqueeze(3).to_broadcast(square4),
                                       tops[:, :, 1, :].unsqueeze(2).to_broadcast(square4), ALU.add))
                ordered(dve.max(BS[:, h, 0:8], CA[:, h, :]) for h in range(8))
                ordered(dve.max_index(BP[:, h, 0:8], BS[:, h, 0:8], CA[:, h, :]) for h in range(8))
                ordered(dve.match_replace(CR[:, h, :], BS[:, h, 0:8], CA[:, h, :], -BIG) for h in range(8))
                ordered(dve.max(BS[:, h, 8:16], CR[:, h, :]) for h in range(8))
                ordered(dve.max_index(BP[:, h, 8:16], BS[:, h, 8:16], CR[:, h, :]) for h in range(8))
                link(dve.tensor_copy(PRS[:], BS[:, :, 0]))
                dve.tensor_tensor(BS[:], BS[:], PRS[:].unsqueeze(2).to_broadcast([P, 8, 16]), ALU.subtract)\
                    .then_inc(sem("best_shift"), 1)
                link(dve.tensor_scalar(PA[:, 0], BP[:], 4, None, ALU.logical_shift_right))
                link(dve.tensor_scalar(PA[:, 1], BP[:], 15, None, ALU.bitwise_and))
                link(dve.tensor_copy(PAF[:], PA[:]))
                eq = EQ[:].rearrange("p h (k a) -> p h k a", k=16)
                if t:
                    dve.wait_ge(sem("turned"), turns1 + t)
                for i in range(2):
                    link(dve.tensor_tensor(eq, PAF[:, i].unsqueeze(3).to_broadcast(square4),
                                           IOTA[:, 0:16].unsqueeze(1).unsqueeze(1).to_broadcast(square4),
                                           ALU.is_equal))
                    link(dve.tensor_tensor(eq, eq, topf[:, :, i, :].unsqueeze(2).to_broadcast(square4), ALU.mult))
                    link(dve.tensor_reduce(IJG[:, i, :].rearrange("p (h k) -> p h k", h=8), eq, AX_X, ALU.add))
                dve.wait_ge(sem("best_exp"), t + 1)
                link(dve.tensor_reduce(PSUMS[:], BS[:], AX_X, ALU.add))
                link(dve.reciprocal(PRS[:], PSUMS[:]))
                dve.tensor_tensor(IJG[:, 2, :].rearrange("p (h k) -> p h k", h=8), BS[:],
                                  PRS[:].unsqueeze(2).to_broadcast([P, 8, 16]), ALU.mult)\
                    .then_inc(sem("best_ready"), 1)
            dve.wait_ge(sem("turned"), turns1 + TT)

            def hot(token, u):
                dve.tensor_scalar(OI[:, u, :], IOTA[:], IJGT[:, 0, token], None, ALU.is_equal)
                ins = dve.tensor_scalar(OJ[:, u, :], IOTA[:], IJGT[:, 1, token], IJGT[:, 2, token],
                                        ALU.is_equal, ALU.mult)
                if u % 4 == 3:
                    ins.then_inc(sem("hot_ready"), 1)

            for u in range(8):
                hot(slice(u, u + 1), u)
            with dve.Fori(1, TOK // 8) as i:
                for u in range(8):
                    if u % 4 == 0:
                        dve.wait_ge(sem("gates_done"), 2 * i + u // 4 - 1)
                    hot(bass.ds(8 * i + u, 1), u)

            link(dve.memset(ACC[:], 0.0))
            s0, b0, freed0 = st.step, st.block, n["freed"]

            def experts(g):
                dve.wait_ge(sem("gates_loaded"), 16 * g + 16)
                for u in range(8):
                    dve.wait_ge(sem("gelu_ready"), 8 * g + u + 1)
                    k = 8 * g + u + 1
                    dve.tensor_tensor(WF[:, u % 2, :].rearrange("p (b t) -> p b t", t=16),
                                      GE[:, u % 2, :].rearrange("p (b t) -> p b t", t=16),
                                      GG[:, :, u, :], ALU.mult).then_inc(sem("gates_used"), 1)
                    dve.wait_ge(sem("gates_used"), k)
                    dve.tensor_copy(WH[:, u, :], WF[:, u % 2, :]).then_inc(sem("block_free"), 1)
                    dve.wait_ge(sem("block_free"), freed0 + 8 * g + k)
                    dve.tensor_tensor(WL[:, u, :], WF[:, u % 2, :], WH[:, u, :].bitcast(F32), ALU.subtract)\
                        .then_inc(sem("expert_ready"), 1)
                for c in range(8):
                    dve.wait_ge(sem("pe_steps"), s0 + UNIT * 8 + UNIT * (c + 1) + 16 * UNIT * g)
                    dve.tensor_tensor(ACC[:, c, :], ACC[:, c, :], BANK[(b0 + c) % 4][:], ALU.add)\
                        .then_inc(sem("block_free"), 1)

            with dve.Fori(0, EXP_GROUPS) as g:
                experts(g)
            dve.wait_ge(sem("block_free"), freed0 + 16 * EXP_GROUPS)
            for c in range(DC):
                dve.scalar_tensor_tensor(HT[:, c, :], ACC[:, c, :], MOD[:, 40 + c, 0:1], HT[:, c, :],
                                         ALU.mult, ALU.add).then_inc(sem("out_ready"), 1)


def columns(v):
    v = np.asarray(v).reshape(-1)
    return v.reshape(-1, P).T


def feature_major(m):
    t = np.asarray(m).T
    return np.ascontiguousarray(t.reshape(-1, P, t.shape[1]).transpose(1, 0, 2))


def weight_blocks(w, column0=0, count=None):
    w = np.asarray(w)
    k = w.shape[0] // P
    w = w.reshape(k, P, -1, P).transpose(2, 0, 1, 3)
    first = column0 // P
    return w[first:] if count is None else w[first:first + count]


def as_units(blocks):
    b = np.concatenate([np.asarray(x).reshape(-1, P, P) for x in blocks])
    return np.ascontiguousarray(b.reshape(-1, UNIT, P, P).transpose(0, 2, 1, 3)).reshape(-1, P, UNIT * P)


def shape_constants():
    f = np.float32
    c = {"ones": np.ones((P, P), f), "ident": np.eye(P, dtype=f)}
    c["pair"] = np.kron(np.eye(2), np.ones((64, 64))).astype(f)
    s, col = np.arange(P)[:, None] % CH, np.arange(CH)[None, :]
    c["tri"] = np.repeat((s <= col).astype(np.uint32)[:, None, :], 4, axis=1)
    d = np.arange(P)[:, None] - np.arange(TOK)[None, :] + (TOK - P)
    bias = np.zeros((HEADS, P, 3, TOK), f)
    for g, (window, dil) in enumerate(((128, 1), (512, 4), (2048, 16))):
        valid = (d >= 0) & (d % dil == 0) & (d <= window)
        for h in range(HEADS):
            slope = f(2.0 ** (-8.0 * (g * HEADS + h + 1) / 12.0))
            bias[h, :, g] = np.where(valid, -slope * d.astype(f), f(MASKED))
    c["dil_bias"] = bias
    pos = np.arange(TOK)
    e = np.arange(P) % 64
    inv = (10000.0 ** (-np.arange(16, dtype=f) / f(16))).astype(f)
    where = np.where(e[:, None] < 32, (pos // 64)[None, :], (pos % 64)[None, :]).astype(f)
    angle = (where * inv[e % 16][:, None]).astype(f).astype(np.float64)
    c["cos"] = np.cos(angle).astype(f)
    c["sin"] = (np.sin(angle) * np.where(e % 32 < 16, -1.0, 1.0)[:, None]).astype(f)
    swap = np.zeros((P, P), f)
    swap[np.arange(P) ^ 16, np.arange(P)] = 1.0
    c["swap"] = swap
    q, k = np.arange(P)[:, None] % 64, np.arange(64)[None, :]
    start = np.clip(q - 8, 0, 48)
    c["cmask"] = np.where((k >= start) & (k < start + 16), 0.0, MASKED).astype(f)
    c["iota"] = np.repeat(np.arange(P, dtype=f)[None, :], P, axis=0)
    t = np.linspace(0.0, 1.0, TOK, dtype=f)
    w = (f(2.0 * np.pi / TOK) * np.arange(TOK, dtype=f)).astype(f)
    bands = np.linspace(1e-4, 15.0, 16, dtype=f)
    arg = (bands[:, None] * w[None, :]).astype(f).astype(np.float64)
    c["feats"] = np.concatenate([t[None, :], np.cos(arg), -np.sin(arg)]).astype(f)
    deltas = np.abs(np.linspace(np.log(1e-2) / 1.5, np.log(1e-2) / 0.3, 512, dtype=f))
    decay = np.exp(-(t[:, None] * deltas[None, :]).astype(np.float64)).astype(f)
    c["decay"] = np.ascontiguousarray(decay.reshape(TT, P, TOK).transpose(1, 0, 2))
    i = np.arange(TOK)
    theta = 2.0 * np.pi * ((i[:, None] * i[None, :]) % 1024) / 1024.0
    cos, sin = np.cos(theta), -np.sin(theta)
    flips = np.where(i % 2, -1.0, 1.0)
    cos_n, sin_n = cos.copy(), sin.copy()
    cos_n[:, 0], sin_n[:, 0] = flips, flips
    weight = np.where(i == 0, 1.0, 2.0)[:, None] / 1024.0
    inv_cos, inv_sin = cos * weight, sin * weight
    inv_sin[0] = flips / 1024.0
    blk = lambda m: weight_blocks(m.astype(f))
    bc, bcn, bs, bsn = blk(cos), blk(cos_n), blk(sin), blk(sin_n)
    one = [bc, bcn[0:1], bs]
    c["w_hyk"] = as_units(one + one)
    forward = [x[m] for m in range(4) for x in (bc, bsn)]
    ic, is_ = blk(inv_cos), blk(inv_sin)
    inverse = [x[m, k] for m in range(4) for k in range(4) for x in (ic, is_)]
    c["w_hyc"] = as_units((forward + inverse) * 2)
    return c


def lay_out(v):
    a = shape_constants()
    one = lambda name: v[name][0]
    a["x"] = feature_major(v["x"][0])
    a["mem"] = feature_major(v["mem"][0])
    a["ctx"] = feature_major(v["ctx_2"][0])
    parts = {
        "ffn1_pre": v["ffn1_pre_w"], "ffn1_post": v["ffn1_post_w"], "mix_pre": v["mix_pre_w"],
        "mem_norm": v["mem_norm_w"], "mix_post": v["mix_post_w"], "ffn2_pre": v["ffn2_pre_w"],
        "ffn2_post": v["ffn2_post_w"], "norm1": v["norm1_g_2"], "norm2": v["norm2_g_2"],
        "b_gate": v["b_gate"], "lb0": v["hg_lb_logits"][0], "lb1": v["hg_lb_logits"][1],
        "hgn": v["hg_norm_w"], "b_in2": v["b_in_2"], "cw0": v["hy_conv_w_2"][0, 0],
        "cw1": v["hy_conv_w_2"][0, 1], "cw2": v["hy_conv_w_2"][0, 2], "cb": v["hy_conv_b_2"],
        "qg": np.tile(v["q_norm_g_2"][0], 2), "kg": np.tile(v["k_norm_g_2"][0], 2),
        "b_ada": v["b_ada_2"],
    }
    cond = np.stack([columns(v["c_2"][0]), columns(v["c_ctx_2"])], axis=2).reshape(P, 16)
    a["vecs"] = np.ascontiguousarray(np.concatenate(
        [cond if name == "cond" else columns(parts[name]) for name, _ in VECS], axis=1))

    def ffn(k):
        gu = weight_blocks(one(f"ffn{k}_w_gu"))
        a[f"w_ffn{k}_gu"] = as_units([gu[m + half] for m in range(FC) for half in (0, FC)])
        a[f"w_ffn{k}_down"] = as_units([weight_blocks(one(f"ffn{k}_w_down"))])

    ffn(1)
    ffn(2)
    w_in = weight_blocks(one("w_in"))
    a["w_ada"] = as_units([weight_blocks(one("w_ada_2"))])
    a["w_memkv"] = as_units([weight_blocks(one("w_mem_kv"))])
    a["w_hg"] = as_units([w_in[0:16]])
    a["w_dil"] = as_units([w_in[16 + 12 * g + 4 * part + h] for h in range(HEADS) for part in range(3)
                           for g in range(3)])
    a["w_mq"] = as_units([w_in[52:56]])
    br = [weight_blocks(one(k)) for k in ("w_br_hg", "w_br_dil", "w_br_mem")]
    merge = []
    for m in range(0, DC, 2):
        merge += [w_in[56 + 8 * b + m + i] for i in range(2) for b in range(3)]
        merge += [br[b][m + i] for i in range(2) for b in range(3)]
    a["w_merge1"] = as_units(merge)
    a["w_wout1"] = as_units([weight_blocks(one("w_out"))])
    w2 = weight_blocks(one("w_in_2"))
    a["w_ctxkv"] = as_units([w2[16:24]])
    a["w_hyz"] = as_units([w2[0:12]])
    a["w_naqkv"] = as_units([w2[12:24]])
    hy, na = weight_blocks(one("w_hy_out_2")), weight_blocks(one("w_na_out_2"))
    a["w_merge2"] = as_units([x for m in range(DC) for x in (w2[24 + m], w2[32 + m], hy[m], na[m])])
    a["w_wout2"] = as_units([weight_blocks(one("w_out_2"))])
    a["w_wq"] = as_units([weight_blocks(one("peer_w_q_2"))])
    u = one("peer_u_2").reshape(P, EXP_GROUPS, 8, DC, P).transpose(1, 2, 4, 3, 0)
    w = one("peer_v_2").reshape(P, EXP_GROUPS, 8, DC, P).transpose(1, 3, 0, 2, 4)
    a["w_peer"] = np.concatenate([u, w], axis=1).reshape(16 * EXP_GROUPS, P, UNIT * P)
    a["keys"] = np.ascontiguousarray(one("peer_keys_2").reshape(16, P, P).transpose(2, 0, 1))
    a["f1"] = one("hy_f1_w_2")
    a["f23"] = np.ascontiguousarray(np.stack([one("hy_f2_w_2"), one("hy_f3_w_2")], axis=1))
    a["f4"] = one("hy_f4_w_2")
    fv = [one(k) for k in ("hy_f1_b_2", "hy_f2_b_2", "hy_f3_b_2", "hy_sin_freq_2")]
    a["fvec"] = np.ascontiguousarray(np.stack(fv + fv, axis=1))
    a["skip"] = v["hy_skip_2"].reshape(1, 2, TOK)
    dc = np.clip(np.arange(64)[None, :] - np.arange(64)[:, None], -15, 15) + 15
    rpb = one("na_rpb_2")
    table = np.stack([rpb[:, 1 - e:15 - e][:, :, dc] for e in range(2)], axis=1)
    a["na_bias"] = np.ascontiguousarray(table.transpose(0, 1, 3, 2, 4)).reshape(NAH, P, 14 * 64)
    return a


def kernel(**inputs):
    import concourse.bacc as bacc
    from concourse.bass_utils import run_bass_kernel_spmd

    a = lay_out({k: np.asarray(v) for k, v in inputs.items()})
    nc = bacc.Bacc("TRN2", target_bir_lowering=False, num_devices=1)
    aps = {k: nc.dram_tensor(f"in_{k}", x.shape, mybir.dt.from_np(x.dtype), kind="ExternalInput").ap()
           for k, x in a.items()}
    aps["out"] = nc.dram_tensor("out_x", (P, DC, TOK), F32, kind="ExternalOutput").ap()
    program(nc, aps)
    r = run_bass_kernel_spmd(nc, [{f"in_{k}": np.ascontiguousarray(x) for k, x in a.items()}], core_ids=[0])
    out = r.results[0]["out_x"]
    return np.ascontiguousarray(out.transpose(2, 1, 0)).reshape(1, TOK, D)
```

```python
from contextlib import ExitStack

import numpy as np

import concourse.bass as bass
from concourse import mybir

F32 = mybir.dt.float32
F32R = mybir.dt.float32r
U32 = mybir.dt.uint32
ALU = mybir.AluOpType
ACT = mybir.ActivationFunctionType
AX_X = mybir.AxisListType.X

P = 128
TOK = 512
TT = TOK // P
D = 1024
DC = D // P
EPS = 1e-6
FF = 2816
FC = FF // P
NMEM = 256
HEADS = 4
CH = 64
NCH = TOK // CH
HYC = 4
FB = 8
KB = 9
NAH = 8
TOPK = 16
EXP_GROUPS = 16
AHEAD = 9
BY_TILE = 10
BY_TURN = 4
SHARED = EXP_GROUPS - AHEAD
GATE_TURNS = 8
assert 8 * AHEAD == BY_TILE * TT + BY_TURN * GATE_TURNS
UNIT = 8
RING = 4
BIG = 3.0e38
MASKED = -1.0e30

PARTS = [
    ("ada0", 4), ("ffn1_gu", 4 * FC), ("ffn1_down", DC * FC // UNIT),
    ("hg", 16), ("dil", 36), ("memkv", 8), ("mq", 4), ("merge1", 36), ("wout1", 8),
    ("ffn2_gu", 2 * FC), ("ffn2_down", DC * FC // UNIT),
    ("ctxkv", 8), ("hyk", KB), ("hyz", 12), ("hyc", 16), ("naqkv", 12), ("merge2", 24),
    ("wout2", 8), ("wq", 16),
    ("peer_ahead", 8 * AHEAD), ("peer", 16 * (EXP_GROUPS - AHEAD)), ("peer_out", 8 * AHEAD),
]
START = {}
_n = 0
for _name, _count in PARTS:
    START[_name] = _n
    _n += _count
TOTAL = _n

VECS = [
    ("ffn1_pre", 8), ("ffn1_post", 8), ("mix_pre", 8), ("mem_norm", 8), ("mix_post", 8),
    ("ffn2_pre", 8), ("ffn2_post", 8), ("norm1", 8), ("norm2", 8), ("b_gate", 24),
    ("lb0", 4), ("lb1", 4), ("hgn", 1), ("b_in2", 40), ("cw0", 12), ("cw1", 12), ("cw2", 12),
    ("cb", 12), ("qg", 1), ("kg", 1), ("b_ada", 48), ("cond", 16), ("fold", 2),
]
VCOL = {}
_n = 0
for _name, _count in VECS:
    VCOL[_name] = _n
    _n += _count
NVEC = _n


def attention_steps(kind):
    steps = []
    for h in range(NAH if kind == "na" else HEADS):
        for t in range(TT):
            if kind == "dil":
                ranges = [(max(0, P * (t - 1)), P * (t + 1)), (0, P * (t + 1)), (0, P * (t + 1))]
            elif kind == "mem":
                ranges = [(0, NMEM)]
            else:
                ranges = [(0, TOK), (0, NMEM)]
            steps.append((h, t, ranges))
    return steps


class Stepper:

    def __init__(self):
        self.step = 0
        self.told = 0
        self.block = 0
        self.units = 0

    def steps_(self, v):
        return v + UNIT * self.units if not isinstance(self.units, int) else v

    def units_(self, v):
        return v + self.units if not isinstance(self.units, int) else v

    def skip(self, units, blocks):
        self.step += UNIT * units
        self.told = self.step
        self.block += blocks
        self.units = 0


def wait(engine, sem, value):
    if not isinstance(value, int) or value > 0:
        engine.wait_ge(sem, value)


class Link:

    def __init__(self, engine, sem):
        self.engine, self.sem, self.n, self.turn = engine, sem, 0, 0

    def __call__(self, ins):
        self.n += 1
        ins.then_inc(self.sem, 1)
        self.engine.wait_ge(self.sem, self.n + self.turn if not isinstance(self.turn, int) else self.n)


def program(nc, a):
    with ExitStack() as ctx:
        cache = {}

        def sem(name):
            if name not in cache:
                cache[name] = ctx.enter_context(nc.semaphore(name))
            return cache[name]

        base = -(-nc.sbuf_base // 64) * 64
        fixed = [base]

        def place(name, shape, dt=F32, at=None):
            size = 4 * int(np.prod(shape[1:]))
            if at is None:
                at = fixed[0]
                fixed[0] += -(-size // 32) * 32
            return nc.alloc_sbuf_tensor_at(name, shape, dt, offset=at)

        HT = place("residual", [P, DC, TOK])
        RAW = place("weights_raw", [P, RING, UNIT * P])
        HI = place("weights_hi", [P, RING, UNIT * P], F32R)
        LO = place("weights_lo", [P, RING, UNIT * P], F32R)
        x_at = fixed[0]
        XH = place("operand_hi", [P, DC, TOK], F32R)
        XL = place("operand_lo", [P, DC, TOK], F32R)
        ONES = place("ones", [P, P])
        PAIR = place("pair_ones", [P, P])
        IDENT = place("identity", [P, P])
        VEC = place("vectors", [P, NVEC])
        SQ = place("squares", [P, 2, TOK])
        MS = place("mean_square", [P, TOK])
        AR = place("ada_rows", [4, TOK], F32, fixed[0])
        RT = place("root", [P, TOK])
        RSTD = place("reciprocal_root", [P, TOK])
        LB = place("lower_bound", [P, 6, 4])
        MOD = place("modulation", [P, 48, 2])
        COEF = place("modulation_gain", [P, 3, DC])
        CS = place("cond_silu", [P, DC, 2])
        CP = place("cond_parts", [P, DC, 4], F32R)
        NMX = place("negated_max", [P, 2])
        SUM = place("exp_sum", [P, 2])
        RSUM = place("exp_sum_reciprocal", [P, 2])
        A0 = fixed[0]
        END = 229344
        Y2 = END - 32768
        Y3 = END - 49152
        assert END - A0 >= 98304, END - A0

        KBYTE = 1024
        FH = place("hidden_hi", [P, FC, TOK], F32R, A0)
        FL = place("hidden_lo", [P, FC, TOK], F32R, A0 + FC * 2048)
        SG = place("gate_silu", [P, 2, TOK], F32, A0 + FC * 4096)
        HF = place("hidden", [P, 2, TOK], F32, A0 + FC * 4096 + 4096)
        YT = place("branch_out", [P, DC, TOK], F32, x_at)
        XF = place("operand", [P, DC, TOK], F32, A0)

        ZQ, ZF, ZI, ZOG, KF, K2, B0, B1, Q1, K1, Q2, VT = [
            place(n, [P, HEADS, TOK], F32, A0 + i * 8192)
            for i, n in enumerate(["hg_q", "hg_f", "hg_i", "hg_og", "hg_k", "hg_k2", "hg_b0", "hg_b1",
                                   "hg_q1", "hg_k1", "hg_q2", "hg_v"])]
        K2T = place("hg_k2t", [P, HEADS, TOK], F32, A0 + 8192)
        SC = place("hg_scores", [P, HEADS, TT, P], F32, A0 + 2 * 8192)
        TRI = place("hg_causal", [P, 4, CH], U32, A0 + 12 * 8192 + 128)
        assert A0 + 12 * 8192 + 1152 <= END
        STATE = place("hg_state", [P, NCH, HEADS, P], F32, A0 + 6 * 8192)
        DEC = place("hg_decay", [P, HEADS * NCH], F32, A0 + 12 * 8192)
        OF = place("hg_out", [P, HEADS, TOK], F32, A0)
        YH = [place(f"branch{i}_hi", [P, 4, TOK], F32R, Y3 + i * 16384) for i in range(3)]
        YL = [place(f"branch{i}_lo", [P, 4, TOK], F32R, Y3 + i * 16384 + 8192) for i in range(3)]
        DZ = place("dil_qkv", [P, 9, TOK], F32, A0)
        DV = place("dil_v", [P, 3, TT, P], F32, A0 + 18432)
        DB = place("dil_bias", [P, 3, TOK], F32, A0 + 24576)
        DS = place("att_scores", [P, 2, 3 * TOK], F32, A0 + 30720)
        DP = place("att_probs_t", [P, 2, 4 * P], F32, A0 + 43008)
        DO = place("att_out", [P, HEADS, TOK], F32, Y3 + 2 * 16384)
        MT = place("memory", [P, DC, NMEM], F32, A0)
        MF = place("memory_operand", [P, DC, NMEM], F32, A0 + 8192)
        MH = place("memory_hi", [P, DC, NMEM], F32R, A0 + 16384)
        ML = place("memory_lo", [P, DC, NMEM], F32R, A0 + 24576)
        MKV = place("memory_kv", [P, 8, NMEM], F32, A0)
        MQ = place("memory_q", [P, 4, TOK], F32, A0 + 8192)
        MV = place("memory_v", [P, HEADS, 2, P], F32, A0 + 16384)
        MO = place("memory_out", [P, HEADS, TOK], F32, A0 + 20480)
        MG = place("merge_gates", [P, 6, TOK], F32, A0)
        MP = place("merge_products", [P, 3, TOK], F32, A0 + 12288)
        MY = place("merged", [P, DC, TOK], F32, A0 + 18432)
        CT = place("context", [P, DC, NMEM], F32, A0)
        CF = place("context_operand", [P, DC, NMEM], F32, A0 + 8192)
        CXH = place("context_hi", [P, DC, NMEM], F32R, A0 + 16384)
        CXL = place("context_lo", [P, DC, NMEM], F32R, A0 + 24576)
        CVF = place("context_vt", [P, 4, NMEM], F32, A0 + 32768)
        CK = place("context_k", [P, 4, NMEM], F32, END - 8192)
        CV = place("context_v", [P, 2, TOK], F32, END - 4096)
        KHAT = place("filter_dft", [P, 2, KB, TOK], F32, A0)
        W1 = A0 + 2 * KB * 2048
        FX = place("f_hidden", [64, TOK], F32, W1)
        FW4 = place("f4", [64, 2048], F32, W1 + 2048)
        FVEC = place("f_vectors", [64, 8], F32, W1 + 10240)
        FFW = place("filter_forward", [P, TT, TOK], F32, W1 + 10304)
        FBW = place("filter_backward", [P, TT, TOK], F32, W1 + 18496)
        FE = place("filter_even", [P, TT, TOK], F32, W1 + 26688)
        FAB = place("filter_abs", [P, 2, TOK], F32, W1 + 34880)
        DCY = place("filter_decay", [P, TT, TOK], F32, W1 + 38976)
        SKIP = place("hy_skip", [1, 2, TOK], F32, W1 + 47168)
        FTS = place("positions", [33, TOK], F32, W1 + 26688)
        FW1 = place("f1", [33, 64], F32, W1 + 28736)
        FW = place("f23", [64, 2, 64], F32, W1 + 28992)
        FA = place("f_argument", [64, 3, TOK], F32, W1 + 10304)
        assert W1 + 47168 + 4096 <= END - 8192
        EOH = place("filter_hi", [P, 8, TOK], F32R, x_at)
        EOL = place("filter_lo", [P, 8, TOK], F32R, x_at + 16384)
        HZ = place("hy_z", [P, 12, TOK], F32, W1)
        HCV = place("hy_conv", [P, 2, TOK], F32, W1 + 24576)
        HTM = place("hy_token_major", [P, 3, TT, TOK], F32, W1 + 28672)
        XF2 = place("operand_2", [P, DC, TOK], F32, W1)
        SH = place("signal_hi", [P, TT, TOK], F32R, W1)
        SL = place("signal_lo", [P, TT, TOK], F32R, W1 + 8192)
        HY = place("hy_out", [P, HYC, TOK], F32, W1 + 16384)
        SPH = place("spectrum_hi", [P, FB, TOK], F32R, x_at)
        SPL = place("spectrum_lo", [P, FB, TOK], F32R, x_at + 16384)
        Y2H = [place(f"second{i}_hi", [P, 4, TOK], F32R, Y2 + i * 16384) for i in range(2)]
        Y2L = [place(f"second{i}_lo", [P, 4, TOK], F32R, Y2 + i * 16384 + 8192) for i in range(2)]
        assert W1 + 53248 <= END - 8192
        NZ = place("na_qkv", [P, 12, TOK], F32, A0)
        NV = place("na_v", [P, TT, TOK], F32, A0 + 24576)
        COS = place("rope_cos", [P, TOK], F32, A0 + 32768)
        SIN = place("rope_sin", [P, TOK], F32, A0 + 34816)
        SWAP = place("rope_swap", [P, P], F32, A0 + 36864)
        CMASK = place("column_mask", [P, 64], F32, A0 + 37376)
        NB = place("na_bias", [P, 2, 14 * 64], F32, A0 + 37632)
        NS = place("na_scores", [P, 2, TOK + NMEM], F32, A0 + 44800)
        NP = place("na_probs_t", [P, 2, 4 * P], F32, A0 + 50944)
        NO = place("na_out", [P, HYC, TOK], F32, A0 + 55040)
        RP = place("rope_products", [P, 2, TOK], F32, A0 + 55040)
        assert A0 + 63232 <= Y2
        QT = place("peer_q", [P, 16, TOK], F32, A0)
        KEYS = place("peer_keys", [P, 16, P], F32, A0 + 32768)
        PS = place("peer_scores", [P, 16, P], F32, A0 + 40960)
        PR = place("peer_scores_rest", [P, 16, P], F32, A0 + 49152)
        CA = place("candidates", [P, 8, 256], F32, A0 + 57344)
        CR = place("candidates_rest", [P, 8, 256], F32, A0 + 65536)
        EQ = place("matches", [P, 8, 256], F32, A0 + 73728)
        s0 = A0 + 81920
        TOPS = place("top_scores", [P, 16, 16], F32, s0)
        TOPI = place("top_index", [P, 16, 16], U32, s0 + 1024)
        TOPF = place("top_index_f", [P, 16, 16], F32, s0 + 2048)
        BS = place("best_scores", [P, 8, 16], F32, s0 + 3072)
        BP = place("best_position", [P, 8, 16], U32, s0 + 3584)
        PA = place("position_parts", [P, 2, 8, 16], U32, s0 + 4096)
        PAF = place("position_parts_f", [P, 2, 8, 16], F32, s0 + 5120)
        IJG = place("expert_ijg", [P, 3, P], F32, s0 + 6144)
        IJGT = place("expert_ijg_t", [P, 3, TOK], F32, s0 + 7680)
        IOTA = place("iota", [P, P], F32, s0 + 13824)
        PSUMS = place("peer_sums", [P, 8], F32, s0 + 14336)
        PRS = place("peer_sums_reciprocal", [P, 8], F32, s0 + 14400)
        assert s0 + 14464 <= END
        OI = place("one_hot_i", [P, 8, P], F32, A0)
        OJ = place("one_hot_j", [P, 8, P], F32, A0 + 4096)
        STG = place("gate_stage", [P, 2, P, 16], F32, A0 + 8192)
        WH = place("expert_hi", [P, 8, TOK], F32R, A0)
        WL = place("expert_lo", [P, 8, TOK], F32R, A0 + 16384)
        ACC = place("peer_sum", [P, DC, TOK], F32, A0 + 32768)
        GG = place("expert_gates", [P, 32, 8, 16], F32, A0 + 49152)
        GE = place("expert_gelu", [P, 2, TOK], F32, A0 + 65536)
        WF = place("expert_act", [P, 2, TOK], F32, A0 + 69632)
        GU = place("expert_gelu_ahead", [P, 8, TOK], F32, A0 + 73728)
        WH2 = place("expert_hi_2", [P, 8, TOK], F32R, x_at)
        WL2 = place("expert_lo_2", [P, 8, TOK], F32R, x_at + 16384)
        assert 73728 + 16384 <= END - A0

        GD = nc.dram_tensor("peer_gates", [32, P, P, 16], F32, kind="Internal").ap()
        UD = nc.dram_tensor("peer_gelu_ahead", [8 * AHEAD, P, TOK], F32, kind="Internal").ap()

        BANK = [ctx.enter_context(nc.psum_tensor(f"bank{i}", [P, TOK], F32)) for i in range(8)]
        SCB = [BANK[5], BANK[6]]
        TRB = [BANK[4], BANK[7]]
        OB = [BANK[2], BANK[3]]
        STB = BANK[4]

        def vec(name, c=0):
            return VEC[:, VCOL[name] + c:VCOL[name] + c + 1]

        block = ctx.enter_context(nc.Block())

        @block.sync
        def _(sp):
            sp.dma_start(VEC[:], a["vecs"]).then_inc(sem("vec_loaded"), 16)
            for n, (dst, src) in enumerate([(ONES, "ones"), (PAIR, "pair"), (IDENT, "ident")]):
                sp.dma_start(dst[:], a[src]).then_inc(sem("const_loaded"), 16)
            sp.dma_start(HT[:], a["x"]).then_inc(sem("x_loaded"), 16)

            def unit(src, n, slot):
                wait(sp, sem("lo_ready"), n - RING + 1)
                sp.dma_start(RAW[:, slot, :], src).then_inc(sem(f"raw_loaded{slot}"), 16)

            def part(name, first=0, count=None):
                n0, src = START[name] + first, a["w_" + name]
                count = (dict(PARTS)[name] if count is None else count)
                done = 0
                while count - done >= 8 and n0 + done < RING:
                    unit(src[first + done], n0 + done, (n0 + done) % RING)
                    done += 1
                turns = (count - done) // RING
                if turns > 1:
                    with sp.Fori(0, turns) as i:
                        for u in range(RING):
                            n = n0 + done + u
                            unit(src[first + done + u + RING * i], n + RING * i, n % RING)
                    done += turns * RING
                while done < count:
                    unit(src[first + done], n0 + done, (n0 + done) % RING)
                    done += 1

            for name, _ in PARTS[:-3]:
                part(name)
            ahead, n0 = a["w_peer_ahead"], START["peer_ahead"]
            part("peer_ahead", 0, BY_TILE * TT + RING)

            def ahead_unit(j, shift=0):
                k = BY_TILE * TT + RING + j
                unit(a["w_peer"][k - 8 * AHEAD] if isinstance(shift, int) and k + shift >= 8 * AHEAD
                     else ahead[k + shift], n0 + k + shift, (n0 + k) % RING)

            def store_stage(i, r):
                s = r % 2
                sp.wait_ge(sem("stage_ready"), 16 * i + 4 * (r + 1))
                sp.dma_start(GD[4 * i + r].rearrange("i j t -> i (j t)"),
                             STG[:, s].rearrange("p j t -> p (j t)")).then_inc(sem(f"stage_stored{s}"), 16)

            with sp.Fori(0, GATE_TURNS - 1) as i:
                for r in range(4):
                    store_stage(i, r)
                    ahead_unit(r, BY_TURN * i)
            for r in range(4):
                store_stage(GATE_TURNS - 1, r)
                ahead_unit(r + BY_TURN * (GATE_TURNS - 1))
            for s in range(2):
                sp.wait_ge(sem(f"stage_stored{s}"), 256)
            gates = GD.rearrange("b i j t -> i b j t")
            sp.dma_start(GG[:], gates[:, :, 0:8, :]).then_inc(sem("gates_loaded"), 16)
            n0, src = START["peer"], a["w_peer"]
            part("peer", RING, 8)
            sp.wait_ge(sem("gates_used"), 8)
            sp.dma_start(GG[:], gates[:, :, 8:16, :]).then_inc(sem("gates_loaded"), 16)
            with sp.Fori(0, SHARED - 1) as g:
                for u in range(16):
                    n = n0 + 12 + u
                    unit(src[12 + u + 16 * g], n + 16 * g, n % RING)
                sp.wait_ge(sem("gates_used"), 8 * g + 16)
                sp.dma_start(GG[:], gates[:, :, bass.ds(8 * g + 16, 8), :]).then_inc(sem("gates_loaded"), 16)
            for s in range(2):
                sp.wait_ge(sem(f"ahead_stored{s}"), 16 * 4 * AHEAD)
            by_group = UD.rearrange("(g u) p t -> g p u t", u=8)
            sp.dma_start(GU[:], by_group[0]).then_inc(sem("ahead_loaded"), 16)
            part("peer", 12 + 16 * (SHARED - 1), 4)
            n0, src = START["peer_out"], a["w_peer_out"]
            with sp.Fori(0, AHEAD - 1) as g:
                for u in range(8):
                    if u == 2:
                        sp.wait_ge(sem("gates_used"), 8 * (SHARED + 1) + 8 * g)
                        sp.dma_start(GG[:], gates[:, :, bass.ds(8 * g + 8 * (SHARED + 1), 8), :])\
                            .then_inc(sem("gates_loaded"), 16)
                        sp.dma_start(GU[:], by_group[g + 1]).then_inc(sem("ahead_loaded"), 16)
                    unit(src[u + 8 * g], n0 + u + 8 * g, (n0 + u) % RING)
            part("peer_out", 8 * (AHEAD - 1), 8)
            sp.wait_ge(sem("out_ready"), DC)
            sp.dma_start(a["out"], HT[:]).then_inc(sem("out_stored"), 16)
            sp.wait_ge(sem("out_stored"), 16)

        @block.gpsimd
        def _(pool):
            def low(n, slot):
                wait(pool, sem("hi_ready"), n + 1)
                wait(pool, sem("pe_steps"), UNIT * (n - RING + 1))
                pool.tensor_tensor(LO[:, slot, :], RAW[:, slot, :], HI[:, slot, :].bitcast(F32),
                                   ALU.subtract).then_inc(sem("lo_ready"), 1)

            for n in range(RING):
                low(n, n)
            with pool.Fori(1, TOTAL // RING) as i:
                for u in range(RING):
                    low(RING * i + u, u)
            for n in range(TOTAL // RING * RING, TOTAL):
                low(n, n % RING)

        @block.tensor
        def _(pe):
            st = Stepper()
            owner = {}
            n = {"square": 0, "sum": 0, "turn": 0, "piece": 0, "prob": 0, "ov": 0, "gate": 0,
                 "freed": 0, "ag": 0, "small": 0}

            def claim(b):
                if b in owner:
                    wait(pe, sem(owner[b][0]), owner[b][1])

            def block_(kc, hi, lo, width=TOK, gate=False, in_loop=False, piece=None, ready=None):
                b = st.block % 4
                for k in range(kc) if piece is None else piece:
                    if ready:
                        ready(k)
                    if st.step % UNIT == 0:
                        pe.wait_ge(sem("lo_ready"), st.units_(st.step // UNIT + 1))
                    if k == 0 and not in_loop:
                        claim(b)
                    slot, col = (st.step // UNIT) % RING, st.step % UNIT
                    wh = HI[:, slot, col * P:(col + 1) * P]
                    wl = LO[:, slot, col * P:(col + 1) * P]
                    out = BANK[b][:, 0:width]
                    pe.matmul(out, wh, hi(k), start=(k == 0), stop=False)
                    pe.matmul(out, wh, lo(k), start=False, stop=False)
                    ins = pe.matmul(out, wl, hi(k), start=False, stop=(k == kc - 1))
                    st.step += 1
                    if st.step % UNIT == 0 or k == kc - 1:
                        ins.then_inc(sem("pe_steps"), st.step - st.told)
                        st.told = st.step
                if piece is not None and piece[-1] < kc - 1:
                    return
                st.block += 1
                if gate:
                    n["gate"] += 1
                    owner[b] = ("gate_ready", n["gate"])
                elif not in_loop:
                    n["freed"] += 1
                    owner[b] = ("block_free", n["freed"])

            def x_ops():
                return (lambda k: XH[:, k, :]), (lambda k: XL[:, k, :])

            def operand(total):
                n["operand"] = n.get("operand", 0) + total
                pe.wait_ge(sem("operand_ready"), n["operand"])

            def sums(pieces, matrix, width, first_wait=None):
                claim(4)
                for c in range(pieces):
                    pe.wait_ge(sem("square_ready"), n["square"] + 1)
                    pe.matmul(STB[:, 0:width], matrix[:], SQ[:, n["square"] % 2, 0:width],
                              start=(c == 0), stop=(c == pieces - 1)).then_inc(sem("square_used"), 1)
                    n["square"] += 1
                n["sum"] += 1
                owner[4] = ("sum_read", n["sum"])

            def turn(sources):
                b = 4 if n["turn"] % 2 == 0 else 7
                claim(b)
                for i, src in enumerate(sources):
                    rows = src.shape[0]
                    ins = pe.transpose(BANK[b][0:src.shape[-1], i * P:i * P + rows], src, IDENT[0:rows, 0:rows])
                ins.then_inc(sem("turn_done"), 1)
                n["turn"] += 1
                owner[b] = ("turned", n["turn"])

            def ffn(name):
                operand(DC)
                hi, lo = x_ops()
                for b in range(4):
                    claim(b)
                freed = n["freed"]
                ada = name == "ffn1"
                per = 8 if ada else 4

                def two_pairs(i):
                    for u in range(4):
                        if u % 2 == 0:
                            wait(pe, sem("block_free"), freed + 4 * i + u - 2)
                        block_(DC, hi, lo, in_loop=True)
                        if ada:
                            if u == 0:
                                ada_fold(i)
                            ada_unit(u)

                two_pairs(0)
                turns = FC // 2
                with pe.Fori(1, turns) as i:
                    st.units = per * (i - 1)
                    two_pairs(i)
                st.units = 0
                st.skip(per * (turns - 2), 4 * (turns - 2))
                if ada:
                    ada_fold(turns)
                n["freed"] += 2 * FC
                for b in range(4):
                    owner[(st.block - 4 + b) % 4] = ("block_free", n["freed"])
                pe.wait_ge(sem("hidden_ready"), FC * (1 if name == "ffn1" else 2))
                for m in range(DC):
                    block_(FC, lambda k: FH[:, k, :], lambda k: FL[:, k, :])

            def ada_unit(u):
                pe.wait_ge(sem("lo_ready"), st.units_(st.step // UNIT + 1))
                slot = (st.step // UNIT) % RING
                for j in range(2):
                    k = 2 * u + j
                    w = slice(j * TOK, j * TOK + TOK)
                    pe.matmul(BANK[5][0:4, :], CP[:, k, :], HI[:, slot, w], start=(k == 0), stop=False)
                    ins = pe.matmul(BANK[5][0:4, :], CP[:, k, :], LO[:, slot, w], start=False, stop=(k == DC - 1))
                ins.then_inc(sem("pe_steps"), UNIT)
                st.step += UNIT
                st.told = st.step

            def ada_fold(g):
                pe.wait_ge(sem("ada_rows_ready"), g + 1)
                if not isinstance(g, int) or g:
                    pe.wait_ge(sem("ada_added"), g)
                for m in range(4):
                    ins = pe.matmul(BANK[6][:, 2 * m:2 * m + 2], AR[0:4, m * P:(m + 1) * P],
                                    VEC[0:4, VCOL["fold"]:VCOL["fold"] + 2], start=True, stop=True)
                ins.then_inc(sem("ada_folded"), 1)

            def attend(kind, h0=0, h1=None):
                steps = [s for s in attention_steps(kind) if h0 <= s[0] < (h1 or 99)]

                def scores(h, t, ranges):
                    for g, (k0, k1) in enumerate(ranges):
                        b = 5 + n["piece"] % 2
                        claim(b)
                        q0 = P * t
                        if kind == "dil":
                            lhs, rhs = DZ[:, g, q0:q0 + P], DZ[:, 3 + g, k0:k1]
                        elif kind == "mem":
                            lhs, rhs = MQ[:, h, q0:q0 + P], MKV[:, h, k0:k1]
                        else:
                            r0, c = 64 * (h % 2), h // 2
                            lhs = NZ[r0:r0 + 64, c, q0:q0 + P]
                            rhs = NZ[r0:r0 + 64, 4 + c, :] if g == 0 else CK[r0:r0 + 64, c, :]
                        pe.matmul(BANK[b][:, 0:k1 - k0], lhs, rhs, start=True, stop=True)\
                            .then_inc(sem("score_ready"), 1)
                        n["piece"] += 1
                        owner[b] = ("score_read", n["piece"])

                def values(h, t, ranges):
                    probs = (NS if kind == "na" else DS)[:, n["prob"] % 2]
                    n["prob"] += 1
                    pe.wait_ge(sem("prob_ready"), n["prob"])
                    cols, keys = 0, []
                    for g, (k0, k1) in enumerate(ranges):
                        for k in range(k0, k1, P):
                            if kind == "dil":
                                v = DV[:, g, k // P, :]
                            elif kind == "mem":
                                v = MV[:, h, k // P, :]
                            elif g == 0:
                                v = NV[:, k // P, 64 * h:64 * h + 64]
                            else:
                                v = CV[:, k // P, 64 * h:64 * h + 64]
                            keys.append((cols, v))
                            cols += P
                    b = 2 + n["ov"] % 2
                    claim(b)
                    r0, rows = (64 * (h % 2), 64) if kind == "na" else (0, P)
                    groups = [keys[i:i + 4] for i in range(0, len(keys), 4)]
                    base_ = n["turn"]
                    turn([probs[:, c:c + P] for c, _ in groups[0]])
                    for i, group in enumerate(groups):
                        if i + 1 < len(groups):
                            turn([probs[:, c:c + P] for c, _ in groups[i + 1]])
                        pe.wait_ge(sem("turned"), base_ + i + 1)
                        for j, (_, v) in enumerate(group):
                            ins = pe.matmul(BANK[b][r0:r0 + rows, 0:P], v,
                                            (NP if kind == "na" else DP)[:, n["ag"] % 2, j * P:(j + 1) * P],
                                            start=(i == 0 and j == 0),
                                            stop=(i == len(groups) - 1 and j == len(group) - 1))
                        ins.then_inc(sem("group_used"), 1)
                        n["ag"] += 1
                    n["ov"] += 1
                    owner[b] = ("out_read", n["ov"])

                before = None
                for s in steps:
                    scores(*s)
                    if before:
                        values(*before)
                    before = s
                values(*before)

            pe.wait_ge(sem("const_loaded"), 48)
            sums(DC, ONES, TOK)
            operand(1)
            for u in range(4):
                ada_unit(u)
            ffn("ffn1")
            owner[5] = ("ada_rows_ready", 12)
            owner[6] = ("ada_added", 12)
            sums(DC, ONES, TOK)
            sums(DC, ONES, TOK)
            operand(DC)
            for m in range(16):
                block_(DC, *x_ops())

            pe.wait_ge(sem("block_free"), n["freed"])
            for h in range(HEADS):
                turn([ZI[:, h, t * P:(t + 1) * P] for t in range(TT)])
            pe.wait_ge(sem("hg_factors_ready"), 1)
            for h in range(HEADS):
                turn([K2[:, h, t * P:(t + 1) * P] for t in range(TT)])
            for h in range(HEADS):
                b = 5 + h // 2
                if h % 2 == 0:
                    claim(b)
                for c in range(NCH):
                    r0, t = CH * (c % 2), c // 2
                    ins = pe.matmul(BANK[b][r0:r0 + CH, 256 * (h % 2) + CH * t:256 * (h % 2) + CH * t + CH],
                                    K1[:, h, CH * c:CH * c + CH], Q1[:, h, CH * c:CH * c + CH],
                                    start=True, stop=True)
                if h % 2:
                    ins.then_inc(sem("hg_scores_done"), 1)
                    owner[b] = ("hg_scores_read", h // 2 + 1)
            pe.wait_ge(sem("turned"), n["turn"])
            for c in range(NCH - 1):
                b, r0, t = c % 2, CH * (c % 2), c // 2
                claim(b)
                for h in range(HEADS):
                    ins = pe.matmul(BANK[b][:, h * P:(h + 1) * P], K2T[r0:r0 + CH, h, t * P:(t + 1) * P],
                                    VT[r0:r0 + CH, h, t * P:(t + 1) * P], start=True, stop=True)
                ins.then_inc(sem("kv_done"), 1)
                owner[b] = ("state_ready", c + 1)
            pe.wait_ge(sem("hg_scores_read"), 2)
            pe.wait_ge(sem("state_ready"), NCH - 1)
            for h in range(HEADS):
                b = 5 + h % 2
                claim(b)
                for t in range(TT):
                    pe.matmul(BANK[b][:, P * t:P * t + P], VT[:, h, t * P:(t + 1) * P], SC[:, h, t, :],
                              start=True, stop=False)
                    for c in range(max(1, 2 * t), 2 * t + 2):
                        ins = pe.matmul(BANK[b][:, CH * c:CH * c + CH], STATE[:, c, h, :],
                                        Q2[:, h, CH * c:CH * c + CH], start=False, stop=(c == 2 * t + 1))
                ins.then_inc(sem("hg_out_done"), 1)
                owner[b] = ("hg_out_read", h + 1)
            for h in range(HEADS):
                sums(1, ONES, TOK)

            for h in range(HEADS):
                for m in range(9):
                    block_(DC, *x_ops())
                pe.wait_ge(sem("block_free"), n["freed"])
                for g in range(3):
                    turn([DZ[:, 6 + g, t * P:(t + 1) * P] for t in range(TT)])
                attend("dil", h, h + 1)

            sums(DC, ONES, NMEM)
            operand(4 + 4 + DC)
            for m in range(8):
                block_(DC, lambda k: MH[:, k, :], lambda k: ML[:, k, :], width=NMEM)
            for m in range(4):
                block_(DC, *x_ops())
            pe.wait_ge(sem("block_free"), n["freed"])
            for h in range(HEADS):
                turn([MKV[:, 4 + h, t * P:(t + 1) * P] for t in range(2)])
            attend("mem")

            operand(4)
            for m in range(DC // 2):
                for _ in range(6):
                    block_(DC, *x_ops(), gate=True)
                for _ in range(2):
                    for br in range(3):
                        block_(4, lambda k: YH[br][:, k, :], lambda k: YL[br][:, k, :])
            operand(DC)
            for m in range(DC):
                block_(DC, *x_ops())
            sums(DC, ONES, TOK)
            sums(DC, ONES, TOK)
            ffn("ffn2")
            sums(DC, ONES, TOK)

            sums(DC, ONES, NMEM)
            operand(DC)
            for m in range(8):
                block_(DC, lambda k: CXH[:, k, :], lambda k: CXL[:, k, :], width=NMEM)
            for c in range(4):
                sums(1, PAIR, NMEM)
            pe.wait_ge(sem("block_free"), n["freed"])
            for t in range(2):
                turn([CVF[:, c, t * P:(t + 1) * P] for c in range(4)])

            pe.wait_ge(sem("filter_weights_loaded"), 80)
            for layer in range(3):
                if layer:
                    pe.wait_ge(sem("sin_ready"), layer)
                claim(5)
                lhs = FW1[0:33, :] if layer == 0 else FW[:, layer - 1, :]
                rhs = FTS[0:33, :] if layer == 0 else FX[:]
                pe.matmul(BANK[5][0:64, :], lhs, rhs, start=True, stop=True).then_inc(sem("layer_done"), 1)
                owner[5] = ("layer_read", layer + 1)
            pe.wait_ge(sem("sin_ready"), 3)
            for o in range(2):
                for t in range(TT):
                    for d in range(2):
                        b = 5 + n["small"] % 2
                        claim(b)
                        pe.matmul(BANK[b][:], FX[:, t * P:(t + 1) * P],
                                  FW4[:, (2 * o + d) * TOK:(2 * o + d + 1) * TOK], start=True, stop=True)\
                            .then_inc(sem("filter_done"), 1)
                        n["small"] += 1
                        owner[b] = ("filter_read", n["small"])
                claim(7)
                for i in range(2 * TT):
                    pe.wait_ge(sem("abs_ready"), 8 * o + i + 1)
                    pe.matmul(BANK[7][:], ONES[:], FAB[:, i % 2, :], start=(i == 0), stop=(i == 2 * TT - 1))\
                        .then_inc(sem("abs_used"), 1)
                owner[7] = ("norm_read", o + 1)
                operand(8)
                for m in range(KB):
                    e0 = 0 if m < 5 else 4
                    block_(TT, lambda k: EOH[:, e0 + k, :], lambda k: EOL[:, e0 + k, :])

            sums(DC, ONES, TOK)
            operand(DC)
            for m in range(12):
                block_(DC, *x_ops())
            for c in range(12):
                pe.wait_ge(sem("conv_ready"), c + 1)
                turn([HCV[:, c % 2, t * P:(t + 1) * P] for t in range(TT)])
            for o in range(2):
                operand(TT)
                for m in range(FB):
                    block_(TT, lambda k: SH[:, k, :], lambda k: SL[:, k, :])
                operand(FB)
                for m in range(TT):
                    block_(FB, lambda k: SPH[:, k, :], lambda k: SPL[:, k, :])
            pe.wait_ge(sem("block_free"), n["freed"])
            for t in range(TT):
                turn([HTM[:, 0, t, c * P:(c + 1) * P] for c in range(HYC)])

            operand(4 + DC)
            for m in range(12):
                block_(DC, *x_ops())
            pe.wait_ge(sem("rope_loaded"), 64)
            for c in range(8):
                sums(1, PAIR, TOK)
                pe.wait_ge(sem("normed_ready"), c + 1)
                claim(5)
                pe.matmul(BANK[5][:], SWAP[:], NZ[:, c, :], start=True, stop=True).then_inc(sem("swap_done"), 1)
                owner[5] = ("swap_read", c + 1)
            for t in range(TT):
                turn([NZ[:, 8 + c, t * P:(t + 1) * P] for c in range(4)])
            pe.wait_ge(sem("na_ready"), 1)
            attend("na")

            operand(4)
            for m in range(DC):
                for _ in range(2):
                    block_(DC, *x_ops(), gate=True)
                for br in range(2):
                    block_(4, lambda k: Y2H[br][:, k, :], lambda k: Y2L[br][:, k, :])
            operand(DC)
            for m in range(DC):
                block_(DC, *x_ops())
            sums(DC, ONES, TOK)

            operand(DC)
            for m in range(16):
                block_(DC, *x_ops())
            pe.wait_ge(sem("keys_loaded"), 16)
            pe.wait_ge(sem("block_free"), n["freed"])
            for t in range(TT):
                for q in range(4):
                    b = 5 + n["piece"] % 2
                    claim(b)
                    for j in range(4):
                        ins = pe.matmul(BANK[b][:, j * P:(j + 1) * P], QT[:, 4 * q + j, t * P:(t + 1) * P],
                                        KEYS[:, 4 * q + j, :], start=True, stop=True)
                    ins.then_inc(sem("score_ready"), 1)
                    n["piece"] += 1
                    owner[b] = ("score_read", n["piece"])
                for k in range(BY_TILE):
                    block_(DC, *x_ops(), gate=True)
                pe.wait_ge(sem("best_ready"), t + 1)
                turn([IJG[:, i, :] for i in range(3)])
            pe.wait_ge(sem("turned"), n["turn"])

            for b in (5, 6):
                claim(b)

            gelu0 = n["gate"]

            def gates_turn(i):
                for q in range(16):
                    pe.wait_ge(sem("hot_ready"), 16 * i + q + 1)
                    wait(pe, sem("stage_ready"), 16 * i + q - 1)
                    for u in range(4):
                        s = 4 * (q % 2) + u
                        ins = pe.matmul(BANK[5 + q % 2][:, u * P:(u + 1) * P], OI[:, s, :], OJ[:, s, :],
                                        start=True, stop=True)
                    ins.then_inc(sem("gates_done"), 1)
                    if q % 4 == 0:
                        pe.wait_ge(sem("gate_ready"), gelu0 + 4 * i + q // 4 - 3)
                    block_(DC, *x_ops(), in_loop=True, piece=(2 * (q % 4), 2 * (q % 4) + 1))

            gates_turn(0)
            with pe.Fori(1, GATE_TURNS) as i:
                st.units = 4 * (i - 1)
                gates_turn(i)
            st.units = 0
            st.skip(4 * (GATE_TURNS - 2), 4 * (GATE_TURNS - 2))
            n["gate"] += 4 * GATE_TURNS
            for b in range(4):
                owner[(st.block - 4 + b) % 4] = ("gate_ready", n["gate"])
            for b in (5, 6):
                owner[b] = ("stage_ready", TOK // 4)

            for b in range(4):
                claim(b)
            freed = n["freed"]

            def group(g):
                for m in range(8):
                    pe.wait_ge(sem("block_free"), freed + 16 * g + m - 3)
                    block_(DC, *x_ops(), in_loop=True)
                for m in range(8):
                    pe.wait_ge(sem("block_free"), freed + 16 * g + 8 + m - 3)
                    block_(8, lambda k: WH[:, k, :], lambda k: WL[:, k, :], in_loop=True,
                           ready=(lambda k: pe.wait_ge(sem("expert_ready"), 8 * g + k + 1)) if m == 0 else None)

            with pe.Fori(0, SHARED) as g:
                st.units = 16 * g
                group(g)
            st.units = 0
            st.skip(16 * (SHARED - 1), 16 * (SHARED - 1))

            def outputs(g):
                buffers = (WH2, WL2) if g % 2 == 0 else (WH, WL)
                return (lambda k: buffers[0][:, k, :]), (lambda k: buffers[1][:, k, :])

            def out_group(shift, j):
                pe.wait_ge(sem("expert_ready"), 8 * (SHARED + 1) + 8 * (shift + j))
                for m in range(8):
                    pe.wait_ge(sem("block_free"), freed + 16 * SHARED + 8 * (shift + j) + m - 3)
                    block_(8, *outputs(j), in_loop=True)

            with pe.Fori(0, AHEAD // 2) as i:
                st.units = 16 * i
                for j in range(2):
                    out_group(2 * i, j)
            st.units = 0
            st.skip(16 * (AHEAD // 2 - 1), 16 * (AHEAD // 2 - 1))
            out_group(AHEAD - 1, 0)

        @block.scalar
        def _(act):
            n = {"unit": 0, "square": 0, "sum": 0, "turn": 0, "ag": 0, "ov": 0, "f": 0, "gate": 0,
                 "exp": 0, "freed": 0, "h": 0}

            def split(k, shift=0):
                if isinstance(shift, int):
                    k += shift
                slot = k % RING
                loaded, used = 16 * (k // RING + 1), UNIT * (k - RING + 1)
                if isinstance(shift, int):
                    wait(act, sem(f"raw_loaded{slot}"), loaded)
                    wait(act, sem("pe_steps"), used)
                else:
                    act.wait_ge(sem(f"raw_loaded{slot}"), loaded + 4 * shift)
                    act.wait_ge(sem("pe_steps"), used + UNIT * shift)
                act.activation(HI[:, slot, :], RAW[:, slot, :], ACT.Copy).then_inc(sem("hi_ready"), 1)

            def units(count):
                for _ in range(count):
                    if n["unit"] + 3 < TOTAL:
                        split(n["unit"] + 3)
                    n["unit"] += 1

            def square(src, width, sem_name, value):
                act.wait_ge(sem(sem_name), value)
                wait(act, sem("square_used"), n["square"] - 1)
                act.activation(SQ[:, n["square"] % 2, 0:width], src, ACT.Square)\
                    .then_inc(sem("square_ready"), 1)
                n["square"] += 1

            def root(width):
                n["sum"] += 1
                act.wait_ge(sem("sum_read"), n["sum"])
                act.activation(RT[:, 0:width], MS[:, 0:width], ACT.Sqrt).then_inc(sem("root_ready"), 1)

            def high(dst, src):
                n["f"] += 1
                act.wait_ge(sem("piece_made"), n["f"])
                act.activation(dst, src, ACT.Copy).then_inc(sem("piece_high"), 1)

            def highs(hi, src, count):
                for c in range(count):
                    high(hi[:, c, :], src[:, c, :])

            def highs_after(hi, src, count, name, first, each=0):
                for c in range(count):
                    act.wait_ge(sem(name), first + each * c)
                    act.activation(hi[:, c, :], src[:, c, :], ACT.Copy).then_inc(sem("piece_high"), 1)

            def turned(dst, view=None):
                b = 4 if n["turn"] % 2 == 0 else 7
                n["turn"] += 1
                act.wait_ge(sem("turn_done"), n["turn"])
                cols = int(np.prod(dst.shape[1:]))
                src = BANK[b][0:dst.shape[0], 0:cols]
                if len(dst.shape) == 3:
                    src = src.rearrange("p (a b) -> p a b", a=dst.shape[1])
                act.activation(dst, src, ACT.Copy).then_inc(sem("turned"), 1)

            def ffn(name, freed0):
                n0 = n["unit"]
                mix = 2 if name == "ffn1" else 1

                def two_pairs(i):
                    for u in range(4 * mix):
                        split(n0 + 3 + u, 4 * mix * i)
                        if u % (2 * mix) == 1:
                            p = u // (2 * mix)
                            act.wait_ge(sem("pe_steps"), UNIT * (n0 + u) + UNIT * 4 * mix * i)
                            wait(act, sem("block_free"), freed0 + 4 * i + 2 * p - 2)
                            act.activation(SG[:, p, :], BANK[(n0_block[0] + 2 * p) % 4][:], ACT.Silu)\
                                .then_inc(sem("silu_ready"), 1)

                two_pairs(0)
                with act.Fori(1, FC // 2) as i:
                    two_pairs(i)
                n["unit"] += 2 * FC * mix
                n["freed"] = freed0 + 2 * FC
                n0_block[0] += 2 * FC
                units(DC * FC // UNIT)
                n["freed"] += DC
                n0_block[0] += DC

            n0_block = [0]

            def blocks(count, kc=DC):
                units(count * kc // UNIT)
                n0_block[0] += count
                n["freed"] += count

            def residual_squares():
                for c in range(DC):
                    square(HT[:, c, :], TOK, "h_ready", n["h"] + c + 1)
                n["h"] += DC
                root(TOK)

            def branch_squares(src):
                for c in range(DC):
                    square(src[:, c, :], TOK, "block_free", n["freed"] - DC + c + 1)
                root(TOK)

            def bias(h):
                if h > 1:
                    act.wait_ge(sem("score_read"), na_pieces[0] + 8 * (h - 1))
                act.dma_start(NB[:, h % 2, :], a["na_bias"][h]).then_inc(sem(f"na_bias_loaded{h % 2}"), 16)

            na_pieces = [HEADS * TT * 3 + HEADS * TT]

            def attend(kind, h0=0, h1=99):
                steps = [s for s in attention_steps(kind) if h0 <= s[0] < h1]
                S = NS if kind == "na" else DS
                T = NP if kind == "na" else DP

                def exps(h, t, ranges):
                    width, e = sum(k1 - k0 for k0, k1 in ranges), n["exp"] % 2
                    n["exp"] += 1
                    act.wait_ge(sem("max_ready"), n["exp"])
                    act.activation(S[:, e, 0:width], S[:, e, 0:width], ACT.Exp, bias=NMX[:, e:e + 1],
                                   accum_out=SUM[:, e:e + 1]).then_inc(sem("exp_ready"), 1)

                def transposed(h, t, ranges):
                    left = sum(k1 - k0 for k0, k1 in ranges) // P
                    while left:
                        k = min(4, left)
                        left -= k
                        wait(act, sem("group_used"), n["ag"] - 1)
                        turned(T[:, n["ag"] % 2, 0:k * P])
                        n["ag"] += 1

                def out(h, t, ranges):
                    groups = -(-(sum(k1 - k0 for k0, k1 in ranges) // P) // 4)
                    out_groups[0] += groups
                    act.wait_ge(sem("group_used"), out_groups[0])
                    b = 2 + n["ov"] % 2
                    n["ov"] += 1
                    if kind == "na":
                        r0 = 64 * (h % 2)
                        dst, src = NO[r0:r0 + 64, h // 2, t * P:(t + 1) * P], BANK[b][r0:r0 + 64, 0:P]
                    else:
                        dst, src = (DO if kind == "dil" else MO)[:, h, t * P:(t + 1) * P], BANK[b][:, 0:P]
                    act.activation(dst, src, ACT.Copy).then_inc(sem("out_read"), 1)

                before = None
                for s in steps:
                    if kind == "na" and s[1] == 1 and s[0] + 1 < NAH:
                        bias(s[0] + 1)
                    exps(*s)
                    if before:
                        transposed(*before)
                        out(*before)
                    before = s
                transposed(*before)
                out(*before)

            out_groups = [0]

            for k in range(3):
                split(k)
            act.wait_ge(sem("vec_loaded"), 16)
            c0 = VCOL["cond"]
            act.activation(CS[:].rearrange("p a b -> p (a b)"), VEC[:, c0:c0 + 16], ACT.Silu)\
                .then_inc(sem("cond_ready"), 1)
            act.wait_ge(sem("lb_shifted"), 1)
            act.activation(LB[:, 3:5, :], LB[:, 1:3, :], ACT.Exp).then_inc(sem("lb_exp"), 1)
            for c in range(DC):
                square(HT[:, c, :], TOK, "x_loaded", 16)
            root(TOK)
            highs(XH, XF, DC)
            units(4)
            ffn("ffn1", n["freed"])
            branch_squares(YT)
            residual_squares()
            highs(XH, XF, DC)
            blocks(16)
            act.wait_ge(sem("block_free"), n["freed"])
            act.activation(ZQ[:], ZQ[:], ACT.Silu).then_inc(sem("hg_q_ready"), 1)
            act.activation(ZF[:], ZF[:], ACT.Sigmoid).then_inc(sem("hg_sigmoid"), 1)
            act.activation(ZOG[:], ZOG[:], ACT.Sigmoid).then_inc(sem("hg_og_ready"), 1)
            for h in range(HEADS):
                turned(VT[:, h, :])
            act.dma_start(TRI[:], a["tri"]).then_inc(sem("tri_loaded"), 16)
            act.wait_ge(sem("hg_f_ready"), 1)
            act.activation(B0[:], ZF[:], ACT.Ln).then_inc(sem("hg_log"), 1)
            act.wait_ge(sem("hg_shift"), 1)
            act.activation(Q1[:], B1[:], ACT.Exp).then_inc(sem("hg_exp"), 1)
            act.activation(K1[:], B1[:], ACT.Exp, scale=-1.0).then_inc(sem("hg_exp"), 1)
            act.activation(Q2[:], B0[:], ACT.Exp).then_inc(sem("hg_exp"), 1)
            last = B0[:].rearrange("p h (n c) -> p (h n) c", c=CH)[:, :, CH - 1]
            act.activation(DEC[:], last, ACT.Exp).then_inc(sem("hg_exp"), 1)
            act.wait_ge(sem("hg_shift"), 2)
            act.activation(K2[:], B1[:], ACT.Exp).then_inc(sem("hg_exp"), 1)
            for h in range(HEADS):
                turned(K2T[:, h, :])
            for h in range(HEADS):
                square(OF[:, h, :], TOK, "hg_out_read", h + 1)
                root(TOK)
            highs(YH[0], OF, 4)

            for h in range(HEADS):
                if h:
                    act.wait_ge(sem("score_read"), 12 * h)
                act.dma_start(DB[:], a["dil_bias"][h]).then_inc(sem("bias_loaded"), 16)
                blocks(9)
                for g in range(3):
                    turned(DV[:, g].rearrange("p t d -> p (t d)"))
                attend("dil", h, h + 1)
            highs_after(YH[1], DO, 4, "out_read", n["ov"])

            act.wait_ge(sem("group_used"), out_groups[0])
            act.dma_start(MT[:], a["mem"]).then_inc(sem("mem_loaded"), 16)
            for c in range(DC):
                square(MT[:, c, :], NMEM, "mem_loaded", 16)
            root(NMEM)
            highs(MH, MF, DC)
            blocks(8)
            blocks(4)
            for h in range(HEADS):
                turned(MV[:, h].rearrange("p t d -> p (t d)"))
            attend("mem")
            highs_after(YH[2], MO, 4, "out_read", n["ov"])

            def gate(dst, bias):
                b = n0_block[0] % 4
                units(1)
                act.wait_ge(sem("pe_steps"), UNIT * n["unit"])
                act.activation(dst, BANK[b][:], ACT.Sigmoid, bias=bias).then_inc(sem("gate_ready"), 1)
                n["gate"] += 1
                n0_block[0] += 1

            for m in range(DC // 2):
                wait(act, sem("block_free"), n["freed"])
                for i in range(2):
                    for br in range(3):
                        gate(MG[:, 3 * i + br, :], vec("b_gate", br * DC + 2 * m + i))
                blocks(6, 4)
            highs(XH, MY, DC)
            blocks(DC)
            branch_squares(XF)
            residual_squares()
            highs(XH, XF, DC)
            ffn("ffn2", n["freed"])
            branch_squares(YT)

            act.wait_ge(sem("h_ready"), n["h"] + DC)
            act.dma_start(CT[:], a["ctx"]).then_inc(sem("ctx_loaded"), 16)
            for dst, name in ((FTS, "feats"), (FW1, "f1"), (FW, "f23"), (FW4, "f4"), (FVEC, "fvec")):
                act.dma_start(dst[:], a[name]).then_inc(sem("filter_weights_loaded"), 16)
            act.dma_start(DCY[:], a["decay"]).then_inc(sem("decay_loaded"), 16)
            act.dma_start(SKIP[:], a["skip"]).then_inc(sem("decay_loaded"), 16)
            for c in range(DC):
                square(CT[:, c, :], NMEM, "ctx_loaded", 16)
            root(NMEM)
            highs(CXH, CF, DC)
            blocks(8)
            for c in range(4):
                square(CK[:, c, :], NMEM, "block_free", n["freed"] - 7 + c)
                root(NMEM)
            for t in range(2):
                turned(CV[:, t, :])

            for layer in range(3):
                act.wait_ge(sem("angle_ready"), layer + 1)
                act.activation(FX[:], FA[:, 0, :], ACT.Sin).then_inc(sem("sin_ready"), 1)
            for o in range(2):
                for i in range(2 * TT):
                    t, d = i // 2, i % 2
                    act.wait_ge(sem("filter_read"), 8 * o + i + 1)
                    wait(act, sem("abs_used"), 8 * o + i - 1)
                    act.activation(FAB[:, i % 2, :], (FBW if d else FFW)[:, t, :], ACT.Abs)\
                        .then_inc(sem("abs_ready"), 1)
                highs(EOH[:, 0:4, :], FE, 4)
                highs(EOH[:, 4:8, :], FFW, 4)
                units(4 + o)
                n0_block[0] += KB
                n["freed"] += KB

            for c in range(DC):
                square(HT[:, c, :], TOK, "h_ready", n["h"] + c + 1)
            root(TOK)
            highs(XH, XF2, DC)
            blocks(12)
            for c in range(12):
                turned(HTM[:, c // 4, :, (c % 4) * P:(c % 4 + 1) * P])
            for o in range(2):
                if o == 0:
                    highs_after(SH, HTM[:, 0], TT, "turned", n["turn"])
                else:
                    highs_after(SH, HTM[:, 0], TT, "block_free", n["freed"] - TT + 1, 1)
                for i in range(4):
                    blocks(2, TT)
                    for j in range(2):
                        high(SPH[:, 2 * i + j, :], SQ[:, j, :])
                blocks(TT, FB)
            for t in range(TT):
                turned(HY[:, :, t * P:(t + 1) * P])
            highs_after(Y2H[0], HY, 4, "turned", n["turn"])
            highs(XH, XF, DC)

            for dst, name in ((COS, "cos"), (SIN, "sin"), (SWAP, "swap"), (CMASK, "cmask")):
                act.dma_start(dst[:], a[name]).then_inc(sem("rope_loaded"), 16)
            bias(0)
            blocks(12)
            for c in range(8):
                square(NZ[:, c, :], TOK, "block_free", n["freed"] - 12 + c + 1)
                root(TOK)
            for t in range(TT):
                turned(NV[:, t, :])
            attend("na")
            highs_after(Y2H[1], NO, 4, "out_read", n["ov"])
            for m in range(DC):
                act.wait_ge(sem("block_free"), n["freed"] - (2 if m else 0))
                for br in range(2):
                    gate(MG[:, 2 * (m % 2) + br, :], vec("b_in2", 24 + br * DC + m))
                blocks(2, 4)
            highs(XH, MY, DC)
            blocks(DC)
            branch_squares(HT)

            highs(XH, XF, DC)
            blocks(16)
            act.dma_start(KEYS[:], a["keys"]).then_inc(sem("keys_loaded"), 16)
            act.dma_start(IOTA[:], a["iota"]).then_inc(sem("iota_loaded"), 16)
            def ahead_gelu(j, steps, shift=0):
                s = j % 2
                act.wait_ge(sem("pe_steps"), steps)
                wait(act, sem(f"ahead_stored{s}"), 16 * (j // 2) + (shift if isinstance(shift, int) else 8 * shift))
                act.activation(SQ[:, s, :], BANK[(n0_block[0]) % 4][:], ACT.Gelu).then_inc(sem("gate_ready"), 1)
                act.wait_ge(sem("gate_ready"), n["gate"] + j + 1 + shift)
                act.dma_start(UD[j + shift], SQ[:, s, :]).then_inc(sem(f"ahead_stored{s}"), 16)
                n0_block[0] += 1

            for t in range(TT):
                for k in range(BY_TILE):
                    units(1)
                    ahead_gelu(BY_TILE * t + k, UNIT * n["unit"])
                    if k == BY_TILE - 3:
                        act.wait_ge(sem("best_shift"), t + 1)
                        act.activation(BS[:], BS[:], ACT.Exp).then_inc(sem("best_exp"), 1)
                turned(IJGT[:, :, t * P:(t + 1) * P])

            def stage(i, q16):
                s, q = q16 // 4 % 2, q16 % 4
                act.wait_ge(sem("gates_done"), 16 * i + q16 + 1)
                wait(act, sem(f"stage_stored{s}"), 32 * i + 16 * (q16 // 8))
                act.activation(STG[:, s, :, 4 * q:4 * q + 4].rearrange("p j t -> p t j"),
                               BANK[5 + q % 2][:].rearrange("p (t j) -> p t j", t=4), ACT.Copy)\
                    .then_inc(sem("stage_ready"), 1)

            n0 = n["unit"]

            def gates_turn(i):
                for q in range(16):
                    stage(i, q)
                    if q % 4 == 0:
                        split(n0 + 3 + q // 4, 4 * i)
                    if q % 4 == 3:
                        u = q // 4
                        ahead_gelu(BY_TILE * TT + u, UNIT * (n0 + u + 1) + 4 * UNIT * i, 4 * i)

            gates_turn(0)
            with act.Fori(1, GATE_TURNS) as i:
                gates_turn(i)
            n["unit"] += 4 * GATE_TURNS
            n0 = n["unit"]

            def gelus(g, shift):
                for u in range(16):
                    split(n0 + 3 + u, shift)
                    if u < 8:
                        act.wait_ge(sem("pe_steps"), UNIT * (n0 + u + 1) + UNIT * shift)
                        wait(act, sem("gates_used"), 8 * g + u - 1)
                        act.activation(GE[:, u % 2, :], BANK[(n0_block[0] + u) % 4][:], ACT.Gelu)\
                            .then_inc(sem("gelu_ready"), 1)

            gelus(0, 0)
            with act.Fori(1, SHARED) as g:
                gelus(g, 16 * g)
            n["unit"] += 16 * SHARED
            n0 = n["unit"]
            with act.Fori(0, AHEAD - 1) as g:
                for u in range(8):
                    split(n0 + 3 + u, 8 * g)
            n["unit"] += 8 * (AHEAD - 1)
            units(8)

        @block.vector
        def _(dve):
            st = Stepper()
            n = {"freed": 0, "square": 0, "sum": 0, "high": 0, "piece": 0, "exp": 0, "product": 0,
                 "gate": 0, "groups": [], "operand": 1, "made": 0}
            link = Link(dve, sem("dve_order"))

            def done(kc):
                st.step += kc
                dve.wait_ge(sem("pe_steps"), st.steps_(st.step))
                b = st.block % 4
                st.block += 1
                return BANK[b]

            def free(ins, count=1):
                n["freed"] += count
                ins.then_inc(sem("block_free"), count)

            def evacuated():
                dve.wait_ge(sem("block_free"), n["freed"])

            def copy_blocks(dst, count, kc=DC, width=TOK, bias=None):
                for m in range(count):
                    bank = done(kc)
                    if bias is None:
                        free(dve.tensor_copy(dst[:, m, 0:width], bank[:, 0:width]))
                    else:
                        free(dve.tensor_scalar(dst[:, m, 0:width], bank[:, 0:width], bias(m), None, ALU.add))

            def rstd(pieces, denom, width):
                n["square"] += pieces
                n["sum"] += 1
                dve.wait_ge(sem("square_used"), n["square"])
                dve.tensor_scalar(MS[:, 0:width], STB[:, 0:width], 1.0 / denom, EPS, ALU.mult, ALU.add)\
                    .then_inc(sem("sum_read"), 1)
                dve.wait_ge(sem("root_ready"), n["sum"])
                link(dve.reciprocal(RSTD[:, 0:width], RT[:, 0:width]))

            def made(ins):
                ins.then_inc(sem("piece_made"), 1)
                n["made"] += 1

            def low(dst, src, high):
                n["high"] += 1
                dve.wait_ge(sem("piece_high"), n["high"])
                dve.tensor_tensor(dst, src, high.bitcast(F32), ALU.subtract).then_inc(sem("operand_ready"), 1)
                n["operand"] += 1

            def lows(lo, src, hi, count):
                for c in range(count):
                    low(lo[:, c, :], src[:, c, :], hi[:, c, :])
                dve.wait_ge(sem("operand_ready"), n["operand"])

            def normed(dst, src, hi, lo, width, gain, shift=None):
                for c in range(DC):
                    ins = dve.scalar_tensor_tensor(dst[:, c, :], src[:, c, :], gain(c), RSTD[:, 0:width],
                                                   ALU.mult, ALU.mult)
                    if shift is None:
                        made(ins)
                    else:
                        link(ins)
                        made(dve.tensor_scalar(dst[:, c, :], dst[:, c, :], shift(c), None, ALU.add))
                lows(lo, dst, hi, DC)

            def post(src, name, factor):
                for c in range(DC):
                    link(dve.scalar_tensor_tensor(src[:, c, :], src[:, c, :], vec(name, c), RSTD[:],
                                                  ALU.mult, ALU.mult))
                    dve.scalar_tensor_tensor(HT[:, c, :], src[:, c, :], factor, HT[:, c, :],
                                             ALU.mult, ALU.add).then_inc(sem("h_ready"), 1)

            def ffn(k):
                s0, b0, freed0 = st.step, st.block, n["freed"]
                mix = 1 if k else 2
                with dve.Fori(0, FC // 2) as i:
                    for p in range(2):
                        dve.wait_ge(sem("pe_steps"), s0 + UNIT * ((2 * p + 1) * mix + 1) + 4 * mix * UNIT * i)
                        dve.wait_ge(sem("silu_ready"), FC * k + 2 * i + p + 1)
                        dve.tensor_tensor(HF[:, p, :], SG[:, p, :], BANK[(b0 + 2 * p + 1) % 4][:], ALU.mult)\
                            .then_inc(sem("block_free"), 2)
                        dve.wait_ge(sem("block_free"), freed0 + 4 * i + 2 * p + 2)
                        dve.tensor_copy(FH[:, 2 * i + p, :], HF[:, p, :]).then_inc(sem("hidden_high"), 1)
                        dve.wait_ge(sem("hidden_high"), FC * k + 2 * i + p + 1)
                        dve.tensor_tensor(FL[:, 2 * i + p, :], HF[:, p, :], FH[:, 2 * i + p, :].bitcast(F32),
                                          ALU.subtract).then_inc(sem("hidden_ready"), 1)
                        if k == 0 and p == 0:
                            ada_columns(i)
                    if k == 0:
                        ada_rows(i + 1, s0 + 8 * UNIT + 8 * UNIT * i)
                st.skip(2 * FC * mix, 2 * FC)
                if k == 0:
                    ada_columns(FC // 2)
                n["freed"] += 2 * FC
                copy_blocks(YT, DC, FC)

            def ada_rows(g, steps):
                dve.wait_ge(sem("pe_steps"), steps)
                dve.tensor_copy(AR[:], BANK[5][0:4, :]).then_inc(sem("ada_rows_ready"), 1)

            def ada_columns(g):
                dve.wait_ge(sem("ada_folded"), g + 1)
                which = slice(4 * g, 4 * g + 4) if isinstance(g, int) else bass.ds(4 * g, 4)
                bias = VEC[:, VCOL["b_ada"]:VCOL["b_ada"] + 48][:, which]
                dve.tensor_tensor(MOD[:, which, :], BANK[6][:, 0:8].rearrange("p (m w) -> p m w", w=2),
                                  bias.unsqueeze(2).to_broadcast([P, 4, 2]), ALU.add)\
                    .then_inc(sem("ada_added"), 1)

            def attend(kind, h0=0, h1=99):
                steps = [s for s in attention_steps(kind) if h0 <= s[0] < h1]
                S = NS if kind == "na" else DS
                scale = 0.125 if kind == "na" else P ** -0.5

                def scores(h, t, ranges):
                    e = n["exp"] % 2
                    if n["exp"] >= 2:
                        dve.wait_ge(sem("group_used"), n["groups"][n["exp"] - 2])
                    col = 0
                    for g, (k0, k1) in enumerate(ranges):
                        bank = SCB[n["piece"] % 2]
                        n["piece"] += 1
                        dve.wait_ge(sem("score_ready"), n["piece"])
                        w = k1 - k0
                        dst = S[:, e, col:col + w]
                        if kind == "dil":
                            x0 = k0 + (TOK - P) - P * t
                            ins = dve.scalar_tensor_tensor(dst, bank[:, 0:w], scale, DB[:, g, x0:x0 + w],
                                                           ALU.mult, ALU.add)
                        elif kind == "na" and g == 0:
                            ins = dve.scalar_tensor_tensor(dst, bank[:, 0:w], scale,
                                                           NB[:, h % 2, 64 * (6 - 2 * t):64 * (14 - 2 * t)],
                                                           ALU.mult, ALU.add)
                        else:
                            ins = dve.tensor_scalar(dst, bank[:, 0:w], scale, None, ALU.mult)
                        ins.then_inc(sem("score_read"), 1)
                        col += w
                    before = n["groups"][-1] if n["groups"] else 0
                    n["groups"].append(before - (-(col // P) // 4))
                    n["exp"] += 1
                    dve.wait_ge(sem("score_read"), n["piece"])
                    dve.tensor_reduce(NMX[:, e:e + 1], S[:, e, 0:col], AX_X, ALU.max, negate=True)\
                        .then_inc(sem("max_ready"), 1)

                def divide(h, t, ranges):
                    k = n["product"]
                    n["product"] += 1
                    e, width = k % 2, sum(k1 - k0 for k0, k1 in ranges)
                    dve.wait_ge(sem("exp_ready"), k + 1)
                    link(dve.reciprocal(RSUM[:, e:e + 1], SUM[:, e:e + 1]))
                    dve.tensor_scalar(S[:, e, 0:width], S[:, e, 0:width], RSUM[:, e:e + 1], None, ALU.mult)\
                        .then_inc(sem("prob_ready"), 1)

                before = None
                for s in steps:
                    if kind == "na" and s[1] == 0:
                        h = s[0]
                        dve.wait_ge(sem(f"na_bias_loaded{h % 2}"), 16 * (h // 2 + 1))
                        table = NB[:, h % 2, :].rearrange("p (x c) -> p x c", c=64)
                        link(dve.tensor_tensor(table, table, CMASK[:].unsqueeze(1).to_broadcast([P, 14, 64]),
                                               ALU.add))
                    scores(*s)
                    if before:
                        divide(*before)
                    before = s
                divide(*before)

            dve.wait_ge(sem("vec_loaded"), 16)
            lb = [VEC[:, VCOL["lb0"]:VCOL["lb0"] + 4], VEC[:, VCOL["lb1"]:VCOL["lb1"] + 4]]
            link(dve.tensor_tensor(LB[:, 0, :], lb[0], lb[1], ALU.max))
            link(dve.tensor_tensor(LB[:, 1, :], lb[0], LB[:, 0, :], ALU.subtract))
            dve.tensor_tensor(LB[:, 2, :], lb[1], LB[:, 0, :], ALU.subtract).then_inc(sem("lb_shifted"), 1)
            dve.wait_ge(sem("lb_exp"), 1)
            link(dve.tensor_tensor(LB[:, 0, :], LB[:, 3, :], LB[:, 4, :], ALU.add))
            link(dve.reciprocal(LB[:, 1, :], LB[:, 0, :]))
            link(dve.tensor_tensor(LB[:, 2, :], LB[:, 3, :], LB[:, 1, :], ALU.mult))
            link(dve.tensor_scalar(LB[:, 5, :], LB[:, 2, :], -1.0, 1.0, ALU.mult, ALU.add))
            dve.wait_ge(sem("cond_ready"), 1)
            link(dve.tensor_copy(CP[:, :, 0:2], CS[:]))
            dve.tensor_tensor(CP[:, :, 2:4], CS[:], CP[:, :, 0:2].bitcast(F32), ALU.subtract)\
                .then_inc(sem("operand_ready"), 1)
            rstd(DC, D, TOK)
            normed(XF, HT, XH, XL, TOK, lambda c: vec("ffn1_pre", c))
            st.skip(4, 0)
            ada_rows(0, st.step)
            ffn(0)
            dve.wait_ge(sem("ada_added"), 12)
            norm = [VEC[:, VCOL[k]:VCOL[k] + 8] for k in ("norm1", "norm1", "norm2")]
            for i, (c0, who) in enumerate(((8, 0), (8, 1), (32, 0))):
                link(dve.scalar_tensor_tensor(COEF[:, i, :], MOD[:, c0:c0 + 8, who], 1.0, norm[i],
                                              ALU.add, ALU.mult))
            rstd(DC, D, TOK)
            post(YT, "ffn1_post", 0.5)
            rstd(DC, D, TOK)
            normed(XF, HT, XH, XL, TOK, lambda c: vec("mix_pre", c))

            for z in (ZQ, ZF, ZI, ZOG):
                copy_blocks(z, 4)
            dve.wait_ge(sem("hg_sigmoid"), 1)
            for h in range(HEADS):
                link(dve.tensor_scalar(ZF[:, h, :], ZF[:, h, :], LB[:, 5, h:h + 1], LB[:, 2, h:h + 1],
                                       ALU.mult, ALU.add))
            dve.tensor_scalar(KF[:], ZF[:], -1.0, 1.0, ALU.mult, ALU.add).then_inc(sem("hg_f_ready"), 1)
            dve.wait_ge(sem("hg_log"), 1)
            chunks = [b[:].rearrange("p h (n c) -> p (h n) c", c=CH) for b in (B0, B1)]
            d = 1
            for i in range(6):
                src, dst = chunks[i % 2], chunks[1 - i % 2]
                link(dve.tensor_copy(dst[:, :, 0:d], src[:, :, 0:d]))
                link(dve.tensor_tensor(dst[:, :, d:CH], src[:, :, d:CH], src[:, :, 0:CH - d], ALU.add))
                d *= 2

            def shifted(at, sign):
                edge = chunks[0][:, :, at:at + 1].to_broadcast([P, HEADS * NCH, CH])
                pair = (chunks[0], edge) if sign > 0 else (edge, chunks[0])
                dve.tensor_tensor(chunks[1], *pair, ALU.subtract).then_inc(sem("hg_shift"), 1)

            shifted(CH // 2 - 1, 1)
            dve.wait_ge(sem("hg_exp"), 2)
            shifted(CH - 1, -1)
            dve.wait_ge(sem("hg_q_ready"), 1)
            link(dve.tensor_tensor(Q1[:], Q1[:], ZQ[:], ALU.mult))
            link(dve.tensor_tensor(K1[:], K1[:], KF[:], ALU.mult))
            dve.wait_ge(sem("hg_exp"), 5)
            link(dve.tensor_tensor(Q2[:], Q2[:], ZQ[:], ALU.mult))
            dve.tensor_tensor(K2[:], K2[:], KF[:], ALU.mult).then_inc(sem("hg_factors_ready"), 1)
            dve.wait_ge(sem("turned"), HEADS)
            link(dve.memset(SC[:], 0.0))
            dve.wait_ge(sem("tri_loaded"), 16)
            for i in range(2):
                dve.wait_ge(sem("hg_scores_done"), i + 1)
                for j in range(4):
                    r0 = CH * (j % 2)
                    bank = BANK[5 + i][r0:r0 + CH, 256 * (j // 2):256 * (j // 2) + 256]
                    ins = dve.copy_predicated(SC[r0:r0 + CH, 2 * i + j // 2, :, r0:r0 + CH],
                                              TRI[r0:r0 + CH], bank.rearrange("p (t c) -> p t c", c=CH))
                    if j < 3:
                        link(ins)
                ins.then_inc(sem("hg_scores_read"), 1)
            for c in range(NCH - 1):
                dve.wait_ge(sem("kv_done"), c + 1)
                for h in range(HEADS):
                    kv = BANK[c % 2][:, h * P:(h + 1) * P]
                    if c == 0:
                        ins = dve.tensor_copy(STATE[:, 1, h, :], kv)
                    else:
                        ins = dve.scalar_tensor_tensor(STATE[:, c + 1, h, :], STATE[:, c, h, :],
                                                       DEC[:, h * NCH + c:h * NCH + c + 1], kv,
                                                       ALU.mult, ALU.add)
                    if h < HEADS - 1:
                        link.n += 1
                        ins.then_inc(sem("dve_order"), 1)
                ins.then_inc(sem("state_ready"), 1)
                dve.wait_ge(sem("state_ready"), c + 1)
                dve.wait_ge(sem("dve_order"), link.n)
            for h in range(HEADS):
                dve.wait_ge(sem("hg_out_done"), h + 1)
                dve.tensor_copy(OF[:, h, :], BANK[5 + h % 2][:]).then_inc(sem("hg_out_read"), 1)
            for h in range(HEADS):
                rstd(1, P, TOK)
                link(dve.scalar_tensor_tensor(OF[:, h, :], OF[:, h, :], vec("hgn"), RSTD[:], ALU.mult, ALU.mult))
                dve.wait_ge(sem("hg_og_ready"), 1)
                made(dve.tensor_tensor(OF[:, h, :], OF[:, h, :], ZOG[:, h, :], ALU.mult))
            lows(YL[0], OF, YH[0], 4)

            for h in range(HEADS):
                copy_blocks(DZ, 9)
                dve.wait_ge(sem("bias_loaded"), 16 * (h + 1))
                attend("dil", h, h + 1)
            lows(YL[1], DO, YH[1], 4)

            rstd(DC, D, NMEM)
            normed(MF, MT, MH, ML, NMEM, lambda c: vec("mem_norm", c))
            copy_blocks(MKV, 8, width=NMEM)
            copy_blocks(MQ, 4)
            attend("mem")
            lows(YL[2], MO, YH[2], 4)

            def merge(dst, gates):
                dve.wait_ge(sem("piece_made"), n["made"])
                for i, gate in enumerate(gates):
                    free(dve.tensor_tensor(MP[:, i, :], gate, done(4)[:], ALU.mult))
                evacuated()
                if len(gates) == 3:
                    link(dve.tensor_tensor(MP[:, 0, :], MP[:, 0, :], MP[:, 1, :], ALU.add))
                made(dve.tensor_tensor(dst, MP[:, 0, :], MP[:, len(gates) - 1, :], ALU.add))

            gates_seen = 0
            for m in range(DC // 2):
                st.step += 6 * UNIT
                st.block += 6
                gates_seen += 6
                dve.wait_ge(sem("gate_ready"), gates_seen)
                for i in range(2):
                    merge(MY[:, 2 * m + i, :], [MG[:, 3 * i + br, :] for br in range(3)])
            lows(XL, MY, XH, DC)
            copy_blocks(XF, DC)
            rstd(DC, D, TOK)
            post(XF, "mix_post", 1.0)
            rstd(DC, D, TOK)
            normed(XF, HT, XH, XL, TOK, lambda c: vec("ffn2_pre", c))
            ffn(1)
            rstd(DC, D, TOK)
            post(YT, "ffn2_post", 0.5)

            rstd(DC, D, NMEM)
            normed(CF, CT, CXH, CXL, NMEM, lambda c: COEF[:, 1, c:c + 1], lambda c: MOD[:, c, 1:2])
            copy_blocks(CK, 4, width=NMEM, bias=lambda m: vec("b_in2", 16 + m))
            copy_blocks(CVF, 4, width=NMEM, bias=lambda m: vec("b_in2", 20 + m))
            for c in range(4):
                rstd(1, 64, NMEM)
                link(dve.scalar_tensor_tensor(CK[:, c, :], CK[:, c, :], vec("kg"), RSTD[:, 0:NMEM],
                                              ALU.mult, ALU.mult))

            dve.wait_ge(sem("filter_weights_loaded"), 80)
            round_up = 1.5 * 2.0 ** 23
            two_pi_hi = 6.28125
            two_pi_lo = 2.0 * np.pi - two_pi_hi
            for layer in range(3):
                dve.wait_ge(sem("layer_done"), layer + 1)
                dve.tensor_scalar(FA[:, 0, :], BANK[5][0:64, :], FVEC[:, layer:layer + 1], FVEC[:, 3:4],
                                  ALU.add, ALU.mult).then_inc(sem("layer_read"), 1)
                dve.wait_ge(sem("layer_read"), layer + 1)
                link(dve.tensor_scalar(FA[:, 1, :], FA[:, 0, :], 1.0 / (2.0 * np.pi), round_up, ALU.mult, ALU.add))
                link(dve.tensor_scalar(FA[:, 1, :], FA[:, 1, :], round_up, None, ALU.subtract))
                link(dve.scalar_tensor_tensor(FA[:, 2, :], FA[:, 1, :], -two_pi_hi, FA[:, 0, :], ALU.mult, ALU.add))
                link(dve.scalar_tensor_tensor(FA[:, 0, :], FA[:, 1, :], -two_pi_lo, FA[:, 2, :], ALU.mult, ALU.add))
                dve.tensor_scalar(FA[:, 0, :], FA[:, 0, :], 3.1415925, -3.1415925, ALU.min, ALU.max)\
                    .then_inc(sem("angle_ready"), 1)
            dve.wait_ge(sem("sin_ready"), 3)
            dve.wait_ge(sem("decay_loaded"), 32)
            for o in range(2):
                for i in range(2 * TT):
                    t, d = i // 2, i % 2
                    k = 8 * o + i
                    dve.wait_ge(sem("filter_done"), k + 1)
                    dve.tensor_tensor((FBW if d else FFW)[:, t, :], BANK[5 + k % 2][:], DCY[:, t, :], ALU.mult)\
                        .then_inc(sem("filter_read"), 1)
                dve.wait_ge(sem("abs_used"), 8 * (o + 1))
                dve.reciprocal(RSTD[:], BANK[7][:]).then_inc(sem("norm_read"), 1)
                dve.wait_ge(sem("norm_read"), o + 1)
                link(dve.memset(FBW[0:1, 0, :], 0.0))
                link(dve.tensor_tensor(FE[:], FFW[:], FBW[:], ALU.add))
                link(dve.tensor_tensor(FFW[:], FFW[:], FBW[:], ALU.subtract))
                for t in range(TT):
                    ins = dve.tensor_tensor(FE[:, t, :], FE[:, t, :], RSTD[:], ALU.mult)
                    if t == 0:
                        link(ins)
                        ins = dve.tensor_tensor(FE[0:1, 0, :], FE[0:1, 0, :], SKIP[0:1, o, :], ALU.add)
                    made(ins)
                for t in range(TT):
                    made(dve.tensor_tensor(FFW[:, t, :], FFW[:, t, :], RSTD[:], ALU.mult))
                lows(EOL[:, 0:4, :], FE, EOH[:, 0:4, :], 4)
                lows(EOL[:, 4:8, :], FFW, EOH[:, 4:8, :], 4)
                copy_blocks(KHAT[:, o], KB, TT)

            rstd(DC, D, TOK)
            normed(XF2, HT, XH, XL, TOK, lambda c: COEF[:, 0, c:c + 1], lambda c: MOD[:, c, 0:1])
            turns0 = 4 + 4 + 12 + sum(-(-(sum(k1 - k0 for k0, k1 in r) // P) // 4)
                                      for kind in ("dil", "mem") for _, _, r in attention_steps(kind)) + 4 + 2
            for c in range(12):
                bank = done(DC)
                free(dve.tensor_scalar(HZ[:, c, :], bank[:], vec("b_in2", c), None, ALU.add))
            evacuated()
            for c in range(12):
                if c >= 2:
                    dve.wait_ge(sem("turned"), turns0 + c - 1)
                z, out = HZ[:, c, :], HCV[:, c % 2, :]
                link(dve.tensor_scalar(out, z, vec("cw1", c), vec("cb", c), ALU.mult, ALU.add))
                link(dve.scalar_tensor_tensor(out[:, 1:TOK], z[:, 0:TOK - 1], vec("cw0", c), out[:, 1:TOK],
                                              ALU.mult, ALU.add))
                dve.scalar_tensor_tensor(out[:, 0:TOK - 1], z[:, 1:TOK], vec("cw2", c), out[:, 0:TOK - 1],
                                         ALU.mult, ALU.add).then_inc(sem("conv_ready"), 1)
            dve.wait_ge(sem("turned"), turns0 + 12)
            for o in range(2):
                lows(SL, HTM[:, 0], SH, TT)
                for i in range(4):
                    ar, ai = done(TT), done(TT)
                    kr, ki = KHAT[:, o, i, :], KHAT[:, o, 5 + i, :]
                    kr2 = KHAT[:, o, 4, :] if i == 0 else kr
                    t0, t1 = HCV[:, 0, :], HCV[:, 1, :]
                    dve.wait_ge(sem("piece_made"), n["made"])
                    link(dve.tensor_tensor(t0, ar[:], kr, ALU.mult))
                    link(dve.tensor_tensor(t1, ai[:], ki, ALU.mult))
                    made(dve.tensor_tensor(SQ[:, 0, :], t0, t1, ALU.subtract))
                    dve.wait_ge(sem("piece_made"), n["made"])
                    link(dve.tensor_tensor(t0, ar[:], ki, ALU.mult))
                    free(dve.tensor_tensor(t1, ai[:], kr2, ALU.mult), 2)
                    evacuated()
                    made(dve.tensor_tensor(SQ[:, 1, :], t0, t1, ALU.add))
                    for j in range(2):
                        low(SPL[:, 2 * i + j, :], SQ[:, j, :], SPH[:, 2 * i + j, :])
                for t in range(TT):
                    bank = done(FB)
                    free(dve.tensor_tensor(HTM[:, 0, t, :], bank[:], HTM[:, 1 + o, t, :], ALU.mult))
                evacuated()
            lows(Y2L[0], HY, Y2H[0], 4)
            normed(XF, HT, XH, XL, TOK, lambda c: COEF[:, 0, c:c + 1], lambda c: MOD[:, c, 0:1])

            copy_blocks(NZ, 12, bias=lambda m: vec("b_in2", 12 + m))
            dve.wait_ge(sem("rope_loaded"), 64)
            for c in range(8):
                rstd(1, 64, TOK)
                dve.scalar_tensor_tensor(NZ[:, c, :], NZ[:, c, :], vec("qg" if c < 4 else "kg"), RSTD[:],
                                         ALU.mult, ALU.mult).then_inc(sem("normed_ready"), 1)
                dve.wait_ge(sem("normed_ready"), c + 1)
                dve.wait_ge(sem("swap_done"), c + 1)
                link(dve.tensor_tensor(RP[:, 0, :], NZ[:, c, :], COS[:], ALU.mult))
                dve.tensor_tensor(RP[:, 1, :], BANK[5][:], SIN[:], ALU.mult).then_inc(sem("swap_read"), 1)
                dve.wait_ge(sem("swap_read"), c + 1)
                ins = dve.tensor_tensor(NZ[:, c, :], RP[:, 0, :], RP[:, 1, :], ALU.add)
                if c == 7:
                    ins.then_inc(sem("na_ready"), 1)
                else:
                    link(ins)
            attend("na")
            lows(Y2L[1], NO, Y2H[1], 4)
            for m in range(DC):
                st.step += 2 * UNIT
                st.block += 2
                gates_seen += 2
                dve.wait_ge(sem("gate_ready"), gates_seen)
                merge(MY[:, m, :], [MG[:, 2 * (m % 2) + br, :] for br in range(2)])
            lows(XL, MY, XH, DC)
            for m in range(DC):
                bank = done(DC)
                free(dve.scalar_tensor_tensor(HT[:, m, :], bank[:], MOD[:, 16 + m, 0:1], HT[:, m, :],
                                              ALU.mult, ALU.add))

            rstd(DC, D, TOK)
            normed(XF, HT, XH, XL, TOK, lambda c: COEF[:, 2, c:c + 1], lambda c: MOD[:, 24 + c, 0:1])
            copy_blocks(QT, 16)
            dve.wait_ge(sem("iota_loaded"), 16)
            turns1 = turns0 + 12 + 4 + 4 + 2 * NAH * TT
            def ordered(instructions):
                for ins in instructions:
                    link.n += 1
                    ins.then_inc(sem("dve_order"), 1)
                dve.wait_ge(sem("dve_order"), link.n)

            for t in range(TT):
                for q in range(4):
                    bank = SCB[n["piece"] % 2]
                    n["piece"] += 1
                    dve.wait_ge(sem("score_ready"), n["piece"])
                    dve.tensor_copy(PS[:, 4 * q:4 * q + 4, :].rearrange("p a b -> p (a b)"), bank[:])\
                        .then_inc(sem("score_read"), 1)
                dve.wait_ge(sem("score_read"), n["piece"])
                ordered(dve.max(TOPS[:, j, 0:8], PS[:, j, :]) for j in range(16))
                ordered(dve.max_index(TOPI[:, j, 0:8], TOPS[:, j, 0:8], PS[:, j, :]) for j in range(16))
                ordered(dve.match_replace(PR[:, j, :], TOPS[:, j, 0:8], PS[:, j, :], -BIG) for j in range(16))
                ordered(dve.max(TOPS[:, j, 8:16], PR[:, j, :]) for j in range(16))
                ordered(dve.max_index(TOPI[:, j, 8:16], TOPS[:, j, 8:16], PR[:, j, :]) for j in range(16))
                link(dve.tensor_copy(TOPF[:], TOPI[:]))
                tops = TOPS[:].rearrange("p (h two) k -> p h two k", two=2)
                topf = TOPF[:].rearrange("p (h two) k -> p h two k", two=2)
                square4 = [P, 8, 16, 16]
                link(dve.tensor_tensor(CA[:].rearrange("p h (a b) -> p h a b", a=16),
                                       tops[:, :, 0, :].unsqueeze(3).to_broadcast(square4),
                                       tops[:, :, 1, :].unsqueeze(2).to_broadcast(square4), ALU.add))
                ordered(dve.max(BS[:, h, 0:8], CA[:, h, :]) for h in range(8))
                ordered(dve.max_index(BP[:, h, 0:8], BS[:, h, 0:8], CA[:, h, :]) for h in range(8))
                ordered(dve.match_replace(CR[:, h, :], BS[:, h, 0:8], CA[:, h, :], -BIG) for h in range(8))
                ordered(dve.max(BS[:, h, 8:16], CR[:, h, :]) for h in range(8))
                ordered(dve.max_index(BP[:, h, 8:16], BS[:, h, 8:16], CR[:, h, :]) for h in range(8))
                link(dve.tensor_copy(PRS[:], BS[:, :, 0]))
                dve.tensor_tensor(BS[:], BS[:], PRS[:].unsqueeze(2).to_broadcast([P, 8, 16]), ALU.subtract)\
                    .then_inc(sem("best_shift"), 1)
                link(dve.tensor_scalar(PA[:, 0], BP[:], 4, None, ALU.logical_shift_right))
                link(dve.tensor_scalar(PA[:, 1], BP[:], 15, None, ALU.bitwise_and))
                link(dve.tensor_copy(PAF[:], PA[:]))
                eq = EQ[:].rearrange("p h (k a) -> p h k a", k=16)
                if t:
                    dve.wait_ge(sem("turned"), turns1 + t)
                for i in range(2):
                    link(dve.tensor_tensor(eq, PAF[:, i].unsqueeze(3).to_broadcast(square4),
                                           IOTA[:, 0:16].unsqueeze(1).unsqueeze(1).to_broadcast(square4),
                                           ALU.is_equal))
                    link(dve.tensor_tensor(eq, eq, topf[:, :, i, :].unsqueeze(2).to_broadcast(square4), ALU.mult))
                    link(dve.tensor_reduce(IJG[:, i, :].rearrange("p (h k) -> p h k", h=8), eq, AX_X, ALU.add))
                dve.wait_ge(sem("best_exp"), t + 1)
                link(dve.tensor_reduce(PSUMS[:], BS[:], AX_X, ALU.add))
                link(dve.reciprocal(PRS[:], PSUMS[:]))
                dve.tensor_tensor(IJG[:, 2, :].rearrange("p (h k) -> p h k", h=8), BS[:],
                                  PRS[:].unsqueeze(2).to_broadcast([P, 8, 16]), ALU.mult)\
                    .then_inc(sem("best_ready"), 1)
            dve.wait_ge(sem("turned"), turns1 + TT)

            def hot(token, u):
                dve.tensor_scalar(OI[:, u, :], IOTA[:], IJGT[:, 0, token], None, ALU.is_equal)
                ins = dve.tensor_scalar(OJ[:, u, :], IOTA[:], IJGT[:, 1, token], IJGT[:, 2, token],
                                        ALU.is_equal, ALU.mult)
                if u % 4 == 3:
                    ins.then_inc(sem("hot_ready"), 1)

            def hot_turn(i):
                for u in range(64):
                    if u % 4 == 0:
                        wait(dve, sem("gates_done"), 16 * i + u // 4 - 1)
                    hot(slice(u, u + 1) if isinstance(i, int) else bass.ds(64 * i + u, 1), u % 8)

            hot_turn(0)
            with dve.Fori(1, GATE_TURNS) as i:
                hot_turn(i)
            st.skip(8 * AHEAD, 8 * AHEAD)

            link(dve.memset(ACC[:], 0.0))
            s0, b0, freed0 = st.step, st.block, n["freed"]

            def ahead_piece(g, buffers, u):
                if u == 0:
                    dve.wait_ge(sem("gates_loaded"), 16 * (SHARED + 1) + 16 * g)
                    dve.wait_ge(sem("ahead_loaded"), 16 * g + 16)
                k = 8 * SHARED + 8 * g + u + 1
                dve.tensor_tensor(WF[:, u % 2, :].rearrange("p (b t) -> p b t", t=16),
                                  GU[:, u, :].rearrange("p (b t) -> p b t", t=16),
                                  GG[:, :, u, :], ALU.mult).then_inc(sem("gates_used"), 1)
                dve.wait_ge(sem("gates_used"), k)
                dve.tensor_copy(buffers[0][:, u, :], WF[:, u % 2, :]).then_inc(sem("ahead_high"), 1)
                dve.wait_ge(sem("ahead_high"), 8 * g + u + 1)
                dve.tensor_tensor(buffers[1][:, u, :], WF[:, u % 2, :], buffers[0][:, u, :].bitcast(F32),
                                  ALU.subtract).then_inc(sem("expert_ready"), 1)

            def add(c, steps):
                dve.wait_ge(sem("pe_steps"), steps)
                dve.tensor_tensor(ACC[:, c, :], ACC[:, c, :], BANK[(b0 + c) % 4][:], ALU.add)\
                    .then_inc(sem("block_free"), 1)

            def experts(g, ahead=False):
                dve.wait_ge(sem("gates_loaded"), 16 * g + 16)
                for u in range(8):
                    dve.wait_ge(sem("gelu_ready"), 8 * g + u + 1)
                    k = 8 * g + u + 1
                    dve.tensor_tensor(WF[:, u % 2, :].rearrange("p (b t) -> p b t", t=16),
                                      GE[:, u % 2, :].rearrange("p (b t) -> p b t", t=16),
                                      GG[:, :, u, :], ALU.mult).then_inc(sem("gates_used"), 1)
                    dve.wait_ge(sem("gates_used"), k)
                    dve.tensor_copy(WH[:, u, :], WF[:, u % 2, :]).then_inc(sem("block_free"), 1)
                    dve.wait_ge(sem("block_free"), freed0 + 8 * g + k)
                    dve.tensor_tensor(WL[:, u, :], WF[:, u % 2, :], WH[:, u, :].bitcast(F32), ALU.subtract)\
                        .then_inc(sem("expert_ready"), 1)
                for c in range(8):
                    if ahead and c < 4:
                        for u in range(2):
                            ahead_piece(0, (WH2, WL2), 2 * c + u)
                    add(c, s0 + UNIT * 8 + UNIT * (c + 1) + 16 * UNIT * g)

            with dve.Fori(0, SHARED - 1) as g:
                experts(g)
            experts(SHARED - 1, True)
            s1 = s0 + 16 * UNIT * SHARED

            def out_group(shift, j):
                for c in range(8):
                    if c < 4:
                        for u in range(2):
                            ahead_piece(shift + j + 1, (WH, WL) if j == 0 else (WH2, WL2), 2 * c + u)
                    add(c, s1 + UNIT * (c + 1) + 8 * UNIT * (shift + j))

            with dve.Fori(0, AHEAD // 2) as i:
                for j in range(2):
                    out_group(2 * i, j)
            for c in range(8):
                add(c, s1 + UNIT * (c + 1) + 8 * UNIT * (AHEAD - 1))
            dve.wait_ge(sem("block_free"), freed0 + 16 * SHARED + 8 * AHEAD)
            for c in range(DC):
                dve.scalar_tensor_tensor(HT[:, c, :], ACC[:, c, :], MOD[:, 40 + c, 0:1], HT[:, c, :],
                                         ALU.mult, ALU.add).then_inc(sem("out_ready"), 1)


def columns(v):
    v = np.asarray(v).reshape(-1)
    return v.reshape(-1, P).T


def feature_major(m):
    t = np.asarray(m).T
    return np.ascontiguousarray(t.reshape(-1, P, t.shape[1]).transpose(1, 0, 2))


def weight_blocks(w, column0=0, count=None):
    w = np.asarray(w)
    k = w.shape[0] // P
    w = w.reshape(k, P, -1, P).transpose(2, 0, 1, 3)
    first = column0 // P
    return w[first:] if count is None else w[first:first + count]


def as_units(blocks):
    b = np.concatenate([np.asarray(x).reshape(-1, P, P) for x in blocks])
    return np.ascontiguousarray(b.reshape(-1, UNIT, P, P).transpose(0, 2, 1, 3)).reshape(-1, P, UNIT * P)


def shape_constants():
    f = np.float32
    c = {"ones": np.ones((P, P), f), "ident": np.eye(P, dtype=f)}
    c["pair"] = np.kron(np.eye(2), np.ones((64, 64))).astype(f)
    s, col = np.arange(P)[:, None] % CH, np.arange(CH)[None, :]
    c["tri"] = np.repeat((s <= col).astype(np.uint32)[:, None, :], 4, axis=1)
    d = np.arange(P)[:, None] - np.arange(TOK)[None, :] + (TOK - P)
    bias = np.zeros((HEADS, P, 3, TOK), f)
    for g, (window, dil) in enumerate(((128, 1), (512, 4), (2048, 16))):
        valid = (d >= 0) & (d % dil == 0) & (d <= window)
        for h in range(HEADS):
            slope = f(2.0 ** (-8.0 * (g * HEADS + h + 1) / 12.0))
            bias[h, :, g] = np.where(valid, -slope * d.astype(f), f(MASKED))
    c["dil_bias"] = bias
    pos = np.arange(TOK)
    e = np.arange(P) % 64
    inv = (10000.0 ** (-np.arange(16, dtype=f) / f(16))).astype(f)
    where = np.where(e[:, None] < 32, (pos // 64)[None, :], (pos % 64)[None, :]).astype(f)
    angle = (where * inv[e % 16][:, None]).astype(f).astype(np.float64)
    c["cos"] = np.cos(angle).astype(f)
    c["sin"] = (np.sin(angle) * np.where(e % 32 < 16, -1.0, 1.0)[:, None]).astype(f)
    swap = np.zeros((P, P), f)
    swap[np.arange(P) ^ 16, np.arange(P)] = 1.0
    c["swap"] = swap
    q, k = np.arange(P)[:, None] % 64, np.arange(64)[None, :]
    start = np.clip(q - 8, 0, 48)
    c["cmask"] = np.where((k >= start) & (k < start + 16), 0.0, MASKED).astype(f)
    c["iota"] = np.repeat(np.arange(P, dtype=f)[None, :], P, axis=0)
    t = np.linspace(0.0, 1.0, TOK, dtype=f)
    w = (f(2.0 * np.pi / TOK) * np.arange(TOK, dtype=f)).astype(f)
    bands = np.linspace(1e-4, 15.0, 16, dtype=f)
    arg = (bands[:, None] * w[None, :]).astype(f).astype(np.float64)
    c["feats"] = np.concatenate([t[None, :], np.cos(arg), -np.sin(arg)]).astype(f)
    deltas = np.abs(np.linspace(np.log(1e-2) / 1.5, np.log(1e-2) / 0.3, 512, dtype=f))
    decay = np.exp(-(t[:, None] * deltas[None, :]).astype(np.float64)).astype(f)
    c["decay"] = np.ascontiguousarray(decay.reshape(TT, P, TOK).transpose(1, 0, 2))
    i = np.arange(TOK)
    theta = 2.0 * np.pi * ((i[:, None] * i[None, :]) % 1024) / 1024.0
    cos, sin = np.cos(theta), -np.sin(theta)
    flips = np.where(i % 2, -1.0, 1.0)
    cos_n, sin_n = cos.copy(), sin.copy()
    cos_n[:, 0], sin_n[:, 0] = flips, flips
    weight = np.where(i == 0, 1.0, 2.0)[:, None] / 1024.0
    inv_cos, inv_sin = cos * weight, sin * weight
    inv_sin[0] = flips / 1024.0
    blk = lambda m: weight_blocks(m.astype(f))
    bc, bcn, bs, bsn = blk(cos), blk(cos_n), blk(sin), blk(sin_n)
    one = [bc, bcn[0:1], bs]
    c["w_hyk"] = as_units(one + one)
    forward = [x[m] for m in range(4) for x in (bc, bsn)]
    ic, is_ = blk(inv_cos), blk(inv_sin)
    inverse = [x[m, k] for m in range(4) for k in range(4) for x in (ic, is_)]
    c["w_hyc"] = as_units((forward + inverse) * 2)
    return c


def lay_out(v):
    a = shape_constants()
    one = lambda name: v[name][0]
    a["x"] = feature_major(v["x"][0])
    a["mem"] = feature_major(v["mem"][0])
    a["ctx"] = feature_major(v["ctx_2"][0])
    parts = {
        "ffn1_pre": v["ffn1_pre_w"], "ffn1_post": v["ffn1_post_w"], "mix_pre": v["mix_pre_w"],
        "mem_norm": v["mem_norm_w"], "mix_post": v["mix_post_w"], "ffn2_pre": v["ffn2_pre_w"],
        "ffn2_post": v["ffn2_post_w"], "norm1": v["norm1_g_2"], "norm2": v["norm2_g_2"],
        "b_gate": v["b_gate"], "lb0": v["hg_lb_logits"][0], "lb1": v["hg_lb_logits"][1],
        "hgn": v["hg_norm_w"], "b_in2": v["b_in_2"], "cw0": v["hy_conv_w_2"][0, 0],
        "cw1": v["hy_conv_w_2"][0, 1], "cw2": v["hy_conv_w_2"][0, 2], "cb": v["hy_conv_b_2"],
        "qg": np.tile(v["q_norm_g_2"][0], 2), "kg": np.tile(v["k_norm_g_2"][0], 2),
        "b_ada": v["b_ada_2"],
    }
    cond = np.stack([columns(v["c_2"][0]), columns(v["c_ctx_2"])], axis=2).reshape(P, 16)
    fold = np.tile(np.eye(2, dtype=np.float32), (P // 2, 1))
    wide = {"cond": cond, "fold": fold}
    a["vecs"] = np.ascontiguousarray(np.concatenate(
        [wide[name] if name in wide else columns(parts[name]) for name, _ in VECS], axis=1))

    def ffn(k):
        gu = weight_blocks(one(f"ffn{k}_w_gu"))
        a[f"w_ffn{k}_gu"] = as_units([gu[m + half] for m in range(FC) for half in (0, FC)])
        a[f"w_ffn{k}_down"] = as_units([weight_blocks(one(f"ffn{k}_w_down"))])

    ffn(1)
    ffn(2)
    w_in = weight_blocks(one("w_in"))
    ada = one("w_ada_2").reshape(4, 2, P, 12, TOK).transpose(3, 0, 2, 1, 4).reshape(48, P, UNIT * P)
    a["w_ada0"] = np.ascontiguousarray(ada[0:4])
    a["w_ffn1_gu"] = np.stack([a["w_ffn1_gu"], ada[4:]], axis=1).reshape(4 * FC, P, UNIT * P)
    a["w_memkv"] = as_units([weight_blocks(one("w_mem_kv"))])
    a["w_hg"] = as_units([w_in[0:16]])
    a["w_dil"] = as_units([w_in[16 + 12 * g + 4 * part + h] for h in range(HEADS) for part in range(3)
                           for g in range(3)])
    a["w_mq"] = as_units([w_in[52:56]])
    br = [weight_blocks(one(k)) for k in ("w_br_hg", "w_br_dil", "w_br_mem")]
    merge = []
    for m in range(0, DC, 2):
        merge += [w_in[56 + 8 * b + m + i] for i in range(2) for b in range(3)]
        merge += [br[b][m + i] for i in range(2) for b in range(3)]
    a["w_merge1"] = as_units(merge)
    a["w_wout1"] = as_units([weight_blocks(one("w_out"))])
    w2 = weight_blocks(one("w_in_2"))
    a["w_ctxkv"] = as_units([w2[16:24]])
    a["w_hyz"] = as_units([w2[0:12]])
    a["w_naqkv"] = as_units([w2[12:24]])
    hy, na = weight_blocks(one("w_hy_out_2")), weight_blocks(one("w_na_out_2"))
    a["w_merge2"] = as_units([x for m in range(DC) for x in (w2[24 + m], w2[32 + m], hy[m], na[m])])
    a["w_wout2"] = as_units([weight_blocks(one("w_out_2"))])
    a["w_wq"] = as_units([weight_blocks(one("peer_w_q_2"))])
    u = one("peer_u_2").reshape(P, EXP_GROUPS, 8, DC, P).transpose(1, 2, 4, 3, 0)
    w = one("peer_v_2").reshape(P, EXP_GROUPS, 8, DC, P).transpose(1, 3, 0, 2, 4)
    u, w = (m.reshape(EXP_GROUPS, 8, P, UNIT * P) for m in (u, w))
    a["w_peer_ahead"] = np.ascontiguousarray(u[SHARED:]).reshape(8 * AHEAD, P, UNIT * P)
    a["w_peer"] = np.concatenate([u[:SHARED], w[:SHARED]], axis=1).reshape(16 * SHARED, P, UNIT * P)
    a["w_peer_out"] = np.ascontiguousarray(w[SHARED:]).reshape(8 * AHEAD, P, UNIT * P)
    a["keys"] = np.ascontiguousarray(one("peer_keys_2").reshape(16, P, P).transpose(2, 0, 1))
    a["f1"] = one("hy_f1_w_2")
    a["f23"] = np.ascontiguousarray(np.stack([one("hy_f2_w_2"), one("hy_f3_w_2")], axis=1))
    a["f4"] = one("hy_f4_w_2")
    fv = [one(k) for k in ("hy_f1_b_2", "hy_f2_b_2", "hy_f3_b_2", "hy_sin_freq_2")]
    a["fvec"] = np.ascontiguousarray(np.stack(fv + fv, axis=1))
    a["skip"] = v["hy_skip_2"].reshape(1, 2, TOK)
    dc = np.clip(np.arange(64)[None, :] - np.arange(64)[:, None], -15, 15) + 15
    rpb = one("na_rpb_2")
    table = np.stack([rpb[:, 1 - e:15 - e][:, :, dc] for e in range(2)], axis=1)
    a["na_bias"] = np.ascontiguousarray(table.transpose(0, 1, 3, 2, 4)).reshape(NAH, P, 14 * 64)
    return a


def kernel(**inputs):
    import concourse.bacc as bacc
    from concourse.bass_utils import run_bass_kernel_spmd

    a = lay_out({k: np.asarray(v) for k, v in inputs.items()})
    nc = bacc.Bacc("TRN2", target_bir_lowering=False, num_devices=1)
    aps = {k: nc.dram_tensor(f"in_{k}", x.shape, mybir.dt.from_np(x.dtype), kind="ExternalInput").ap()
           for k, x in a.items()}
    aps["out"] = nc.dram_tensor("out_x", (P, DC, TOK), F32, kind="ExternalOutput").ap()
    program(nc, aps)
    r = run_bass_kernel_spmd(nc, [{f"in_{k}": np.ascontiguousarray(x) for k, x in a.items()}], core_ids=[0])
    out = r.results[0]["out_x"]
    return np.ascontiguousarray(out.transpose(2, 1, 0)).reshape(1, TOK, D)
```

```python
from contextlib import ExitStack

import numpy as np

import concourse.bass as bass
from concourse import mybir

F32 = mybir.dt.float32
F32R = mybir.dt.float32r
U32 = mybir.dt.uint32
ALU = mybir.AluOpType
ACT = mybir.ActivationFunctionType
AX_X = mybir.AxisListType.X

P = 128
TOK = 512
TT = TOK // P
D = 1024
DC = D // P
EPS = 1e-6
FF = 2816
FC = FF // P
NMEM = 256
HEADS = 4
CH = 64
NCH = TOK // CH
HYC = 4
FB = 8
KB = 9
NAH = 8
TOPK = 16
EXP_GROUPS = 16
AHEAD = 9
BY_TILE = 10
BY_TURN = 4
SHARED = EXP_GROUPS - AHEAD
GATE_TURNS = 8
assert 8 * AHEAD == BY_TILE * TT + BY_TURN * GATE_TURNS
UNIT = 8
RING = 4
BIG = 3.0e38
MASKED = -1.0e30

PARTS = [
    ("ada0", 4), ("ffn1_gu", 4 * FC), ("ffn1_down", DC * FC // UNIT),
    ("hg", 24), ("dil", 44), ("mq", 4), ("memkv", 8), ("gate1", 8), ("merge1", 12), ("wout1", 8),
    ("ffn2_gu", 2 * FC), ("ffn2_down", DC * FC // UNIT),
    ("ctxkv", 8), ("hyk", KB), ("hyz", 12), ("hyc", 16), ("naqkv", 12), ("gate2", 16), ("merge2", 8),
    ("wout2", 8), ("wq", 16),
    ("peer_ahead", 8 * AHEAD), ("peer", 16 * (EXP_GROUPS - AHEAD)), ("peer_out", 8 * AHEAD),
]
START = {}
_n = 0
for _name, _count in PARTS:
    START[_name] = _n
    _n += _count
TOTAL = _n

VECS = [
    ("ffn1_pre", 8), ("ffn1_post", 8), ("mix_pre", 8), ("mem_norm", 8), ("mix_post", 8),
    ("ffn2_pre", 8), ("ffn2_post", 8), ("norm1", 8), ("norm2", 8), ("b_gate", 24),
    ("lb0", 4), ("lb1", 4), ("hgn", 1), ("b_in2", 40), ("cw0", 12), ("cw1", 12), ("cw2", 12),
    ("cb", 12), ("qg", 1), ("kg", 1), ("b_ada", 48), ("cond", 16), ("fold", 2),
]
VCOL = {}
_n = 0
for _name, _count in VECS:
    VCOL[_name] = _n
    _n += _count
NVEC = _n


def attention_steps(kind):
    steps = []
    for h in range(NAH if kind == "na" else HEADS):
        for t in range(TT):
            if kind == "dil":
                ranges = [(max(0, P * (t - 1)), P * (t + 1)), (0, P * (t + 1)), (0, P * (t + 1))]
            elif kind == "mem":
                ranges = [(0, NMEM)]
            else:
                ranges = [(0, TOK), (0, NMEM)]
            steps.append((h, t, ranges))
    return steps


def gate_parts(kind):
    return 4 if kind == "na" else 2


class Stepper:

    def __init__(self):
        self.step = 0
        self.told = 0
        self.block = 0
        self.units = 0

    def steps_(self, v):
        return v + UNIT * self.units if not isinstance(self.units, int) else v

    def units_(self, v):
        return v + self.units if not isinstance(self.units, int) else v

    def skip(self, units, blocks):
        self.step += UNIT * units
        self.told = self.step
        self.block += blocks
        self.units = 0


def wait(engine, sem, value):
    if not isinstance(value, int) or value > 0:
        engine.wait_ge(sem, value)


class Link:

    def __init__(self, engine, sem):
        self.engine, self.sem, self.n, self.turn = engine, sem, 0, 0

    def __call__(self, ins):
        self.n += 1
        ins.then_inc(self.sem, 1)
        self.engine.wait_ge(self.sem, self.n + self.turn if not isinstance(self.turn, int) else self.n)


def program(nc, a):
    with ExitStack() as ctx:
        cache = {}

        def sem(name):
            if name not in cache:
                cache[name] = ctx.enter_context(nc.semaphore(name))
            return cache[name]

        base = -(-nc.sbuf_base // 64) * 64
        fixed = [base]

        def place(name, shape, dt=F32, at=None):
            size = 4 * int(np.prod(shape[1:]))
            if at is None:
                at = fixed[0]
                fixed[0] += -(-size // 32) * 32
            return nc.alloc_sbuf_tensor_at(name, shape, dt, offset=at)

        HT = place("residual", [P, DC, TOK])
        RAW = place("weights_raw", [P, RING, UNIT * P])
        HI = place("weights_hi", [P, RING, UNIT * P], F32R)
        LO = place("weights_lo", [P, RING, UNIT * P], F32R)
        x_at = fixed[0]
        XH = place("operand_hi", [P, DC, TOK], F32R)
        XL = place("operand_lo", [P, DC, TOK], F32R)
        ONES = place("ones", [P, P])
        PAIR = place("pair_ones", [P, P])
        IDENT = place("identity", [P, P])
        VEC = place("vectors", [P, NVEC])
        SQ = place("squares", [P, 2, TOK])
        MS = place("mean_square", [P, TOK])
        AR = place("ada_rows", [4, TOK], F32, fixed[0])
        RT = place("root", [P, TOK])
        RSTD = place("reciprocal_root", [P, TOK])
        LB = place("lower_bound", [P, 6, 4])
        MOD = place("modulation", [P, 48, 2])
        COEF = place("modulation_gain", [P, 3, DC])
        CS = place("cond_silu", [P, DC, 2])
        CP = place("cond_parts", [P, DC, 4], F32R)
        NMX = place("negated_max", [P, 2])
        SUM = place("exp_sum", [P, 2])
        RSUM = place("exp_sum_reciprocal", [P, 2])
        A0 = fixed[0]
        END = 229344
        Y2 = END - 32768
        Y3 = END - 49152
        assert END - A0 >= 98304, END - A0

        KBYTE = 1024
        FH = place("hidden_hi", [P, FC, TOK], F32R, A0)
        FL = place("hidden_lo", [P, FC, TOK], F32R, A0 + FC * 2048)
        SG = place("gate_silu", [P, 2, TOK], F32, A0 + FC * 4096)
        HF = place("hidden", [P, 2, TOK], F32, A0 + FC * 4096 + 4096)
        YT = place("branch_out", [P, DC, TOK], F32, x_at)
        XF = place("operand", [P, DC, TOK], F32, A0)

        ZQ, ZF, ZI, ZOG, KF, K2, B0, B1, Q1, K1, Q2, VT = [
            place(n, [P, HEADS, TOK], F32, A0 + i * 8192)
            for i, n in enumerate(["hg_q", "hg_f", "hg_i", "hg_og", "hg_k", "hg_k2", "hg_b0", "hg_b1",
                                   "hg_q1", "hg_k1", "hg_q2", "hg_v"])]
        K2T = place("hg_k2t", [P, HEADS, TOK], F32, A0 + 8192)
        SC = place("hg_scores", [P, HEADS, TT, P], F32, A0 + 2 * 8192)
        TRI = place("hg_causal", [P, 4, CH], U32, A0 + 12 * 8192 + 128)
        assert A0 + 12 * 8192 + 1152 <= END
        STATE = place("hg_state", [P, NCH, HEADS, P], F32, A0 + 6 * 8192)
        DEC = place("hg_decay", [P, HEADS * NCH], F32, A0 + 12 * 8192)
        OF = place("hg_out", [P, HEADS, TOK], F32, A0)
        YH = [place(f"branch{i}_hi", [P, 4, TOK], F32R, Y3 + i * 16384) for i in range(3)]
        YL = [place(f"branch{i}_lo", [P, 4, TOK], F32R, Y3 + i * 16384 + 8192) for i in range(3)]
        DZ = place("dil_qkv", [P, 9, TOK], F32, A0)
        DV = place("dil_v", [P, 3, TT, P], F32, A0 + 18432)
        DB = place("dil_bias", [P, 3, TOK], F32, A0 + 24576)
        DS = place("att_scores", [P, 2, 3 * TOK], F32, A0 + 30720)
        DP = place("att_probs_t", [P, 2, 4 * P], F32, A0 + 43008)
        DO = place("att_out", [P, HEADS, TOK], F32, Y3 + 2 * 16384)
        MT = place("memory", [P, DC, NMEM], F32, A0)
        MF = place("memory_operand", [P, DC, NMEM], F32, A0 + 8192)
        MH = place("memory_hi", [P, DC, NMEM], F32R, A0 + 16384)
        ML = place("memory_lo", [P, DC, NMEM], F32R, A0 + 24576)
        MKV = place("memory_kv", [P, 8, NMEM], F32, A0)
        MQ = place("memory_q", [P, 4, TOK], F32, END - 8192)
        MV = place("memory_v", [P, HEADS, 2, P], F32, A0 + 16384)
        MO = place("memory_out", [P, HEADS, TOK], F32, A0 + 20480)
        MG = place("merge_gates", [P, 2, 6, TOK], F32, A0)
        MP = place("merge_products", [P, 3, TOK], F32, A0 + 24576)
        MY = place("merged", [P, DC, TOK], F32, A0 + 30720)
        assert A0 + 30720 + 16384 <= Y3
        CT = place("context", [P, DC, NMEM], F32, x_at + 16384)
        CXL = place("context_lo", [P, DC, NMEM], F32R, x_at + 16384)
        CXH = place("context_hi", [P, DC, NMEM], F32R, x_at + 24576)
        CVF = place("context_vt", [P, 4, NMEM], F32, A0 + 32768)
        CK = place("context_k", [P, 4, NMEM], F32, END - 8192)
        CV = place("context_v", [P, 2, TOK], F32, END - 4096)
        KHAT = place("filter_dft", [P, 2, KB, TOK], F32, A0)
        W1 = A0 + 2 * KB * 2048
        FX = place("f_hidden", [64, TOK], F32, W1)
        FW4 = place("f4", [64, 2048], F32, W1 + 2048)
        FVEC = place("f_vectors", [64, 8], F32, W1 + 10240)
        FFW = place("filter_forward", [P, TT, TOK], F32, W1 + 10304)
        FBW = place("filter_backward", [P, TT, TOK], F32, W1 + 18496)
        FE = place("filter_even", [P, TT, TOK], F32, W1 + 26688)
        FAB = place("filter_abs", [P, 2, TOK], F32, W1 + 34880)
        DCY = place("filter_decay", [P, TT, TOK], F32, W1 + 38976)
        SKIP = place("hy_skip", [1, 2, TOK], F32, W1 + 47168)
        FTS = place("positions", [33, TOK], F32, W1 + 26688)
        FW1 = place("f1", [33, 64], F32, W1 + 28736)
        FW = place("f23", [64, 2, 64], F32, W1 + 28992)
        FA = place("f_argument", [64, 3, TOK], F32, W1 + 10304)
        assert W1 + 47168 + 4096 <= END - 8192
        EOH = place("filter_hi", [P, 8, TOK], F32R, x_at)
        EOL = place("filter_lo", [P, 8, TOK], F32R, x_at + 16384)
        HZ = place("hy_z", [P, 12, TOK], F32, W1)
        HCV = place("hy_conv", [P, 2, TOK], F32, W1 + 24576)
        HTM = place("hy_token_major", [P, 3, TT, TOK], F32, W1 + 28672)
        XF2 = place("operand_2", [P, DC, TOK], F32, W1)
        SH = place("signal_hi", [P, TT, TOK], F32R, W1)
        SL = place("signal_lo", [P, TT, TOK], F32R, W1 + 8192)
        HY = place("hy_out", [P, HYC, TOK], F32, W1 + 16384)
        SPH = place("spectrum_hi", [P, FB, TOK], F32R, x_at)
        SPL = place("spectrum_lo", [P, FB, TOK], F32R, x_at + 16384)
        Y2H = [place(f"second{i}_hi", [P, 4, TOK], F32R, Y2 + i * 16384) for i in range(2)]
        Y2L = [place(f"second{i}_lo", [P, 4, TOK], F32R, Y2 + i * 16384 + 8192) for i in range(2)]
        assert W1 + 53248 <= END - 8192
        NZ = place("na_qkv", [P, 12, TOK], F32, A0)
        NV = place("na_v", [P, TT, TOK], F32, A0 + 24576)
        COS = place("rope_cos", [P, TOK], F32, A0 + 32768)
        SIN = place("rope_sin", [P, TOK], F32, A0 + 34816)
        SWAP = place("rope_swap", [P, P], F32, A0 + 36864)
        CMASK = place("column_mask", [P, 64], F32, A0 + 37376)
        NB = place("na_bias", [P, 2, 14 * 64], F32, A0 + 37632)
        NS = place("na_scores", [P, 2, TOK + NMEM], F32, A0 + 44800)
        NP = place("na_probs_t", [P, 2, 4 * P], F32, A0 + 50944)
        NO = place("na_out", [P, HYC, TOK], F32, A0 + 55040)
        RP = place("rope_products", [P, 2, TOK], F32, A0 + 55040)
        GST = place("gate_store", [P, 2, TOK], F32, A0 + 59136)
        assert A0 + 63232 <= Y2
        QT = place("peer_q", [P, 16, TOK], F32, A0)
        KEYS = place("peer_keys", [P, 16, P], F32, A0 + 32768)
        PS = place("peer_scores", [P, 16, P], F32, A0 + 40960)
        PR = place("peer_scores_rest", [P, 16, P], F32, A0 + 49152)
        CA = place("candidates", [P, 8, 256], F32, A0 + 57344)
        CR = place("candidates_rest", [P, 8, 256], F32, A0 + 65536)
        EQ = place("matches", [P, 8, 256], F32, A0 + 73728)
        s0 = A0 + 81920
        TOPS = place("top_scores", [P, 16, 16], F32, s0)
        TOPI = place("top_index", [P, 16, 16], U32, s0 + 1024)
        TOPF = place("top_index_f", [P, 16, 16], F32, s0 + 2048)
        BS = place("best_scores", [P, 8, 16], F32, s0 + 3072)
        BP = place("best_position", [P, 8, 16], U32, s0 + 3584)
        PA = place("position_parts", [P, 2, 8, 16], U32, s0 + 4096)
        PAF = place("position_parts_f", [P, 2, 8, 16], F32, s0 + 5120)
        IJG = place("expert_ijg", [P, 3, P], F32, s0 + 6144)
        IJGT = place("expert_ijg_t", [P, 3, TOK], F32, s0 + 7680)
        IOTA = place("iota", [P, P], F32, s0 + 13824)
        PSUMS = place("peer_sums", [P, 8], F32, s0 + 14336)
        PRS = place("peer_sums_reciprocal", [P, 8], F32, s0 + 14400)
        assert s0 + 14464 <= END
        OI = place("one_hot_i", [P, 8, P], F32, A0)
        OJ = place("one_hot_j", [P, 8, P], F32, A0 + 4096)
        STG = place("gate_stage", [P, 2, P, 16], F32, A0 + 8192)
        WH = place("expert_hi", [P, 8, TOK], F32R, A0)
        WL = place("expert_lo", [P, 8, TOK], F32R, A0 + 16384)
        ACC = place("peer_sum", [P, DC, TOK], F32, A0 + 32768)
        GG = place("expert_gates", [P, 32, 8, 16], F32, A0 + 49152)
        GE = place("expert_gelu", [P, 2, TOK], F32, A0 + 65536)
        WF = place("expert_act", [P, 2, TOK], F32, A0 + 69632)
        GU = place("expert_gelu_ahead", [P, 8, TOK], F32, A0 + 73728)
        WH2 = place("expert_hi_2", [P, 8, TOK], F32R, x_at)
        WL2 = place("expert_lo_2", [P, 8, TOK], F32R, x_at + 16384)
        assert 73728 + 16384 <= END - A0

        GD = nc.dram_tensor("peer_gates", [32, P, P, 16], F32, kind="Internal").ap()
        G1 = nc.dram_tensor("merge_gates_1", [3 * DC, P, TOK], F32, kind="Internal").ap()
        G2 = nc.dram_tensor("merge_gates_2", [2 * DC, P, TOK], F32, kind="Internal").ap()
        UD = nc.dram_tensor("peer_gelu_ahead", [8 * AHEAD, P, TOK], F32, kind="Internal").ap()

        BANK = [ctx.enter_context(nc.psum_tensor(f"bank{i}", [P, TOK], F32)) for i in range(8)]
        SCB = [BANK[5], BANK[6]]
        TRB = [BANK[4], BANK[7]]
        OB = [BANK[2], BANK[3]]
        STB = BANK[4]

        def vec(name, c=0):
            return VEC[:, VCOL[name] + c:VCOL[name] + c + 1]

        branches_ready = []

        block = ctx.enter_context(nc.Block())

        @block.sync
        def _(sp):
            sp.dma_start(VEC[:], a["vecs"]).then_inc(sem("vec_loaded"), 16)
            for n, (dst, src) in enumerate([(ONES, "ones"), (PAIR, "pair"), (IDENT, "ident")]):
                sp.dma_start(dst[:], a[src]).then_inc(sem("const_loaded"), 16)
            for c in range(DC):
                sp.dma_start(HT[:, c, :], a["x"][:, c, :]).then_inc(sem(f"x_loaded{c}"), 16)

            def unit(src, n, slot):
                wait(sp, sem("lo_ready"), n - RING + 1)
                sp.dma_start(RAW[:, slot, :], src).then_inc(sem(f"raw_loaded{slot}"), 16)

            def part(name, first=0, count=None):
                n0, src = START[name] + first, a["w_" + name]
                count = (dict(PARTS)[name] if count is None else count)
                done = 0
                while count - done >= 8 and n0 + done < RING:
                    unit(src[first + done], n0 + done, (n0 + done) % RING)
                    done += 1
                turns = (count - done) // RING
                if turns > 1:
                    with sp.Fori(0, turns) as i:
                        for u in range(RING):
                            n = n0 + done + u
                            unit(src[first + done + u + RING * i], n + RING * i, n % RING)
                    done += turns * RING
                while done < count:
                    unit(src[first + done], n0 + done, (n0 + done) % RING)
                    done += 1

            for name, _ in PARTS[:-3]:
                part(name)
            ahead, n0 = a["w_peer_ahead"], START["peer_ahead"]
            part("peer_ahead", 0, BY_TILE * TT + RING)

            def ahead_unit(j, shift=0):
                k = BY_TILE * TT + RING + j
                unit(a["w_peer"][k - 8 * AHEAD] if isinstance(shift, int) and k + shift >= 8 * AHEAD
                     else ahead[k + shift], n0 + k + shift, (n0 + k) % RING)

            def store_stage(i, r):
                s = r % 2
                sp.wait_ge(sem("stage_ready"), 16 * i + 4 * (r + 1))
                sp.dma_start(GD[4 * i + r].rearrange("i j t -> i (j t)"),
                             STG[:, s].rearrange("p j t -> p (j t)")).then_inc(sem(f"stage_stored{s}"), 16)

            with sp.Fori(0, GATE_TURNS - 1) as i:
                for r in range(4):
                    ahead_unit(r, BY_TURN * i)
                    store_stage(i, r)
            for r in range(4):
                ahead_unit(r + BY_TURN * (GATE_TURNS - 1))
                store_stage(GATE_TURNS - 1, r)
            for s in range(2):
                sp.wait_ge(sem(f"stage_stored{s}"), 256)
            gates = GD.rearrange("b i j t -> i b j t")
            sp.dma_start(GG[:], gates[:, :, 0:8, :]).then_inc(sem("gates_loaded"), 16)
            n0, src = START["peer"], a["w_peer"]
            part("peer", RING, 8)
            sp.wait_ge(sem("gates_used"), 8)
            sp.dma_start(GG[:], gates[:, :, 8:16, :]).then_inc(sem("gates_loaded"), 16)
            with sp.Fori(0, SHARED - 1) as g:
                for u in range(16):
                    n = n0 + 12 + u
                    unit(src[12 + u + 16 * g], n + 16 * g, n % RING)
                sp.wait_ge(sem("gates_used"), 8 * g + 16)
                sp.dma_start(GG[:], gates[:, :, bass.ds(8 * g + 16, 8), :]).then_inc(sem("gates_loaded"), 16)
            for s in range(2):
                sp.wait_ge(sem(f"ahead_stored{s}"), 16 * 4 * AHEAD)
            by_group = UD.rearrange("(g u) p t -> g p u t", u=8)
            sp.dma_start(GU[:], by_group[0]).then_inc(sem("ahead_loaded"), 16)
            part("peer", 12 + 16 * (SHARED - 1), 4)
            n0, src = START["peer_out"], a["w_peer_out"]
            with sp.Fori(0, AHEAD - 1) as g:
                for u in range(8):
                    if u == 2:
                        sp.wait_ge(sem("gates_used"), 8 * (SHARED + 1) + 8 * g)
                        sp.dma_start(GG[:], gates[:, :, bass.ds(8 * g + 8 * (SHARED + 1), 8), :])\
                            .then_inc(sem("gates_loaded"), 16)
                        sp.dma_start(GU[:], by_group[g + 1]).then_inc(sem("ahead_loaded"), 16)
                    unit(src[u + 8 * g], n0 + u + 8 * g, (n0 + u) % RING)
            part("peer_out", 8 * (AHEAD - 1), 8)
            for c in range(DC):
                sp.wait_ge(sem("out_ready"), c + 1)
                sp.dma_start(a["out"][:, c, :], HT[:, c, :]).then_inc(sem("out_stored"), 16)
            sp.wait_ge(sem("out_stored"), 16 * DC)

        @block.gpsimd
        def _(pool):
            def low(n, slot):
                wait(pool, sem("hi_ready"), n + 1)
                wait(pool, sem("pe_steps"), UNIT * (n - RING + 1))
                pool.tensor_tensor(LO[:, slot, :], RAW[:, slot, :], HI[:, slot, :].bitcast(F32),
                                   ALU.subtract).then_inc(sem("lo_ready"), 1)

            for n in range(RING):
                low(n, n)
            with pool.Fori(1, TOTAL // RING) as i:
                for u in range(RING):
                    low(RING * i + u, u)
            for n in range(TOTAL // RING * RING, TOTAL):
                low(n, n % RING)

        @block.tensor
        def _(pe):
            st = Stepper()
            owner = {}
            n = {"square": 0, "sum": 0, "turn": 0, "piece": 0, "prob": 0, "ov": 0, "gate": 0,
                 "freed": 0, "ag": 0, "small": 0, "beside": 0}

            def claim(b):
                if b in owner:
                    wait(pe, sem(owner[b][0]), owner[b][1])

            def block_(kc, hi, lo, width=TOK, gate=False, in_loop=False, piece=None, ready=None,
                       bank=None):
                b = st.block % 4 if bank is None else bank
                for k in range(kc) if piece is None else piece:
                    if ready:
                        ready(k)
                    if st.step % UNIT == 0:
                        pe.wait_ge(sem("lo_ready"), st.units_(st.step // UNIT + 1))
                    if k == 0 and not in_loop:
                        claim(b)
                    slot, col = (st.step // UNIT) % RING, st.step % UNIT
                    wh = HI[:, slot, col * P:(col + 1) * P]
                    wl = LO[:, slot, col * P:(col + 1) * P]
                    out = BANK[b][:, 0:width]
                    pe.matmul(out, wh, hi(k), start=(k == 0), stop=False)
                    pe.matmul(out, wh, lo(k), start=False, stop=False)
                    ins = pe.matmul(out, wl, hi(k), start=False, stop=(k == kc - 1))
                    st.step += 1
                    if st.step % UNIT == 0 or k == kc - 1:
                        ins.then_inc(sem("pe_steps"), st.step - st.told)
                        st.told = st.step
                if piece is not None and piece[-1] < kc - 1:
                    return
                if bank is None:
                    st.block += 1
                if gate:
                    n["gate"] += 1
                    owner[b] = ("gate_ready", n["gate"])
                elif not in_loop:
                    n["freed"] += 1
                    owner[b] = ("block_free", n["freed"])

            def x_ops():
                return (lambda k: XH[:, k, :]), (lambda k: XL[:, k, :])

            def operand(total):
                n["operand"] = n.get("operand", 0) + total
                pe.wait_ge(sem("operand_ready"), n["operand"])

            def pieces_of(total):
                base = n.get("operand", 0)
                n["operand"] = base + total
                return lambda k: pe.wait_ge(sem("operand_ready"), base + k + 1)

            def sums(pieces, matrix, width, first_wait=None):
                claim(4)
                for c in range(pieces):
                    pe.wait_ge(sem("square_ready"), n["square"] + 1)
                    pe.matmul(STB[:, 0:width], matrix[:], SQ[:, n["square"] % 2, 0:width],
                              start=(c == 0), stop=(c == pieces - 1)).then_inc(sem("square_used"), 1)
                    n["square"] += 1
                n["sum"] += 1
                owner[4] = ("sum_read", n["sum"])

            def sum_pair(matrix):
                claim(4)
                for j in range(2):
                    pe.wait_ge(sem("square_ready"), n["square"] + 1)
                    pe.matmul(STB[:, j * NMEM:(j + 1) * NMEM], matrix[:], SQ[:, n["square"] % 2, 0:NMEM],
                              start=True, stop=True).then_inc(sem("square_used"), 1)
                    n["square"] += 1
                n["sum"] += 1
                owner[4] = ("sum_read", n["sum"])

            def turn(sources):
                b = 4 if n["turn"] % 2 == 0 else 7
                claim(b)
                for i, src in enumerate(sources):
                    rows = src.shape[0]
                    ins = pe.transpose(BANK[b][0:src.shape[-1], i * P:i * P + rows], src, IDENT[0:rows, 0:rows])
                ins.then_inc(sem("turn_done"), 1)
                n["turn"] += 1
                owner[b] = ("turned", n["turn"])

            def ffn(name):
                ready = pieces_of(DC)
                hi, lo = x_ops()
                for b in range(4):
                    claim(b)
                freed = n["freed"]
                ada = name == "ffn1"
                per = 8 if ada else 4

                def two_pairs(i):
                    for u in range(4):
                        if u % 2 == 0:
                            wait(pe, sem("block_free"), freed + 4 * i + u - 2)
                        block_(DC, hi, lo, in_loop=True, ready=ready if isinstance(i, int) and u == 0 else None)
                        if ada:
                            if u == 0:
                                ada_fold(i)
                            ada_unit(u)

                two_pairs(0)
                turns = FC // 2
                with pe.Fori(1, turns) as i:
                    st.units = per * (i - 1)
                    two_pairs(i)
                st.units = 0
                st.skip(per * (turns - 2), 4 * (turns - 2))
                if ada:
                    ada_fold(turns)
                n["freed"] += 2 * FC
                for b in range(4):
                    owner[(st.block - 4 + b) % 4] = ("block_free", n["freed"])
                pe.wait_ge(sem("hidden_ready"), FC * (1 if name == "ffn1" else 2))
                for m in range(DC):
                    block_(FC, lambda k: FH[:, k, :], lambda k: FL[:, k, :])
                    if name == "ffn2" and m == 1:
                        sums(DC, ONES, NMEM)

            def gate_block(part=0, parts=1):
                size = DC // parts
                block_(DC, *x_ops(), gate=True, bank=n["beside"] % 2,
                       piece=range(part * size, part * size + size))
                if part == parts - 1:
                    n["beside"] += 1

            def ada_unit(u):
                pe.wait_ge(sem("lo_ready"), st.units_(st.step // UNIT + 1))
                slot = (st.step // UNIT) % RING
                for j in range(2):
                    k = 2 * u + j
                    w = slice(j * TOK, j * TOK + TOK)
                    pe.matmul(BANK[5][0:4, :], CP[:, k, :], HI[:, slot, w], start=(k == 0), stop=False)
                    ins = pe.matmul(BANK[5][0:4, :], CP[:, k, :], LO[:, slot, w], start=False, stop=(k == DC - 1))
                ins.then_inc(sem("pe_steps"), UNIT)
                st.step += UNIT
                st.told = st.step

            def ada_fold(g):
                pe.wait_ge(sem("ada_rows_ready"), g + 1)
                if not isinstance(g, int) or g:
                    pe.wait_ge(sem("ada_added"), g)
                for m in range(4):
                    ins = pe.matmul(BANK[6][:, 2 * m:2 * m + 2], AR[0:4, m * P:(m + 1) * P],
                                    VEC[0:4, VCOL["fold"]:VCOL["fold"] + 2], start=True, stop=True)
                ins.then_inc(sem("ada_folded"), 1)

            def attend(kind, h0=0, h1=None):
                steps = [s for s in attention_steps(kind) if h0 <= s[0] < (h1 or 99)]

                def scores(h, t, ranges):
                    for g, (k0, k1) in enumerate(ranges):
                        b = 5 + n["piece"] % 2
                        claim(b)
                        q0 = P * t
                        if kind == "dil":
                            lhs, rhs = DZ[:, g, q0:q0 + P], DZ[:, 3 + g, k0:k1]
                        elif kind == "mem":
                            lhs, rhs = MQ[:, h, q0:q0 + P], MKV[:, h, k0:k1]
                        else:
                            r0, c = 64 * (h % 2), h // 2
                            lhs = NZ[r0:r0 + 64, c, q0:q0 + P]
                            rhs = NZ[r0:r0 + 64, 4 + c, :] if g == 0 else CK[r0:r0 + 64, c, :]
                        pe.matmul(BANK[b][:, 0:k1 - k0], lhs, rhs, start=True, stop=True)\
                            .then_inc(sem("score_ready"), 1)
                        n["piece"] += 1
                        owner[b] = ("score_read", n["piece"])

                def values(step, h, t, ranges):
                    probs = (NS if kind == "na" else DS)[:, n["prob"] % 2]
                    n["prob"] += 1
                    pe.wait_ge(sem("prob_ready"), n["prob"])
                    cols, keys = 0, []
                    for g, (k0, k1) in enumerate(ranges):
                        for k in range(k0, k1, P):
                            if kind == "dil":
                                v = DV[:, g, k // P, :]
                            elif kind == "mem":
                                v = MV[:, h, k // P, :]
                            elif g == 0:
                                v = NV[:, k // P, 64 * h:64 * h + 64]
                            else:
                                v = CV[:, k // P, 64 * h:64 * h + 64]
                            keys.append((cols, v))
                            cols += P
                    b = 2 + n["ov"] % 2
                    claim(b)
                    r0, rows = (64 * (h % 2), 64) if kind == "na" else (0, P)
                    groups = [keys[i:i + 4] for i in range(0, len(keys), 4)]
                    base_ = n["turn"]
                    turn([probs[:, c:c + P] for c, _ in groups[0]])
                    for i, group in enumerate(groups):
                        if i + 1 < len(groups):
                            turn([probs[:, c:c + P] for c, _ in groups[i + 1]])
                        if i == 0:
                            gate_block(step % gate_parts(kind), gate_parts(kind))
                        pe.wait_ge(sem("turned"), base_ + i + 1)
                        for j, (_, v) in enumerate(group):
                            ins = pe.matmul(BANK[b][r0:r0 + rows, 0:P], v,
                                            (NP if kind == "na" else DP)[:, n["ag"] % 2, j * P:(j + 1) * P],
                                            start=(i == 0 and j == 0),
                                            stop=(i == len(groups) - 1 and j == len(group) - 1))
                        ins.then_inc(sem("group_used"), 1)
                        n["ag"] += 1
                    n["ov"] += 1
                    owner[b] = ("out_read", n["ov"])

                before = None
                for i, s in enumerate(steps):
                    scores(*s)
                    if before:
                        values(i - 1, *before)
                    before = s
                values(len(steps) - 1, *before)

            pe.wait_ge(sem("const_loaded"), 48)
            sums(DC, ONES, TOK)
            operand(1)
            for u in range(4):
                ada_unit(u)
            ffn("ffn1")
            owner[5] = ("ada_rows_ready", 12)
            owner[6] = ("ada_added", 12)
            sums(DC, ONES, TOK)
            sums(DC, ONES, TOK)
            ready = pieces_of(DC)
            for m in range(16):
                block_(DC, *x_ops(), ready=ready if m == 0 else None)

            pe.wait_ge(sem("block_free"), n["freed"])
            for h in range(HEADS):
                turn([ZI[:, h, t * P:(t + 1) * P] for t in range(TT)])
            for _ in range(6):
                gate_block()
            pe.wait_ge(sem("hg_factors_ready"), 1)
            for h in range(HEADS):
                turn([K2[:, h, t * P:(t + 1) * P] for t in range(TT)])
            for h in range(HEADS):
                b = 5 + h // 2
                if h % 2 == 0:
                    claim(b)
                for c in range(NCH):
                    r0, t = CH * (c % 2), c // 2
                    ins = pe.matmul(BANK[b][r0:r0 + CH, 256 * (h % 2) + CH * t:256 * (h % 2) + CH * t + CH],
                                    K1[:, h, CH * c:CH * c + CH], Q1[:, h, CH * c:CH * c + CH],
                                    start=True, stop=True)
                if h % 2:
                    ins.then_inc(sem("hg_scores_done"), 1)
                    owner[b] = ("hg_scores_read", h // 2 + 1)
            pe.wait_ge(sem("turned"), n["turn"])
            for c in range(NCH - 1):
                b, r0, t = 2 + c % 2, CH * (c % 2), c // 2
                claim(b)
                for h in range(HEADS):
                    ins = pe.matmul(BANK[b][:, h * P:(h + 1) * P], K2T[r0:r0 + CH, h, t * P:(t + 1) * P],
                                    VT[r0:r0 + CH, h, t * P:(t + 1) * P], start=True, stop=True)
                ins.then_inc(sem("kv_done"), 1)
                owner[b] = ("state_ready", c + 1)
                gate_block(c % 4, 4)
            gate_block(3, 4)
            pe.wait_ge(sem("hg_scores_read"), 2)
            pe.wait_ge(sem("state_ready"), NCH - 1)
            for h in range(HEADS):
                b = 5 + h % 2
                claim(b)
                for t in range(TT):
                    pe.matmul(BANK[b][:, P * t:P * t + P], VT[:, h, t * P:(t + 1) * P], SC[:, h, t, :],
                              start=True, stop=False)
                    for c in range(max(1, 2 * t), 2 * t + 2):
                        ins = pe.matmul(BANK[b][:, CH * c:CH * c + CH], STATE[:, c, h, :],
                                        Q2[:, h, CH * c:CH * c + CH], start=False, stop=(c == 2 * t + 1))
                ins.then_inc(sem("hg_out_done"), 1)
                owner[b] = ("hg_out_read", h + 1)
            for h in range(HEADS):
                for m in range(9):
                    block_(DC, *x_ops())
                    if h == 0 and m < HEADS:
                        sums(1, ONES, TOK)
                pe.wait_ge(sem("block_free"), n["freed"])
                for g in range(3):
                    turn([DZ[:, 6 + g, t * P:(t + 1) * P] for t in range(TT)])
                attend("dil", h, h + 1)

            operand(4 + 4)
            for m in range(4):
                block_(DC, *x_ops())
                if m == 0:
                    sums(DC, ONES, NMEM)
            ready = pieces_of(DC)
            for m in range(8):
                block_(DC, lambda k: MH[:, k, :], lambda k: ML[:, k, :], width=NMEM,
                       ready=ready if m == 0 else None)
            pe.wait_ge(sem("block_free"), n["freed"])
            for h in range(HEADS):
                turn([MKV[:, 4 + h, t * P:(t + 1) * P] for t in range(2)])
            attend("mem")

            operand(4)
            branches_ready.append(n["operand"])
            for m in range(DC // 2):
                for _ in range(2):
                    for br in range(3):
                        block_(4, lambda k: YH[br][:, k, :], lambda k: YL[br][:, k, :])
            ready = pieces_of(DC)
            for m in range(DC):
                block_(DC, *x_ops(), ready=ready if m == 0 else None)
            sums(DC, ONES, TOK)
            sums(DC, ONES, TOK)
            ffn("ffn2")
            sums(DC, ONES, TOK)

            operand(DC)
            for m in range(8):
                block_(DC, lambda k: CXH[:, k, :], lambda k: CXL[:, k, :], width=NMEM)
            for _ in range(2):
                sum_pair(PAIR)
            pe.wait_ge(sem("block_free"), n["freed"])
            for t in range(2):
                turn([CVF[:, c, t * P:(t + 1) * P] for c in range(4)])

            pe.wait_ge(sem("filter_weights_loaded"), 80)
            for layer in range(3):
                if layer:
                    pe.wait_ge(sem("sin_ready"), layer)
                claim(5)
                lhs = FW1[0:33, :] if layer == 0 else FW[:, layer - 1, :]
                rhs = FTS[0:33, :] if layer == 0 else FX[:]
                pe.matmul(BANK[5][0:64, :], lhs, rhs, start=True, stop=True).then_inc(sem("layer_done"), 1)
                owner[5] = ("layer_read", layer + 1)
            pe.wait_ge(sem("sin_ready"), 3)

            def filter_tile(o, i):
                b = 5 + n["small"] % 2
                t, d = i // 2, i % 2
                claim(b)
                pe.matmul(BANK[b][:], FX[:, t * P:(t + 1) * P],
                          FW4[:, (2 * o + d) * TOK:(2 * o + d + 1) * TOK], start=True, stop=True)\
                    .then_inc(sem("filter_done"), 1)
                n["small"] += 1
                owner[b] = ("filter_read", n["small"])

            def filter_norm(o, i):
                if i == 0:
                    claim(7)
                pe.wait_ge(sem("abs_ready"), 8 * o + i + 1)
                pe.matmul(BANK[7][:], ONES[:], FAB[:, i % 2, :], start=(i == 0), stop=(i == 2 * TT - 1))\
                    .then_inc(sem("abs_used"), 1)
                owner[7] = ("norm_read", o + 1)

            for i in range(2 * TT):
                filter_tile(0, i)
            for i in range(2 * TT):
                filter_norm(0, i)
            for o in range(2):
                ready = pieces_of(2 * TT)
                for m in range(KB):
                    e0 = 0 if m < 5 else 4
                    block_(TT, lambda k: EOH[:, e0 + k, :], lambda k: EOL[:, e0 + k, :],
                           ready=(lambda k: ready(e0 + k)) if m in (0, 5) else None)
                    if o == 0 and m < TT:
                        filter_tile(1, 2 * m)
                        filter_tile(1, 2 * m + 1)
                    if o == 0 and 1 <= m <= TT:
                        filter_norm(1, 2 * m - 2)
                        filter_norm(1, 2 * m - 1)

            sums(DC, ONES, TOK)
            ready = pieces_of(DC)
            for c in range(13):
                if c < 12:
                    block_(DC, *x_ops(), ready=ready if c == 0 else None)
                if c:
                    pe.wait_ge(sem("conv_ready"), c)
                    turn([HCV[:, (c - 1) % 2, t * P:(t + 1) * P] for t in range(TT)])
            for o in range(2):
                ready = pieces_of(TT)
                for m in range(FB):
                    block_(TT, lambda k: SH[:, k, :], lambda k: SL[:, k, :], ready=ready if m == 0 else None)
                ready = pieces_of(FB)
                for m in range(TT):
                    block_(FB, lambda k: SPH[:, k, :], lambda k: SPL[:, k, :], ready=ready if m == 0 else None)

            ready = pieces_of(DC)
            for m in range(12):
                block_(DC, *x_ops(), ready=ready if m == 0 else None)
                if m == 0:
                    for t in range(TT):
                        turn([HTM[:, 0, t, c * P:(c + 1) * P] for c in range(HYC)])
            pe.wait_ge(sem("rope_loaded"), 64)
            for c in range(8):
                sums(1, PAIR, TOK)
                gate_block()
                pe.wait_ge(sem("normed_ready"), c + 1)
                claim(5)
                pe.matmul(BANK[5][:], SWAP[:], NZ[:, c, :], start=True, stop=True).then_inc(sem("swap_done"), 1)
                owner[5] = ("swap_read", c + 1)
            for t in range(TT):
                turn([NZ[:, 8 + c, t * P:(t + 1) * P] for c in range(4)])
            pe.wait_ge(sem("na_ready"), 1)
            attend("na")

            operand(4 + 4)
            branches_ready.append(n["operand"])
            for m in range(DC):
                for br in range(2):
                    block_(4, lambda k: Y2H[br][:, k, :], lambda k: Y2L[br][:, k, :])
            ready = pieces_of(DC)
            for m in range(DC):
                block_(DC, *x_ops(), ready=ready if m == 0 else None)
            sums(DC, ONES, TOK)

            ready = pieces_of(DC)
            for m in range(16):
                block_(DC, *x_ops(), ready=ready if m == 0 else None)
            pe.wait_ge(sem("keys_loaded"), 16)
            pe.wait_ge(sem("block_free"), n["freed"])
            for t in range(TT):
                for q in range(4):
                    b = 5 + n["piece"] % 2
                    claim(b)
                    for j in range(4):
                        ins = pe.matmul(BANK[b][:, j * P:(j + 1) * P], QT[:, 4 * q + j, t * P:(t + 1) * P],
                                        KEYS[:, 4 * q + j, :], start=True, stop=True)
                    ins.then_inc(sem("score_ready"), 1)
                    n["piece"] += 1
                    owner[b] = ("score_read", n["piece"])
                for k in range(BY_TILE):
                    block_(DC, *x_ops(), gate=True)
                pe.wait_ge(sem("best_ready"), t + 1)
                turn([IJG[:, i, :] for i in range(3)])
            pe.wait_ge(sem("turned"), n["turn"])

            for b in (5, 6):
                claim(b)

            gelu0 = n["gate"]

            def gates_turn(i):
                for q in range(16):
                    pe.wait_ge(sem("hot_ready"), 16 * i + q + 1)
                    wait(pe, sem("stage_ready"), 16 * i + q - 1)
                    for u in range(4):
                        s = 4 * (q % 2) + u
                        ins = pe.matmul(BANK[5 + q % 2][:, u * P:(u + 1) * P], OI[:, s, :], OJ[:, s, :],
                                        start=True, stop=True)
                    ins.then_inc(sem("gates_done"), 1)
                    if q % 4 == 0:
                        pe.wait_ge(sem("gate_ready"), gelu0 + 4 * i + q // 4 - 3)
                    block_(DC, *x_ops(), in_loop=True, piece=(2 * (q % 4), 2 * (q % 4) + 1))

            gates_turn(0)
            with pe.Fori(1, GATE_TURNS) as i:
                st.units = 4 * (i - 1)
                gates_turn(i)
            st.units = 0
            st.skip(4 * (GATE_TURNS - 2), 4 * (GATE_TURNS - 2))
            n["gate"] += 4 * GATE_TURNS
            for b in range(4):
                owner[(st.block - 4 + b) % 4] = ("gate_ready", n["gate"])
            for b in (5, 6):
                owner[b] = ("stage_ready", TOK // 4)

            for b in range(4):
                claim(b)
            freed = n["freed"]

            def group(g):
                for m in range(8):
                    pe.wait_ge(sem("block_free"), freed + 16 * g + m - 3)
                    block_(DC, *x_ops(), in_loop=True)
                for m in range(8):
                    pe.wait_ge(sem("block_free"), freed + 16 * g + 8 + m - 3)
                    block_(8, lambda k: WH[:, k, :], lambda k: WL[:, k, :], in_loop=True,
                           ready=(lambda k: pe.wait_ge(sem("expert_ready"), 8 * g + k + 1)) if m == 0 else None)

            with pe.Fori(0, SHARED) as g:
                st.units = 16 * g
                group(g)
            st.units = 0
            st.skip(16 * (SHARED - 1), 16 * (SHARED - 1))

            def outputs(g):
                buffers = (WH2, WL2) if g % 2 == 0 else (WH, WL)
                return (lambda k: buffers[0][:, k, :]), (lambda k: buffers[1][:, k, :])

            def out_group(shift, j):
                pe.wait_ge(sem("expert_ready"), 8 * (SHARED + 1) + 8 * (shift + j))
                for m in range(8):
                    pe.wait_ge(sem("block_free"), freed + 16 * SHARED + 8 * (shift + j) + m - 3)
                    block_(8, *outputs(j), in_loop=True)

            with pe.Fori(0, AHEAD // 2) as i:
                st.units = 16 * i
                for j in range(2):
                    out_group(2 * i, j)
            st.units = 0
            st.skip(16 * (AHEAD // 2 - 1), 16 * (AHEAD // 2 - 1))
            out_group(AHEAD - 1, 0)

        @block.scalar
        def _(act):
            n = {"unit": 0, "square": 0, "sum": 0, "turn": 0, "ag": 0, "ov": 0, "f": 0, "gate": 0,
                 "exp": 0, "freed": 0, "h": 0, "beside": 0, "load": 0, "open": 0}

            def split(k, shift=0):
                if isinstance(shift, int):
                    k += shift
                slot = k % RING
                loaded, used = 16 * (k // RING + 1), UNIT * (k - RING + 1)
                if isinstance(shift, int):
                    wait(act, sem(f"raw_loaded{slot}"), loaded)
                    wait(act, sem("pe_steps"), used)
                else:
                    act.wait_ge(sem(f"raw_loaded{slot}"), loaded + 4 * shift)
                    act.wait_ge(sem("pe_steps"), used + UNIT * shift)
                act.activation(HI[:, slot, :], RAW[:, slot, :], ACT.Copy).then_inc(sem("hi_ready"), 1)

            def units(count):
                for _ in range(count):
                    if n["unit"] + 3 < TOTAL:
                        split(n["unit"] + 3)
                    n["unit"] += 1

            def stored():
                for s in range(2):
                    wait(act, sem(f"gate_stored{s}"), 16 * ((n["beside"] + 1 - s) // 2))

            def gate_block(bias, dst, stage=None):
                s = n["beside"] % 2
                units(1)
                if stage is None:
                    wait(act, sem("square_used"), n["square"])
                act.wait_ge(sem("pe_steps"), UNIT * n["unit"])
                wait(act, sem(f"gate_stored{s}"), 16 * (n["beside"] // 2))
                src = (SQ if stage is None else stage)[:, s, :]
                act.activation(src, BANK[s][:], ACT.Identity, bias=bias).then_inc(sem("gate_ready"), 1)
                n["gate"] += 1
                n["beside"] += 1
                act.wait_ge(sem("gate_ready"), n["gate"])
                act.dma_start(dst, src).then_inc(sem(f"gate_stored{s}"), 16)

            def gate1():
                k = n["beside"]
                m, i, br = k // 6, k % 6 // 3, k % 3
                gate_block(vec("b_gate", br * DC + 2 * m + i), G1[k])

            def gate2(stage=None):
                k = n["beside"] - 3 * DC
                m, br = k // 2, k % 2
                gate_block(vec("b_in2", 24 + br * DC + m), G2[k], stage)

            def load_gates(source, count, first, freed):
                s = n["load"] % 2
                n["load"] += 1
                act.wait_ge(sem("block_free"), freed)
                act.dma_start(MG[:, s, 0:count, :], source[first:first + count].rearrange("g p t -> p g t"))\
                    .then_inc(sem(f"gates_back{s}"), 16)

            def open_gates(count):
                s = n["open"] % 2
                n["open"] += 1
                act.wait_ge(sem(f"gates_back{s}"), 16 * ((n["open"] + 1) // 2))
                for i in range(2):
                    part = MG[:, s, i * count // 2:(i + 1) * count // 2, :].rearrange("p g t -> p (g t)")
                    act.activation(part, part, ACT.Sigmoid).then_inc(sem("gates_open"), 1)

            def square(src, width, sem_name, value):
                act.wait_ge(sem(sem_name), value)
                wait(act, sem("square_used"), n["square"] - 1)
                act.activation(SQ[:, n["square"] % 2, 0:width], src, ACT.Square)\
                    .then_inc(sem("square_ready"), 1)
                n["square"] += 1

            def root(width):
                n["sum"] += 1
                act.wait_ge(sem("sum_read"), n["sum"])
                act.activation(RT[:, 0:width], MS[:, 0:width], ACT.Sqrt).then_inc(sem("root_ready"), 1)

            def high(dst, src, shift=None):
                n["f"] += 1
                act.wait_ge(sem("piece_made"), n["f"])
                if shift is None:
                    ins = act.activation(dst, src, ACT.Copy)
                else:
                    ins = act.activation(dst, src, ACT.Identity, bias=shift)
                ins.then_inc(sem("piece_high"), 1)

            def highs(hi, src, count, shift=None, first=0):
                for c in range(first, first + count):
                    high(hi[:, c, :], src[:, c, :], shift(c) if shift else None)

            def highs_after(hi, src, count, name, first, each=0):
                for c in range(count):
                    act.wait_ge(sem(name), first + each * c)
                    act.activation(hi[:, c, :], src[:, c, :], ACT.Copy).then_inc(sem("piece_high"), 1)

            def turned(dst, view=None):
                b = 4 if n["turn"] % 2 == 0 else 7
                n["turn"] += 1
                act.wait_ge(sem("turn_done"), n["turn"])
                cols = int(np.prod(dst.shape[1:]))
                src = BANK[b][0:dst.shape[0], 0:cols]
                if len(dst.shape) == 3:
                    src = src.rearrange("p (a b) -> p a b", a=dst.shape[1])
                act.activation(dst, src, ACT.Copy).then_inc(sem("turned"), 1)

            def ffn(name, freed0):
                n0 = n["unit"]
                mix = 2 if name == "ffn1" else 1

                def two_pairs(i):
                    for u in range(4 * mix):
                        split(n0 + 3 + u, 4 * mix * i)
                        if u % (2 * mix) == 1:
                            p = u // (2 * mix)
                            act.wait_ge(sem("pe_steps"), UNIT * (n0 + u) + UNIT * 4 * mix * i)
                            wait(act, sem("block_free"), freed0 + 4 * i + 2 * p - 2)
                            act.activation(SG[:, p, :], BANK[(n0_block[0] + 2 * p) % 4][:], ACT.Silu)\
                                .then_inc(sem("silu_ready"), 1)

                two_pairs(0)
                with act.Fori(1, FC // 2) as i:
                    two_pairs(i)
                n["unit"] += 2 * FC * mix
                n["freed"] = freed0 + 2 * FC
                n0_block[0] += 2 * FC
                if name == "ffn1":
                    units(DC * FC // UNIT)
                else:
                    act.wait_ge(sem("pe_steps"), UNIT * n["unit"])
                    act.dma_start(CT[:], a["ctx"]).then_inc(sem("ctx_loaded"), 16)
                    units(6)
                    for c in range(DC):
                        square(CT[:, c, :], NMEM, "ctx_loaded", 16)
                    root(NMEM)
                    highs(CXH, CT, DC, lambda c: MOD[:, c, 1:2])
                    units(DC * FC // UNIT - 6)
                n["freed"] += DC
                n0_block[0] += DC

            n0_block = [0]

            def blocks(count, kc=DC):
                units(count * kc // UNIT)
                n0_block[0] += count
                n["freed"] += count

            def residual_squares():
                for c in range(DC):
                    square(HT[:, c, :], TOK, "h_ready", n["h"] + c + 1)
                n["h"] += DC
                root(TOK)

            def branch_squares(src):
                for c in range(DC):
                    square(src[:, c, :], TOK, "block_free", n["freed"] - DC + c + 1)
                root(TOK)

            def bias(h):
                if h > 1:
                    act.wait_ge(sem("score_read"), na_pieces[0] + 8 * (h - 1))
                act.dma_start(NB[:, h % 2, :], a["na_bias"][h]).then_inc(sem(f"na_bias_loaded{h % 2}"), 16)

            na_pieces = [HEADS * TT * 3 + HEADS * TT]

            def attend(kind, h0=0, h1=99):
                steps = [s for s in attention_steps(kind) if h0 <= s[0] < h1]
                S = NS if kind == "na" else DS
                T = NP if kind == "na" else DP

                def exps(h, t, ranges):
                    width, e = sum(k1 - k0 for k0, k1 in ranges), n["exp"] % 2
                    n["exp"] += 1
                    act.wait_ge(sem("max_ready"), n["exp"])
                    act.activation(S[:, e, 0:width], S[:, e, 0:width], ACT.Exp, bias=NMX[:, e:e + 1],
                                   accum_out=SUM[:, e:e + 1]).then_inc(sem("exp_ready"), 1)

                def transposed(h, t, ranges):
                    left = sum(k1 - k0 for k0, k1 in ranges) // P
                    while left:
                        k = min(4, left)
                        left -= k
                        wait(act, sem("group_used"), n["ag"] - 1)
                        turned(T[:, n["ag"] % 2, 0:k * P])
                        n["ag"] += 1

                def out(h, t, ranges):
                    groups = -(-(sum(k1 - k0 for k0, k1 in ranges) // P) // 4)
                    out_groups[0] += groups
                    act.wait_ge(sem("group_used"), out_groups[0])
                    b = 2 + n["ov"] % 2
                    n["ov"] += 1
                    if kind == "na":
                        r0 = 64 * (h % 2)
                        dst, src = NO[r0:r0 + 64, h // 2, t * P:(t + 1) * P], BANK[b][r0:r0 + 64, 0:P]
                    else:
                        dst, src = (DO if kind == "dil" else MO)[:, h, t * P:(t + 1) * P], BANK[b][:, 0:P]
                    act.activation(dst, src, ACT.Copy).then_inc(sem("out_read"), 1)

                exps(*steps[0])
                for i, s in enumerate(steps):
                    if kind == "na" and s[1] == 1 and s[0] + 1 < NAH:
                        bias(s[0] + 1)
                    transposed(*s)
                    if i + 1 < len(steps):
                        exps(*steps[i + 1])
                    if i % gate_parts(kind) == gate_parts(kind) - 1:
                        gate2() if kind == "na" else gate1()
                    out(*s)

            out_groups = [0]

            act.wait_ge(sem("vec_loaded"), 16)
            c0 = VCOL["cond"]
            act.activation(CS[:].rearrange("p a b -> p (a b)"), VEC[:, c0:c0 + 16], ACT.Silu)\
                .then_inc(sem("cond_ready"), 1)
            act.wait_ge(sem("lb_shifted"), 1)
            act.activation(LB[:, 3:5, :], LB[:, 1:3, :], ACT.Exp).then_inc(sem("lb_exp"), 1)
            for c in range(DC):
                square(HT[:, c, :], TOK, f"x_loaded{c}", 16)
            for k in range(3):
                split(k)
            root(TOK)
            highs(XH, XF, DC)
            units(4)
            ffn("ffn1", n["freed"])
            branch_squares(YT)
            residual_squares()
            highs(XH, XF, DC)
            blocks(16)
            act.wait_ge(sem("block_free"), n["freed"])
            act.activation(ZQ[:], ZQ[:], ACT.Silu).then_inc(sem("hg_q_ready"), 1)
            act.activation(ZF[:], ZF[:], ACT.Sigmoid).then_inc(sem("hg_sigmoid"), 1)
            act.activation(ZOG[:], ZOG[:], ACT.Sigmoid).then_inc(sem("hg_og_ready"), 1)
            for h in range(HEADS):
                turned(VT[:, h, :])
            act.dma_start(TRI[:], a["tri"]).then_inc(sem("tri_loaded"), 16)
            act.wait_ge(sem("hg_f_ready"), 1)
            act.activation(B0[:], ZF[:], ACT.Ln).then_inc(sem("hg_log"), 1)
            for _ in range(5):
                gate1()
            act.wait_ge(sem("hg_shift"), 1)
            act.activation(Q1[:], B1[:], ACT.Exp).then_inc(sem("hg_exp"), 1)
            act.activation(K1[:], B1[:], ACT.Exp, scale=-1.0).then_inc(sem("hg_exp"), 1)
            act.activation(Q2[:], B0[:], ACT.Exp).then_inc(sem("hg_exp"), 1)
            last = B0[:].rearrange("p h (n c) -> p (h n) c", c=CH)[:, :, CH - 1]
            act.activation(DEC[:], last, ACT.Exp).then_inc(sem("hg_exp"), 1)
            act.wait_ge(sem("hg_shift"), 2)
            act.activation(K2[:], B1[:], ACT.Exp).then_inc(sem("hg_exp"), 1)
            gate1()
            for h in range(HEADS):
                turned(K2T[:, h, :])
            for _ in range(2):
                gate1()
            stored()
            for h in range(HEADS):
                square(OF[:, h, :], TOK, "hg_out_read", h + 1)
                units(1)
                root(TOK)
            highs(YH[0], OF, 4)

            for h in range(HEADS):
                if h:
                    act.wait_ge(sem("score_read"), 12 * h)
                act.dma_start(DB[:], a["dil_bias"][h]).then_inc(sem("bias_loaded"), 16)
                units(9 if h else 9 - HEADS)
                n0_block[0] += 9
                n["freed"] += 9
                for g in range(3):
                    turned(DV[:, g].rearrange("p t d -> p (t d)"))
                attend("dil", h, h + 1)
            highs_after(YH[1], DO, 4, "out_read", n["ov"])

            act.wait_ge(sem("group_used"), out_groups[0])
            act.dma_start(MT[:], a["mem"]).then_inc(sem("mem_loaded"), 16)
            stored()
            for c in range(DC):
                square(MT[:, c, :], NMEM, "mem_loaded", 16)
            root(NMEM)
            highs(MH, MF, DC)
            blocks(4)
            blocks(8)
            for h in range(HEADS):
                turned(MV[:, h].rearrange("p t d -> p (t d)"))
            attend("mem")
            highs_after(YH[2], MO, 4, "out_read", n["ov"])

            stored()
            act.wait_ge(sem("operand_ready"), branches_ready[0])
            load_gates(G1, 6, 0, n["freed"])
            for m in range(DC // 2):
                if m + 1 < DC // 2:
                    load_gates(G1, 6, 6 * m + 6, n["freed"])
                open_gates(6)
                blocks(6, 4)
                if m:
                    highs(XH, MY, 2, None, 2 * m - 2)
            highs(XH, MY, 2, None, DC - 2)
            blocks(DC)
            branch_squares(XF)
            residual_squares()
            highs(XH, XF, DC)
            ffn("ffn2", n["freed"])
            act.wait_ge(sem("pe_steps"), UNIT * n["unit"])
            for dst, name in ((FTS, "feats"), (FW1, "f1"), (FW, "f23"), (FW4, "f4"), (FVEC, "fvec")):
                act.dma_start(dst[:], a[name]).then_inc(sem("filter_weights_loaded"), 16)
            act.dma_start(DCY[:], a["decay"]).then_inc(sem("decay_loaded"), 16)
            act.dma_start(SKIP[:], a["skip"]).then_inc(sem("decay_loaded"), 16)
            branch_squares(YT)

            blocks(8)
            for c in range(4):
                square(CK[:, c, :], NMEM, "block_free", n["freed"] - 7 + c)
                if c % 2:
                    root(TOK)
            for t in range(2):
                turned(CV[:, t, :])

            for layer in range(3):
                act.wait_ge(sem("angle_ready"), layer + 1)
                act.activation(FX[:], FA[:, 0, :], ACT.Sin).then_inc(sem("sin_ready"), 1)

            def filter_abs(o, i):
                t, d = i // 2, i % 2
                act.wait_ge(sem("filter_read"), 8 * o + i + 1)
                wait(act, sem("abs_used"), 8 * o + i - 1)
                act.activation(FAB[:, i % 2, :], (FBW if d else FFW)[:, t, :], ACT.Abs)\
                    .then_inc(sem("abs_ready"), 1)

            for i in range(2 * TT):
                filter_abs(0, i)
            highs(EOH[:, 0:4, :], FE, 4)
            highs(EOH[:, 4:8, :], FFW, 4)
            for m in range(TT):
                if m % 2:
                    units(1)
                filter_abs(1, 2 * m)
                filter_abs(1, 2 * m + 1)
            highs(EOH[:, 0:4, :], FE, 4)
            units(2)
            highs(EOH[:, 4:8, :], FFW, 4)
            units(5)
            n0_block[0] += 2 * KB
            n["freed"] += 2 * KB

            for c in range(DC):
                square(HT[:, c, :], TOK, "h_ready", n["h"] + c + 1)
            root(TOK)
            highs(XH, XF2, DC, lambda c: MOD[:, c, 0:1])
            for c in range(13):
                if c < 12:
                    blocks(1)
                if c:
                    turned(HTM[:, (c - 1) // 4, :, ((c - 1) % 4) * P:((c - 1) % 4 + 1) * P])
            for o in range(2):
                if o == 0:
                    highs_after(SH, HTM[:, 0], TT, "turned", n["turn"])
                else:
                    highs_after(SH, HTM[:, 0], TT, "block_free", n["freed"] - TT + 1, 1)
                for i in range(4):
                    blocks(2, TT)
                    for j in range(2):
                        high(SPH[:, 2 * i + j, :], SQ[:, j, :])
                blocks(TT, FB)
            act.wait_ge(sem("pe_steps"), UNIT * n["unit"])
            highs(XH, XF, DC, lambda c: MOD[:, c, 0:1])
            for t in range(TT):
                turned(HY[:, :, t * P:(t + 1) * P])
            highs_after(Y2H[0], HY, 4, "turned", n["turn"])

            for dst, name in ((COS, "cos"), (SIN, "sin"), (SWAP, "swap"), (CMASK, "cmask")):
                act.dma_start(dst[:], a[name]).then_inc(sem("rope_loaded"), 16)
            bias(0)
            blocks(12)
            square(NZ[:, 0, :], TOK, "block_free", n["freed"] - 12 + 1)
            for c in range(8):
                root(TOK)
                if c < 7:
                    square(NZ[:, c + 1, :], TOK, "block_free", n["freed"] - 12 + c + 2)
                gate2(GST)
            stored()
            for t in range(TT):
                turned(NV[:, t, :])
            attend("na")
            highs_after(Y2H[1], NO, 4, "out_read", n["ov"])
            stored()
            act.wait_ge(sem("operand_ready"), branches_ready[1])
            load_gates(G2, 4, 0, n["freed"])
            for m in range(DC // 2):
                if m + 1 < DC // 2:
                    load_gates(G2, 4, 4 * m + 4, n["freed"])
                open_gates(4)
                blocks(4, 4)
                if m:
                    highs(XH, MY, 2, None, 2 * m - 2)
            highs(XH, MY, 2, None, DC - 2)
            blocks(DC)
            branch_squares(HT)

            highs(XH, XF, DC, lambda c: MOD[:, 24 + c, 0:1])
            blocks(16)
            act.dma_start(KEYS[:], a["keys"]).then_inc(sem("keys_loaded"), 16)
            act.dma_start(IOTA[:], a["iota"]).then_inc(sem("iota_loaded"), 16)
            def ahead_gelu(j, steps, shift=0):
                s = j % 2
                act.wait_ge(sem("pe_steps"), steps)
                wait(act, sem(f"ahead_stored{s}"), 16 * (j // 2) + (shift if isinstance(shift, int) else 8 * shift))
                act.activation(SQ[:, s, :], BANK[(n0_block[0]) % 4][:], ACT.Gelu).then_inc(sem("gate_ready"), 1)
                act.wait_ge(sem("gate_ready"), n["gate"] + j + 1 + shift)
                act.dma_start(UD[j + shift], SQ[:, s, :]).then_inc(sem(f"ahead_stored{s}"), 16)
                n0_block[0] += 1

            for t in range(TT):
                for k in range(BY_TILE):
                    units(1)
                    ahead_gelu(BY_TILE * t + k, UNIT * n["unit"])
                    if k == BY_TILE - 3:
                        act.wait_ge(sem("best_shift"), t + 1)
                        act.activation(BS[:], BS[:], ACT.Exp).then_inc(sem("best_exp"), 1)
                turned(IJGT[:, :, t * P:(t + 1) * P])

            def stage(i, q16):
                s, q = q16 // 4 % 2, q16 % 4
                act.wait_ge(sem("gates_done"), 16 * i + q16 + 1)
                wait(act, sem(f"stage_stored{s}"), 32 * i + 16 * (q16 // 8))
                act.activation(STG[:, s, :, 4 * q:4 * q + 4].rearrange("p j t -> p t j"),
                               BANK[5 + q % 2][:].rearrange("p (t j) -> p t j", t=4), ACT.Copy)\
                    .then_inc(sem("stage_ready"), 1)

            n0 = n["unit"]

            def gates_turn(i):
                for q in range(16):
                    stage(i, q)
                    if q % 4 == 2:
                        split(n0 + 3 + q // 4, 4 * i)
                    if q % 4 == 3:
                        u = q // 4
                        ahead_gelu(BY_TILE * TT + u, UNIT * (n0 + u + 1) + 4 * UNIT * i, 4 * i)

            gates_turn(0)
            with act.Fori(1, GATE_TURNS) as i:
                gates_turn(i)
            n["unit"] += 4 * GATE_TURNS
            n0 = n["unit"]

            def gelus(g, shift):
                for u in range(16):
                    split(n0 + 3 + u, shift)
                    if u < 8:
                        act.wait_ge(sem("pe_steps"), UNIT * (n0 + u + 1) + UNIT * shift)
                        wait(act, sem("gates_used"), 8 * g + u - 1)
                        act.activation(GE[:, u % 2, :], BANK[(n0_block[0] + u) % 4][:], ACT.Gelu)\
                            .then_inc(sem("gelu_ready"), 1)

            gelus(0, 0)
            with act.Fori(1, SHARED) as g:
                gelus(g, 16 * g)
            n["unit"] += 16 * SHARED
            n0 = n["unit"]
            with act.Fori(0, AHEAD - 1) as g:
                for u in range(8):
                    split(n0 + 3 + u, 8 * g)
            n["unit"] += 8 * (AHEAD - 1)
            units(8)

        @block.vector
        def _(dve):
            st = Stepper()
            n = {"freed": 0, "square": 0, "sum": 0, "high": 0, "piece": 0, "exp": 0, "product": 0,
                 "gate": 0, "groups": [], "operand": 1, "made": 0}
            link = Link(dve, sem("dve_order"))

            def done(kc):
                st.step += kc
                dve.wait_ge(sem("pe_steps"), st.steps_(st.step))
                b = st.block % 4
                st.block += 1
                return BANK[b]

            def free(ins, count=1):
                n["freed"] += count
                ins.then_inc(sem("block_free"), count)

            def evacuated():
                dve.wait_ge(sem("block_free"), n["freed"])

            def copy_blocks(dst, count, kc=DC, width=TOK, bias=None, first=0):
                for m in range(first, first + count):
                    bank = done(kc)
                    if bias is None:
                        free(dve.tensor_copy(dst[:, m, 0:width], bank[:, 0:width]))
                    else:
                        free(dve.tensor_scalar(dst[:, m, 0:width], bank[:, 0:width], bias(m), None, ALU.add))

            def rstd(pieces, denom, width):
                n["square"] += pieces
                n["sum"] += 1
                dve.wait_ge(sem("square_used"), n["square"])
                dve.tensor_scalar(MS[:, 0:width], STB[:, 0:width], 1.0 / denom, EPS, ALU.mult, ALU.add)\
                    .then_inc(sem("sum_read"), 1)
                dve.wait_ge(sem("root_ready"), n["sum"])
                link(dve.reciprocal(RSTD[:, 0:width], RT[:, 0:width]))

            def made(ins):
                ins.then_inc(sem("piece_made"), 1)
                n["made"] += 1

            def low(dst, src, high, shift=None):
                n["high"] += 1
                dve.wait_ge(sem("piece_high"), n["high"])
                if shift is None:
                    ins = dve.tensor_tensor(dst, src, high.bitcast(F32), ALU.subtract)
                else:
                    ins = dve.scalar_tensor_tensor(dst, src, shift, high.bitcast(F32), ALU.add, ALU.subtract)
                ins.then_inc(sem("operand_ready"), 1)
                n["operand"] += 1

            def lows(lo, src, hi, count, shift=None, first=0):
                for c in range(first, first + count):
                    low(lo[:, c, :], src[:, c, :], hi[:, c, :], shift(c) if shift else None)
                dve.wait_ge(sem("operand_ready"), n["operand"])

            def normed(dst, src, hi, lo, width, gain, shift=None):
                for c in range(DC + 2):
                    if c < DC:
                        made(dve.scalar_tensor_tensor(dst[:, c, :], src[:, c, :], gain(c), RSTD[:, 0:width],
                                                      ALU.mult, ALU.mult))
                    if c >= 2:
                        low(lo[:, c - 2, :], dst[:, c - 2, :], hi[:, c - 2, :], shift(c - 2) if shift else None)
                dve.wait_ge(sem("operand_ready"), n["operand"])

            def post(src, name, factor, beside=None):
                for c in range(DC):
                    link(dve.scalar_tensor_tensor(src[:, c, :], src[:, c, :], vec(name, c), RSTD[:],
                                                  ALU.mult, ALU.mult))
                    dve.scalar_tensor_tensor(HT[:, c, :], src[:, c, :], factor, HT[:, c, :],
                                             ALU.mult, ALU.add).then_inc(sem("h_ready"), 1)
                    if beside:
                        beside(c)

            def ffn(k):
                s0, b0, freed0 = st.step, st.block, n["freed"]
                mix = 1 if k else 2
                with dve.Fori(0, FC // 2) as i:
                    for p in range(2):
                        dve.wait_ge(sem("pe_steps"), s0 + UNIT * ((2 * p + 1) * mix + 1) + 4 * mix * UNIT * i)
                        dve.wait_ge(sem("silu_ready"), FC * k + 2 * i + p + 1)
                        dve.tensor_tensor(HF[:, p, :], SG[:, p, :], BANK[(b0 + 2 * p + 1) % 4][:], ALU.mult)\
                            .then_inc(sem("block_free"), 2)
                        dve.wait_ge(sem("block_free"), freed0 + 4 * i + 2 * p + 2)
                        dve.tensor_copy(FH[:, 2 * i + p, :], HF[:, p, :]).then_inc(sem("hidden_high"), 1)
                        dve.wait_ge(sem("hidden_high"), FC * k + 2 * i + p + 1)
                        dve.tensor_tensor(FL[:, 2 * i + p, :], HF[:, p, :], FH[:, 2 * i + p, :].bitcast(F32),
                                          ALU.subtract).then_inc(sem("hidden_ready"), 1)
                        if k == 0 and p == 0:
                            ada_columns(i)
                    if k == 0:
                        ada_rows(i + 1, s0 + 8 * UNIT + 8 * UNIT * i)
                st.skip(2 * FC * mix, 2 * FC)
                if k == 0:
                    ada_columns(FC // 2)
                n["freed"] += 2 * FC
                if k == 0:
                    copy_blocks(YT, DC, FC)
                else:
                    copy_blocks(YT, 2, FC)
                    rstd(DC, D, NMEM)
                    normed(CT, CT, CXH, CXL, NMEM, lambda c: COEF[:, 1, c:c + 1], lambda c: MOD[:, c, 1:2])
                    copy_blocks(YT, DC - 2, FC, first=2)

            def ada_rows(g, steps):
                dve.wait_ge(sem("pe_steps"), steps)
                dve.tensor_copy(AR[:], BANK[5][0:4, :]).then_inc(sem("ada_rows_ready"), 1)

            def ada_columns(g):
                dve.wait_ge(sem("ada_folded"), g + 1)
                which = slice(4 * g, 4 * g + 4) if isinstance(g, int) else bass.ds(4 * g, 4)
                bias = VEC[:, VCOL["b_ada"]:VCOL["b_ada"] + 48][:, which]
                dve.tensor_tensor(MOD[:, which, :], BANK[6][:, 0:8].rearrange("p (m w) -> p m w", w=2),
                                  bias.unsqueeze(2).to_broadcast([P, 4, 2]), ALU.add)\
                    .then_inc(sem("ada_added"), 1)

            def attend(kind, h0=0, h1=99):
                steps = [s for s in attention_steps(kind) if h0 <= s[0] < h1]
                S = NS if kind == "na" else DS
                scale = 0.125 if kind == "na" else P ** -0.5

                def scores(h, t, ranges):
                    e = n["exp"] % 2
                    if n["exp"] >= 2:
                        dve.wait_ge(sem("group_used"), n["groups"][n["exp"] - 2])
                    col = 0
                    for g, (k0, k1) in enumerate(ranges):
                        bank = SCB[n["piece"] % 2]
                        n["piece"] += 1
                        dve.wait_ge(sem("score_ready"), n["piece"])
                        w = k1 - k0
                        dst = S[:, e, col:col + w]
                        if kind == "dil":
                            x0 = k0 + (TOK - P) - P * t
                            ins = dve.scalar_tensor_tensor(dst, bank[:, 0:w], scale, DB[:, g, x0:x0 + w],
                                                           ALU.mult, ALU.add)
                        elif kind == "na" and g == 0:
                            ins = dve.scalar_tensor_tensor(dst, bank[:, 0:w], scale,
                                                           NB[:, h % 2, 64 * (6 - 2 * t):64 * (14 - 2 * t)],
                                                           ALU.mult, ALU.add)
                        else:
                            ins = dve.tensor_scalar(dst, bank[:, 0:w], scale, None, ALU.mult)
                        ins.then_inc(sem("score_read"), 1)
                        col += w
                    before = n["groups"][-1] if n["groups"] else 0
                    n["groups"].append(before - (-(col // P) // 4))
                    n["exp"] += 1
                    dve.wait_ge(sem("score_read"), n["piece"])
                    dve.tensor_reduce(NMX[:, e:e + 1], S[:, e, 0:col], AX_X, ALU.max, negate=True)\
                        .then_inc(sem("max_ready"), 1)

                def divide(h, t, ranges):
                    k = n["product"]
                    n["product"] += 1
                    e, width = k % 2, sum(k1 - k0 for k0, k1 in ranges)
                    dve.wait_ge(sem("exp_ready"), k + 1)
                    link(dve.reciprocal(RSUM[:, e:e + 1], SUM[:, e:e + 1]))
                    dve.tensor_scalar(S[:, e, 0:width], S[:, e, 0:width], RSUM[:, e:e + 1], None, ALU.mult)\
                        .then_inc(sem("prob_ready"), 1)

                for s in steps:
                    if kind == "na" and s[1] == 0:
                        h = s[0]
                        dve.wait_ge(sem(f"na_bias_loaded{h % 2}"), 16 * (h // 2 + 1))
                        table = NB[:, h % 2, :].rearrange("p (x c) -> p x c", c=64)
                        link(dve.tensor_tensor(table, table, CMASK[:].unsqueeze(1).to_broadcast([P, 14, 64]),
                                               ALU.add))
                    scores(*s)
                    divide(*s)

            dve.wait_ge(sem("vec_loaded"), 16)
            lb = [VEC[:, VCOL["lb0"]:VCOL["lb0"] + 4], VEC[:, VCOL["lb1"]:VCOL["lb1"] + 4]]
            link(dve.tensor_tensor(LB[:, 0, :], lb[0], lb[1], ALU.max))
            link(dve.tensor_tensor(LB[:, 1, :], lb[0], LB[:, 0, :], ALU.subtract))
            dve.tensor_tensor(LB[:, 2, :], lb[1], LB[:, 0, :], ALU.subtract).then_inc(sem("lb_shifted"), 1)
            dve.wait_ge(sem("lb_exp"), 1)
            link(dve.tensor_tensor(LB[:, 0, :], LB[:, 3, :], LB[:, 4, :], ALU.add))
            link(dve.reciprocal(LB[:, 1, :], LB[:, 0, :]))
            link(dve.tensor_tensor(LB[:, 2, :], LB[:, 3, :], LB[:, 1, :], ALU.mult))
            link(dve.tensor_scalar(LB[:, 5, :], LB[:, 2, :], -1.0, 1.0, ALU.mult, ALU.add))
            dve.wait_ge(sem("cond_ready"), 1)
            link(dve.tensor_copy(CP[:, :, 0:2], CS[:]))
            dve.tensor_tensor(CP[:, :, 2:4], CS[:], CP[:, :, 0:2].bitcast(F32), ALU.subtract)\
                .then_inc(sem("operand_ready"), 1)
            rstd(DC, D, TOK)
            normed(XF, HT, XH, XL, TOK, lambda c: vec("ffn1_pre", c))
            st.skip(4, 0)
            ada_rows(0, st.step)
            ffn(0)
            dve.wait_ge(sem("ada_added"), 12)
            norm = [VEC[:, VCOL[k]:VCOL[k] + 8] for k in ("norm1", "norm1", "norm2")]
            for i, (c0, who) in enumerate(((8, 0), (8, 1), (32, 0))):
                link(dve.scalar_tensor_tensor(COEF[:, i, :], MOD[:, c0:c0 + 8, who], 1.0, norm[i],
                                              ALU.add, ALU.mult))
            rstd(DC, D, TOK)
            post(YT, "ffn1_post", 0.5)
            rstd(DC, D, TOK)
            normed(XF, HT, XH, XL, TOK, lambda c: vec("mix_pre", c))

            for z in (ZQ, ZF, ZI, ZOG):
                copy_blocks(z, 4)
            st.skip(8, 0)
            dve.wait_ge(sem("hg_sigmoid"), 1)
            for h in range(HEADS):
                link(dve.tensor_scalar(ZF[:, h, :], ZF[:, h, :], LB[:, 5, h:h + 1], LB[:, 2, h:h + 1],
                                       ALU.mult, ALU.add))
            dve.tensor_scalar(KF[:], ZF[:], -1.0, 1.0, ALU.mult, ALU.add).then_inc(sem("hg_f_ready"), 1)
            dve.wait_ge(sem("hg_log"), 1)
            chunks = [b[:].rearrange("p h (n c) -> p (h n) c", c=CH) for b in (B0, B1)]
            d = 1
            for i in range(6):
                src, dst = chunks[i % 2], chunks[1 - i % 2]
                link(dve.tensor_copy(dst[:, :, 0:d], src[:, :, 0:d]))
                link(dve.tensor_tensor(dst[:, :, d:CH], src[:, :, d:CH], src[:, :, 0:CH - d], ALU.add))
                d *= 2

            def shifted(at, sign):
                edge = chunks[0][:, :, at:at + 1].to_broadcast([P, HEADS * NCH, CH])
                pair = (chunks[0], edge) if sign > 0 else (edge, chunks[0])
                dve.tensor_tensor(chunks[1], *pair, ALU.subtract).then_inc(sem("hg_shift"), 1)

            shifted(CH // 2 - 1, 1)
            dve.wait_ge(sem("hg_exp"), 2)
            shifted(CH - 1, -1)
            dve.wait_ge(sem("hg_q_ready"), 1)
            link(dve.tensor_tensor(Q1[:], Q1[:], ZQ[:], ALU.mult))
            link(dve.tensor_tensor(K1[:], K1[:], KF[:], ALU.mult))
            dve.wait_ge(sem("hg_exp"), 5)
            link(dve.tensor_tensor(Q2[:], Q2[:], ZQ[:], ALU.mult))
            dve.tensor_tensor(K2[:], K2[:], KF[:], ALU.mult).then_inc(sem("hg_factors_ready"), 1)
            dve.wait_ge(sem("turned"), HEADS)
            link(dve.memset(SC[:], 0.0))
            dve.wait_ge(sem("tri_loaded"), 16)
            for i in range(2):
                dve.wait_ge(sem("hg_scores_done"), i + 1)
                for j in range(4):
                    r0 = CH * (j % 2)
                    bank = BANK[5 + i][r0:r0 + CH, 256 * (j // 2):256 * (j // 2) + 256]
                    ins = dve.copy_predicated(SC[r0:r0 + CH, 2 * i + j // 2, :, r0:r0 + CH],
                                              TRI[r0:r0 + CH], bank.rearrange("p (t c) -> p t c", c=CH))
                    if j < 3:
                        link(ins)
                ins.then_inc(sem("hg_scores_read"), 1)
            for c in range(NCH - 1):
                dve.wait_ge(sem("kv_done"), c + 1)
                for h in range(HEADS):
                    kv = BANK[2 + c % 2][:, h * P:(h + 1) * P]
                    if c == 0:
                        ins = dve.tensor_copy(STATE[:, 1, h, :], kv)
                    else:
                        ins = dve.scalar_tensor_tensor(STATE[:, c + 1, h, :], STATE[:, c, h, :],
                                                       DEC[:, h * NCH + c:h * NCH + c + 1], kv,
                                                       ALU.mult, ALU.add)
                    if h < HEADS - 1:
                        link.n += 1
                        ins.then_inc(sem("dve_order"), 1)
                ins.then_inc(sem("state_ready"), 1)
                dve.wait_ge(sem("state_ready"), c + 1)
                dve.wait_ge(sem("dve_order"), link.n)
            for h in range(HEADS):
                dve.wait_ge(sem("hg_out_done"), h + 1)
                dve.tensor_copy(OF[:, h, :], BANK[5 + h % 2][:]).then_inc(sem("hg_out_read"), 1)
            for h in range(HEADS):
                rstd(1, P, TOK)
                link(dve.scalar_tensor_tensor(OF[:, h, :], OF[:, h, :], vec("hgn"), RSTD[:], ALU.mult, ALU.mult))
                dve.wait_ge(sem("hg_og_ready"), 1)
                made(dve.tensor_tensor(OF[:, h, :], OF[:, h, :], ZOG[:, h, :], ALU.mult))
            lows(YL[0], OF, YH[0], 4)

            for h in range(HEADS):
                copy_blocks(DZ, 9)
                dve.wait_ge(sem("bias_loaded"), 16 * (h + 1))
                attend("dil", h, h + 1)
                st.skip(2, 0)
            lows(YL[1], DO, YH[1], 4)

            rstd(DC, D, NMEM)
            normed(MF, MT, MH, ML, NMEM, lambda c: vec("mem_norm", c))
            copy_blocks(MQ, 4)
            copy_blocks(MKV, 8, width=NMEM)
            attend("mem")
            st.skip(8, 0)
            lows(YL[2], MO, YH[2], 4)

            def merge(dst, gates):
                dve.wait_ge(sem("piece_made"), n["made"])
                for i, gate in enumerate(gates):
                    free(dve.tensor_tensor(MP[:, i, :], gate, done(4)[:], ALU.mult))
                evacuated()
                if len(gates) == 3:
                    link(dve.tensor_tensor(MP[:, 0, :], MP[:, 0, :], MP[:, 1, :], ALU.add))
                made(dve.tensor_tensor(dst, MP[:, 0, :], MP[:, len(gates) - 1, :], ALU.add))

            for m in range(DC // 2):
                for i in range(2):
                    dve.wait_ge(sem("gates_open"), 2 * m + i + 1)
                    merge(MY[:, 2 * m + i, :], [MG[:, m % 2, 3 * i + br, :] for br in range(3)])
                if m:
                    lows(XL, MY, XH, 2, None, 2 * m - 2)
            lows(XL, MY, XH, 2, None, DC - 2)
            copy_blocks(XF, DC)
            rstd(DC, D, TOK)
            post(XF, "mix_post", 1.0)
            rstd(DC, D, TOK)
            normed(XF, HT, XH, XL, TOK, lambda c: vec("ffn2_pre", c))
            ffn(1)
            rstd(DC, D, TOK)

            def context_block(c):
                bank = done(DC)
                dst = CK[:, c, :] if c < 4 else CVF[:, c - 4, :]
                free(dve.tensor_scalar(dst, bank[:, 0:NMEM], vec("b_in2", 16 + c), None, ALU.add))

            post(YT, "ffn2_post", 0.5, context_block)
            evacuated()
            for pair in range(2):
                rstd(2, 64, TOK)
                for j in range(2):
                    c = 2 * pair + j
                    link(dve.scalar_tensor_tensor(CK[:, c, :], CK[:, c, :], vec("kg"),
                                                  RSTD[:, j * NMEM:(j + 1) * NMEM], ALU.mult, ALU.mult))

            dve.wait_ge(sem("filter_weights_loaded"), 80)
            round_up = 1.5 * 2.0 ** 23
            two_pi_hi = 6.28125
            two_pi_lo = 2.0 * np.pi - two_pi_hi
            for layer in range(3):
                dve.wait_ge(sem("layer_done"), layer + 1)
                dve.tensor_scalar(FA[:, 0, :], BANK[5][0:64, :], FVEC[:, layer:layer + 1], FVEC[:, 3:4],
                                  ALU.add, ALU.mult).then_inc(sem("layer_read"), 1)
                dve.wait_ge(sem("layer_read"), layer + 1)
                link(dve.tensor_scalar(FA[:, 1, :], FA[:, 0, :], 1.0 / (2.0 * np.pi), round_up, ALU.mult, ALU.add))
                link(dve.tensor_scalar(FA[:, 1, :], FA[:, 1, :], round_up, None, ALU.subtract))
                link(dve.scalar_tensor_tensor(FA[:, 2, :], FA[:, 1, :], -two_pi_hi, FA[:, 0, :], ALU.mult, ALU.add))
                link(dve.scalar_tensor_tensor(FA[:, 0, :], FA[:, 1, :], -two_pi_lo, FA[:, 2, :], ALU.mult, ALU.add))
                dve.tensor_scalar(FA[:, 0, :], FA[:, 0, :], 3.1415925, -3.1415925, ALU.min, ALU.max)\
                    .then_inc(sem("angle_ready"), 1)
            dve.wait_ge(sem("sin_ready"), 3)
            dve.wait_ge(sem("decay_loaded"), 32)

            def filter_taps(o, i):
                t, d = i // 2, i % 2
                k = 8 * o + i
                dve.wait_ge(sem("filter_done"), k + 1)
                dve.tensor_tensor((FBW if d else FFW)[:, t, :], BANK[5 + k % 2][:], DCY[:, t, :], ALU.mult)\
                    .then_inc(sem("filter_read"), 1)

            for i in range(2 * TT):
                filter_taps(0, i)

            def transformed(o, m, norm):
                free(dve.tensor_tensor(KHAT[:, o, m, :], done(TT)[:], norm[:], ALU.mult))

            for o, norm in enumerate((RSTD, RT)):
                dve.wait_ge(sem("abs_used"), 8 * (o + 1))
                link(dve.tensor_tensor(SKIP[0:1, o, :], SKIP[0:1, o, :], BANK[7][0:1, :], ALU.mult))
                dve.reciprocal(norm[:], BANK[7][:]).then_inc(sem("norm_read"), 1)
                dve.wait_ge(sem("norm_read"), o + 1)
                link(dve.memset(FBW[0:1, 0, :], 0.0))
                for t in range(TT):
                    ins = dve.tensor_tensor(FE[:, t, :], FFW[:, t, :], FBW[:, t, :], ALU.add)
                    if t == 0:
                        link(ins)
                        ins = dve.tensor_tensor(FE[0:1, 0, :], FE[0:1, 0, :], SKIP[0:1, o, :], ALU.add)
                    made(ins)
                dve.wait_ge(sem("piece_made"), n["made"])
                if o == 1:
                    lows(EOL[:, 0:4, :], FE, EOH[:, 0:4, :], 4)
                    for m in range(5, KB):
                        transformed(0, m, RSTD)
                for t in range(TT):
                    made(dve.tensor_tensor(FFW[:, t, :], FFW[:, t, :], FBW[:, t, :], ALU.subtract))
                    if o == 0:
                        low(EOL[:, t, :], FE[:, t, :], EOH[:, t, :])
                dve.wait_ge(sem("piece_made"), n["made"])
                lows(EOL[:, 4:8, :], FFW, EOH[:, 4:8, :], 4)
                if o == 0:
                    for m in range(5):
                        transformed(0, m, RSTD)
                        if m < TT:
                            filter_taps(1, 2 * m)
                            filter_taps(1, 2 * m + 1)
                else:
                    for m in range(KB):
                        transformed(1, m, RT)
            evacuated()

            rstd(DC, D, TOK)
            normed(XF2, HT, XH, XL, TOK, lambda c: COEF[:, 0, c:c + 1], lambda c: MOD[:, c, 0:1])
            turns0 = 4 + 4 + 12 + sum(-(-(sum(k1 - k0 for k0, k1 in r) // P) // 4)
                                      for kind in ("dil", "mem") for _, _, r in attention_steps(kind)) + 4 + 2
            for c in range(12):
                bank = done(DC)
                free(dve.tensor_scalar(HZ[:, c, :], bank[:], vec("b_in2", c), None, ALU.add))
                evacuated()
                if c >= 2:
                    dve.wait_ge(sem("turned"), turns0 + c - 1)
                z, out = HZ[:, c, :], HCV[:, c % 2, :]
                link(dve.tensor_scalar(out, z, vec("cw1", c), vec("cb", c), ALU.mult, ALU.add))
                link(dve.scalar_tensor_tensor(out[:, 1:TOK], z[:, 0:TOK - 1], vec("cw0", c), out[:, 1:TOK],
                                              ALU.mult, ALU.add))
                dve.scalar_tensor_tensor(out[:, 0:TOK - 1], z[:, 1:TOK], vec("cw2", c), out[:, 0:TOK - 1],
                                         ALU.mult, ALU.add).then_inc(sem("conv_ready"), 1)
            dve.wait_ge(sem("turned"), turns0 + 12)
            for o in range(2):
                lows(SL, HTM[:, 0], SH, TT)
                for i in range(4):
                    ar, ai = done(TT), done(TT)
                    kr, ki = KHAT[:, o, i, :], KHAT[:, o, 5 + i, :]
                    kr2 = KHAT[:, o, 4, :] if i == 0 else kr
                    t0, t1 = HCV[:, 0, :], HCV[:, 1, :]
                    dve.wait_ge(sem("piece_made"), n["made"])
                    link(dve.tensor_tensor(t0, ar[:], kr, ALU.mult))
                    link(dve.tensor_tensor(t1, ai[:], ki, ALU.mult))
                    made(dve.tensor_tensor(SQ[:, 0, :], t0, t1, ALU.subtract))
                    dve.wait_ge(sem("piece_made"), n["made"])
                    link(dve.tensor_tensor(t0, ar[:], ki, ALU.mult))
                    free(dve.tensor_tensor(t1, ai[:], kr2, ALU.mult), 2)
                    evacuated()
                    made(dve.tensor_tensor(SQ[:, 1, :], t0, t1, ALU.add))
                    for j in range(2):
                        low(SPL[:, 2 * i + j, :], SQ[:, j, :], SPH[:, 2 * i + j, :])
                for t in range(TT):
                    bank = done(FB)
                    free(dve.tensor_tensor(HTM[:, 0, t, :], bank[:], HTM[:, 1 + o, t, :], ALU.mult))
                    if o == 1:
                        for c in (2 * t, 2 * t + 1):
                            made(dve.scalar_tensor_tensor(XF[:, c, :], HT[:, c, :], COEF[:, 0, c:c + 1], RSTD[:],
                                                          ALU.mult, ALU.mult))
                evacuated()
            dve.wait_ge(sem("piece_made"), n["made"])
            lows(XL, XF, XH, DC, lambda c: MOD[:, c, 0:1])

            copy_blocks(NZ, 4, bias=lambda m: vec("b_in2", 12 + m))
            lows(Y2L[0], HY, Y2H[0], 4)
            copy_blocks(NZ, 8, bias=lambda m: vec("b_in2", 12 + m), first=4)
            dve.wait_ge(sem("rope_loaded"), 64)
            for c in range(8):
                rstd(1, 64, TOK)
                dve.scalar_tensor_tensor(NZ[:, c, :], NZ[:, c, :], vec("qg" if c < 4 else "kg"), RSTD[:],
                                         ALU.mult, ALU.mult).then_inc(sem("normed_ready"), 1)
                dve.wait_ge(sem("normed_ready"), c + 1)
                dve.wait_ge(sem("swap_done"), c + 1)
                link(dve.tensor_tensor(RP[:, 0, :], NZ[:, c, :], COS[:], ALU.mult))
                dve.tensor_tensor(RP[:, 1, :], BANK[5][:], SIN[:], ALU.mult).then_inc(sem("swap_read"), 1)
                dve.wait_ge(sem("swap_read"), c + 1)
                ins = dve.tensor_tensor(NZ[:, c, :], RP[:, 0, :], RP[:, 1, :], ALU.add)
                if c == 7:
                    ins.then_inc(sem("na_ready"), 1)
                else:
                    link(ins)
            attend("na")
            lows(Y2L[1], NO, Y2H[1], 4)
            st.skip(16, 0)
            for m in range(DC // 2):
                for i in range(2):
                    dve.wait_ge(sem("gates_open"), DC + 2 * m + i + 1)
                    merge(MY[:, 2 * m + i, :], [MG[:, m % 2, 2 * i + br, :] for br in range(2)])
                if m:
                    lows(XL, MY, XH, 2, None, 2 * m - 2)
            lows(XL, MY, XH, 2, None, DC - 2)
            for m in range(DC):
                bank = done(DC)
                free(dve.scalar_tensor_tensor(HT[:, m, :], bank[:], MOD[:, 16 + m, 0:1], HT[:, m, :],
                                              ALU.mult, ALU.add))

            rstd(DC, D, TOK)
            normed(XF, HT, XH, XL, TOK, lambda c: COEF[:, 2, c:c + 1], lambda c: MOD[:, 24 + c, 0:1])
            copy_blocks(QT, 16)
            dve.wait_ge(sem("iota_loaded"), 16)
            turns1 = turns0 + 12 + 4 + 4 + 2 * NAH * TT
            def ordered(instructions):
                for ins in instructions:
                    link.n += 1
                    ins.then_inc(sem("dve_order"), 1)
                dve.wait_ge(sem("dve_order"), link.n)

            for t in range(TT):
                for q in range(4):
                    bank = SCB[n["piece"] % 2]
                    n["piece"] += 1
                    dve.wait_ge(sem("score_ready"), n["piece"])
                    dve.tensor_copy(PS[:, 4 * q:4 * q + 4, :].rearrange("p a b -> p (a b)"), bank[:])\
                        .then_inc(sem("score_read"), 1)
                dve.wait_ge(sem("score_read"), n["piece"])
                ordered(dve.max(TOPS[:, j, 0:8], PS[:, j, :]) for j in range(16))
                ordered(dve.max_index(TOPI[:, j, 0:8], TOPS[:, j, 0:8], PS[:, j, :]) for j in range(16))
                ordered(dve.match_replace(PR[:, j, :], TOPS[:, j, 0:8], PS[:, j, :], -BIG) for j in range(16))
                ordered(dve.max(TOPS[:, j, 8:16], PR[:, j, :]) for j in range(16))
                ordered(dve.max_index(TOPI[:, j, 8:16], TOPS[:, j, 8:16], PR[:, j, :]) for j in range(16))
                link(dve.tensor_copy(TOPF[:], TOPI[:]))
                tops = TOPS[:].rearrange("p (h two) k -> p h two k", two=2)
                topf = TOPF[:].rearrange("p (h two) k -> p h two k", two=2)
                square4 = [P, 8, 16, 16]
                link(dve.tensor_tensor(CA[:].rearrange("p h (a b) -> p h a b", a=16),
                                       tops[:, :, 0, :].unsqueeze(3).to_broadcast(square4),
                                       tops[:, :, 1, :].unsqueeze(2).to_broadcast(square4), ALU.add))
                ordered(dve.max(BS[:, h, 0:8], CA[:, h, :]) for h in range(8))
                ordered(dve.max_index(BP[:, h, 0:8], BS[:, h, 0:8], CA[:, h, :]) for h in range(8))
                ordered(dve.match_replace(CR[:, h, :], BS[:, h, 0:8], CA[:, h, :], -BIG) for h in range(8))
                ordered(dve.max(BS[:, h, 8:16], CR[:, h, :]) for h in range(8))
                ordered(dve.max_index(BP[:, h, 8:16], BS[:, h, 8:16], CR[:, h, :]) for h in range(8))
                link(dve.tensor_copy(PRS[:], BS[:, :, 0]))
                dve.tensor_tensor(BS[:], BS[:], PRS[:].unsqueeze(2).to_broadcast([P, 8, 16]), ALU.subtract)\
                    .then_inc(sem("best_shift"), 1)
                link(dve.tensor_scalar(PA[:, 0], BP[:], 4, None, ALU.logical_shift_right))
                link(dve.tensor_scalar(PA[:, 1], BP[:], 15, None, ALU.bitwise_and))
                link(dve.tensor_copy(PAF[:], PA[:]))
                eq = EQ[:].rearrange("p h (k a) -> p h k a", k=16)
                if t:
                    dve.wait_ge(sem("turned"), turns1 + t)
                for i in range(2):
                    link(dve.tensor_tensor(eq, PAF[:, i].unsqueeze(3).to_broadcast(square4),
                                           IOTA[:, 0:16].unsqueeze(1).unsqueeze(1).to_broadcast(square4),
                                           ALU.is_equal))
                    link(dve.tensor_tensor(eq, eq, topf[:, :, i, :].unsqueeze(2).to_broadcast(square4), ALU.mult))
                    link(dve.tensor_reduce(IJG[:, i, :].rearrange("p (h k) -> p h k", h=8), eq, AX_X, ALU.add))
                dve.wait_ge(sem("best_exp"), t + 1)
                link(dve.tensor_reduce(PSUMS[:], BS[:], AX_X, ALU.add))
                link(dve.reciprocal(PRS[:], PSUMS[:]))
                dve.tensor_tensor(IJG[:, 2, :].rearrange("p (h k) -> p h k", h=8), BS[:],
                                  PRS[:].unsqueeze(2).to_broadcast([P, 8, 16]), ALU.mult)\
                    .then_inc(sem("best_ready"), 1)
            dve.wait_ge(sem("turned"), turns1 + TT)

            def hot(token, u):
                dve.tensor_scalar(OI[:, u, :], IOTA[:], IJGT[:, 0, token], None, ALU.is_equal)
                ins = dve.tensor_scalar(OJ[:, u, :], IOTA[:], IJGT[:, 1, token], IJGT[:, 2, token],
                                        ALU.is_equal, ALU.mult)
                if u % 4 == 3:
                    ins.then_inc(sem("hot_ready"), 1)

            def hot_turn(i):
                for u in range(64):
                    if u % 4 == 0:
                        wait(dve, sem("gates_done"), 16 * i + u // 4 - 1)
                    hot(slice(u, u + 1) if isinstance(i, int) else bass.ds(64 * i + u, 1), u % 8)

            hot_turn(0)
            with dve.Fori(1, GATE_TURNS) as i:
                hot_turn(i)
            st.skip(8 * AHEAD, 8 * AHEAD)

            link(dve.memset(ACC[:], 0.0))
            s0, b0, freed0 = st.step, st.block, n["freed"]

            def ahead_piece(g, buffers, u):
                if u == 0:
                    dve.wait_ge(sem("gates_loaded"), 16 * (SHARED + 1) + 16 * g)
                    dve.wait_ge(sem("ahead_loaded"), 16 * g + 16)
                k = 8 * SHARED + 8 * g + u + 1
                dve.tensor_tensor(WF[:, u % 2, :].rearrange("p (b t) -> p b t", t=16),
                                  GU[:, u, :].rearrange("p (b t) -> p b t", t=16),
                                  GG[:, :, u, :], ALU.mult).then_inc(sem("gates_used"), 1)
                dve.wait_ge(sem("gates_used"), k)
                dve.tensor_copy(buffers[0][:, u, :], WF[:, u % 2, :]).then_inc(sem("ahead_high"), 1)
                dve.wait_ge(sem("ahead_high"), 8 * g + u + 1)
                dve.tensor_tensor(buffers[1][:, u, :], WF[:, u % 2, :], buffers[0][:, u, :].bitcast(F32),
                                  ALU.subtract).then_inc(sem("expert_ready"), 1)

            def add(c, steps):
                dve.wait_ge(sem("pe_steps"), steps)
                dve.tensor_tensor(ACC[:, c, :], ACC[:, c, :], BANK[(b0 + c) % 4][:], ALU.add)\
                    .then_inc(sem("block_free"), 1)

            def experts(g, ahead=False):
                dve.wait_ge(sem("gates_loaded"), 16 * g + 16)
                for u in range(8):
                    dve.wait_ge(sem("gelu_ready"), 8 * g + u + 1)
                    k = 8 * g + u + 1
                    dve.tensor_tensor(WF[:, u % 2, :].rearrange("p (b t) -> p b t", t=16),
                                      GE[:, u % 2, :].rearrange("p (b t) -> p b t", t=16),
                                      GG[:, :, u, :], ALU.mult).then_inc(sem("gates_used"), 1)
                    dve.wait_ge(sem("gates_used"), k)
                    dve.tensor_copy(WH[:, u, :], WF[:, u % 2, :]).then_inc(sem("block_free"), 1)
                    dve.wait_ge(sem("block_free"), freed0 + 8 * g + k)
                    dve.tensor_tensor(WL[:, u, :], WF[:, u % 2, :], WH[:, u, :].bitcast(F32), ALU.subtract)\
                        .then_inc(sem("expert_ready"), 1)
                for c in range(8):
                    if ahead and c < 4:
                        for u in range(2):
                            ahead_piece(0, (WH2, WL2), 2 * c + u)
                    add(c, s0 + UNIT * 8 + UNIT * (c + 1) + 16 * UNIT * g)

            with dve.Fori(0, SHARED - 1) as g:
                experts(g)
            experts(SHARED - 1, True)
            s1 = s0 + 16 * UNIT * SHARED

            def out_group(shift, j):
                for c in range(8):
                    if c < 4:
                        for u in range(2):
                            ahead_piece(shift + j + 1, (WH, WL) if j == 0 else (WH2, WL2), 2 * c + u)
                    add(c, s1 + UNIT * (c + 1) + 8 * UNIT * (shift + j))

            with dve.Fori(0, AHEAD // 2) as i:
                for j in range(2):
                    out_group(2 * i, j)
            for c in range(8):
                add(c, s1 + UNIT * (c + 1) + 8 * UNIT * (AHEAD - 1))
                dve.wait_ge(sem("block_free"), freed0 + 16 * SHARED + 8 * (AHEAD - 1) + c + 1)
                dve.scalar_tensor_tensor(HT[:, c, :], ACC[:, c, :], MOD[:, 40 + c, 0:1], HT[:, c, :],
                                         ALU.mult, ALU.add).then_inc(sem("out_ready"), 1)


def columns(v):
    v = np.asarray(v).reshape(-1)
    return v.reshape(-1, P).T


def feature_major(m):
    t = np.asarray(m).T
    return np.ascontiguousarray(t.reshape(-1, P, t.shape[1]).transpose(1, 0, 2))


def weight_blocks(w, column0=0, count=None):
    w = np.asarray(w)
    k = w.shape[0] // P
    w = w.reshape(k, P, -1, P).transpose(2, 0, 1, 3)
    first = column0 // P
    return w[first:] if count is None else w[first:first + count]


def as_units(blocks):
    b = np.concatenate([np.asarray(x).reshape(-1, P, P) for x in blocks])
    return np.ascontiguousarray(b.reshape(-1, UNIT, P, P).transpose(0, 2, 1, 3)).reshape(-1, P, UNIT * P)


def shape_constants():
    f = np.float32
    c = {"ones": np.ones((P, P), f), "ident": np.eye(P, dtype=f)}
    c["pair"] = np.kron(np.eye(2), np.ones((64, 64))).astype(f)
    s, col = np.arange(P)[:, None] % CH, np.arange(CH)[None, :]
    c["tri"] = np.repeat((s <= col).astype(np.uint32)[:, None, :], 4, axis=1)
    d = np.arange(P)[:, None] - np.arange(TOK)[None, :] + (TOK - P)
    bias = np.zeros((HEADS, P, 3, TOK), f)
    for g, (window, dil) in enumerate(((128, 1), (512, 4), (2048, 16))):
        valid = (d >= 0) & (d % dil == 0) & (d <= window)
        for h in range(HEADS):
            slope = f(2.0 ** (-8.0 * (g * HEADS + h + 1) / 12.0))
            bias[h, :, g] = np.where(valid, -slope * d.astype(f), f(MASKED))
    c["dil_bias"] = bias
    pos = np.arange(TOK)
    e = np.arange(P) % 64
    inv = (10000.0 ** (-np.arange(16, dtype=f) / f(16))).astype(f)
    where = np.where(e[:, None] < 32, (pos // 64)[None, :], (pos % 64)[None, :]).astype(f)
    angle = (where * inv[e % 16][:, None]).astype(f).astype(np.float64)
    c["cos"] = np.cos(angle).astype(f)
    c["sin"] = (np.sin(angle) * np.where(e % 32 < 16, -1.0, 1.0)[:, None]).astype(f)
    swap = np.zeros((P, P), f)
    swap[np.arange(P) ^ 16, np.arange(P)] = 1.0
    c["swap"] = swap
    q, k = np.arange(P)[:, None] % 64, np.arange(64)[None, :]
    start = np.clip(q - 8, 0, 48)
    c["cmask"] = np.where((k >= start) & (k < start + 16), 0.0, MASKED).astype(f)
    c["iota"] = np.repeat(np.arange(P, dtype=f)[None, :], P, axis=0)
    t = np.linspace(0.0, 1.0, TOK, dtype=f)
    w = (f(2.0 * np.pi / TOK) * np.arange(TOK, dtype=f)).astype(f)
    bands = np.linspace(1e-4, 15.0, 16, dtype=f)
    arg = (bands[:, None] * w[None, :]).astype(f).astype(np.float64)
    c["feats"] = np.concatenate([t[None, :], np.cos(arg), -np.sin(arg)]).astype(f)
    deltas = np.abs(np.linspace(np.log(1e-2) / 1.5, np.log(1e-2) / 0.3, 512, dtype=f))
    decay = np.exp(-(t[:, None] * deltas[None, :]).astype(np.float64)).astype(f)
    c["decay"] = np.ascontiguousarray(decay.reshape(TT, P, TOK).transpose(1, 0, 2))
    i = np.arange(TOK)
    theta = 2.0 * np.pi * ((i[:, None] * i[None, :]) % 1024) / 1024.0
    cos, sin = np.cos(theta), -np.sin(theta)
    flips = np.where(i % 2, -1.0, 1.0)
    cos_n, sin_n = cos.copy(), sin.copy()
    cos_n[:, 0], sin_n[:, 0] = flips, flips
    weight = np.where(i == 0, 1.0, 2.0)[:, None] / 1024.0
    inv_cos, inv_sin = cos * weight, sin * weight
    inv_sin[0] = flips / 1024.0
    blk = lambda m: weight_blocks(m.astype(f))
    bc, bcn, bs, bsn = blk(cos), blk(cos_n), blk(sin), blk(sin_n)
    one = [bc, bcn[0:1], bs]
    c["w_hyk"] = as_units(one + one)
    forward = [x[m] for m in range(4) for x in (bc, bsn)]
    ic, is_ = blk(inv_cos), blk(inv_sin)
    inverse = [x[m, k] for m in range(4) for k in range(4) for x in (ic, is_)]
    c["w_hyc"] = as_units((forward + inverse) * 2)
    return c


def lay_out(v):
    a = shape_constants()
    one = lambda name: v[name][0]
    a["x"] = feature_major(v["x"][0])
    a["mem"] = feature_major(v["mem"][0])
    a["ctx"] = feature_major(v["ctx_2"][0])
    parts = {
        "ffn1_pre": v["ffn1_pre_w"], "ffn1_post": v["ffn1_post_w"], "mix_pre": v["mix_pre_w"],
        "mem_norm": v["mem_norm_w"], "mix_post": v["mix_post_w"], "ffn2_pre": v["ffn2_pre_w"],
        "ffn2_post": v["ffn2_post_w"], "norm1": v["norm1_g_2"], "norm2": v["norm2_g_2"],
        "b_gate": v["b_gate"], "lb0": v["hg_lb_logits"][0], "lb1": v["hg_lb_logits"][1],
        "hgn": v["hg_norm_w"], "b_in2": v["b_in_2"], "cw0": v["hy_conv_w_2"][0, 0],
        "cw1": v["hy_conv_w_2"][0, 1], "cw2": v["hy_conv_w_2"][0, 2], "cb": v["hy_conv_b_2"],
        "qg": np.tile(v["q_norm_g_2"][0], 2), "kg": np.tile(v["k_norm_g_2"][0], 2),
        "b_ada": v["b_ada_2"],
    }
    cond = np.stack([columns(v["c_2"][0]), columns(v["c_ctx_2"])], axis=2).reshape(P, 16)
    fold = np.tile(np.eye(2, dtype=np.float32), (P // 2, 1))
    wide = {"cond": cond, "fold": fold}
    a["vecs"] = np.ascontiguousarray(np.concatenate(
        [wide[name] if name in wide else columns(parts[name]) for name, _ in VECS], axis=1))

    def ffn(k):
        gu = weight_blocks(one(f"ffn{k}_w_gu"))
        a[f"w_ffn{k}_gu"] = as_units([gu[m + half] for m in range(FC) for half in (0, FC)])
        a[f"w_ffn{k}_down"] = as_units([weight_blocks(one(f"ffn{k}_w_down"))])

    ffn(1)
    ffn(2)
    w_in = weight_blocks(one("w_in"))
    ada = one("w_ada_2").reshape(4, 2, P, 12, TOK).transpose(3, 0, 2, 1, 4).reshape(48, P, UNIT * P)
    a["w_ada0"] = np.ascontiguousarray(ada[0:4])
    a["w_ffn1_gu"] = np.stack([a["w_ffn1_gu"], ada[4:]], axis=1).reshape(4 * FC, P, UNIT * P)
    a["w_memkv"] = as_units([weight_blocks(one("w_mem_kv"))])
    gates = [w_in[56 + 8 * b + m + i] for m in range(0, DC, 2) for i in range(2) for b in range(3)]
    a["w_hg"] = as_units([w_in[0:16]] + gates[0:8])
    a["w_dil"] = as_units([x for h in range(HEADS) for x in
                           [w_in[16 + 12 * g + 4 * part + h] for part in range(3) for g in range(3)]
                           + gates[8 + 2 * h:10 + 2 * h]])
    a["w_gate1"] = as_units(gates[16:24])
    a["w_mq"] = as_units([w_in[52:56]])
    br = [weight_blocks(one(k)) for k in ("w_br_hg", "w_br_dil", "w_br_mem")]
    merge = []
    for m in range(0, DC, 2):
        merge += [br[b][m + i] for i in range(2) for b in range(3)]
    a["w_merge1"] = as_units(merge)
    a["w_wout1"] = as_units([weight_blocks(one("w_out"))])
    w2 = weight_blocks(one("w_in_2"))
    a["w_ctxkv"] = as_units([w2[16:24]])
    a["w_hyz"] = as_units([w2[0:12]])
    a["w_naqkv"] = as_units([w2[12:24]])
    hy, na = weight_blocks(one("w_hy_out_2")), weight_blocks(one("w_na_out_2"))
    a["w_gate2"] = as_units([w2[24 + 8 * b + m] for m in range(DC) for b in range(2)])
    a["w_merge2"] = as_units([x for m in range(DC) for x in (hy[m], na[m])])
    a["w_wout2"] = as_units([weight_blocks(one("w_out_2"))])
    a["w_wq"] = as_units([weight_blocks(one("peer_w_q_2"))])
    u = one("peer_u_2").reshape(P, EXP_GROUPS, 8, DC, P).transpose(1, 2, 4, 3, 0)
    w = one("peer_v_2").reshape(P, EXP_GROUPS, 8, DC, P).transpose(1, 3, 0, 2, 4)
    u, w = (m.reshape(EXP_GROUPS, 8, P, UNIT * P) for m in (u, w))
    a["w_peer_ahead"] = np.ascontiguousarray(u[SHARED:]).reshape(8 * AHEAD, P, UNIT * P)
    a["w_peer"] = np.concatenate([u[:SHARED], w[:SHARED]], axis=1).reshape(16 * SHARED, P, UNIT * P)
    a["w_peer_out"] = np.ascontiguousarray(w[SHARED:]).reshape(8 * AHEAD, P, UNIT * P)
    a["keys"] = np.ascontiguousarray(one("peer_keys_2").reshape(16, P, P).transpose(2, 0, 1))
    a["f1"] = one("hy_f1_w_2")
    a["f23"] = np.ascontiguousarray(np.stack([one("hy_f2_w_2"), one("hy_f3_w_2")], axis=1))
    a["f4"] = one("hy_f4_w_2")
    fv = [one(k) for k in ("hy_f1_b_2", "hy_f2_b_2", "hy_f3_b_2", "hy_sin_freq_2")]
    a["fvec"] = np.ascontiguousarray(np.stack(fv + fv, axis=1))
    a["skip"] = v["hy_skip_2"].reshape(1, 2, TOK)
    dc = np.clip(np.arange(64)[None, :] - np.arange(64)[:, None], -15, 15) + 15
    rpb = one("na_rpb_2")
    table = np.stack([rpb[:, 1 - e:15 - e][:, :, dc] for e in range(2)], axis=1)
    a["na_bias"] = np.ascontiguousarray(table.transpose(0, 1, 3, 2, 4)).reshape(NAH, P, 14 * 64)
    return a


def kernel(**inputs):
    import concourse.bacc as bacc
    from concourse.bass_utils import run_bass_kernel_spmd

    a = lay_out({k: np.asarray(v) for k, v in inputs.items()})
    nc = bacc.Bacc("TRN2", target_bir_lowering=False, num_devices=1)
    aps = {k: nc.dram_tensor(f"in_{k}", x.shape, mybir.dt.from_np(x.dtype), kind="ExternalInput").ap()
           for k, x in a.items()}
    aps["out"] = nc.dram_tensor("out_x", (P, DC, TOK), F32, kind="ExternalOutput").ap()
    program(nc, aps)
    r = run_bass_kernel_spmd(nc, [{f"in_{k}": np.ascontiguousarray(x) for k, x in a.items()}], core_ids=[0])
    out = r.results[0]["out_x"]
    return np.ascontiguousarray(out.transpose(2, 1, 0)).reshape(1, TOK, D)
```
